# Optimizing a Trainium2 kernel written in Bass

```python
import math
import jax, jax.numpy as jnp
from jax import lax
import numpy as np

D_MODEL = 1024
BATCH = 1
SEQ = 512
DEPTH = 1
DEC_BATCH = 8
DEC_SEQ = 4
PAST_LEN = 4096
PAGE_SIZE = 128

S5_WIDTH = D_MODEL // 2
S5_GROUP = 16
S5_GROUPS = S5_WIDTH // S5_GROUP
S5_STATE = 64
RET_HEADS = 4
RET_DK = D_MODEL // 8
RET_DV = D_MODEL // 8
RET_WIDTH = RET_HEADS * RET_DV
RET_CHUNK = 128
MIX_WIDTH = S5_WIDTH + RET_WIDTH
IN_WIDTH = S5_WIDTH + RET_HEADS * (2 * RET_DK + 2 * RET_DV)
IN_SPLITS = (S5_WIDTH,
             S5_WIDTH + RET_HEADS * RET_DK,
             S5_WIDTH + 2 * RET_HEADS * RET_DK,
             S5_WIDTH + 2 * RET_HEADS * RET_DK + RET_WIDTH)
D_FF = ((8 * D_MODEL // 3 + 255) // 256) * 256
N_MOD = 9
ROPE_BASE = 10000.0
EPS = 1e-6

kernel_name = 'hymba_s5_retnet_macaron_adaln_step'

def rmsnorm(x, g):
    xf = x.astype(jnp.float32)
    y = xf * lax.rsqrt(jnp.mean(xf * xf, axis=-1, keepdims=True) + EPS) * g.astype(jnp.float32)
    return y.astype(x.dtype)

def modulate(h, shift, scale):
    return h * (1.0 + scale) + shift

def swiglu(h, w_in, w_out):
    a, b = jnp.split(h @ w_in, 2, axis=-1)
    return (jax.nn.silu(a) * b) @ w_out

def head_norm(o):
    mu = jnp.mean(o, axis=-1, keepdims=True)
    var = jnp.mean(jnp.square(o - mu), axis=-1, keepdims=True)
    return (o - mu) * lax.rsqrt(var + EPS)

def rotary(x, pos):
    half = x.shape[-1] // 2
    inv = ROPE_BASE ** (-jnp.arange(half, dtype=jnp.float32) / half)
    ang = pos[:, None] * inv[None, :]
    cos = jnp.cos(ang)[None, :, None, :]
    sin = jnp.sin(ang)[None, :, None, :]
    x1, x2 = x[..., :half], x[..., half:]
    return jnp.concatenate([x1 * cos - x2 * sin, x1 * sin + x2 * cos], axis=-1)

def _ssm_combine(e1, e2):
    a1, b1 = e1
    a2, b2 = e2
    return a1 * a2, a2 * b1 + b2

def s5_scan(u, lam_re, lam_im, log_dt, b_re, b_im, c_re, c_im, d_skip, h0_re, h0_im):
    f = jnp.float32
    Bsz, L, _ = u.shape
    lam = lax.complex(lam_re.astype(f), lam_im.astype(f))
    dt = jnp.exp(log_dt.astype(f))[:, None]
    lam_bar = jnp.exp(lam * dt)
    b_bar = ((lam_bar - 1.0) / lam)[:, :, None] * lax.complex(b_re.astype(f), b_im.astype(f))
    cmat = lax.complex(c_re.astype(f), c_im.astype(f))
    ug = u.astype(f).reshape(Bsz, L, S5_GROUPS, S5_GROUP)
    bu = jnp.einsum('blgc,gnc->blgn', ug.astype(jnp.complex64), b_bar)
    a = jnp.broadcast_to(lam_bar, bu.shape)
    _, xs = lax.associative_scan(_ssm_combine, (a, bu), axis=1)
    steps = jnp.arange(1, L + 1, dtype=f)[:, None, None]
    decay_h0 = jnp.exp(lam[None] * (dt[None] * steps))
    h0 = lax.complex(h0_re.astype(f), h0_im.astype(f))
    xs = xs + decay_h0[None] * h0[:, None]
    y = jnp.einsum('gcn,blgn->blgc', cmat, xs).real + d_skip.astype(f).reshape(S5_GROUPS, S5_GROUP) * ug
    h_last = xs[:, -1]
    return y.reshape(Bsz, L, S5_WIDTH), h_last.real, h_last.imag

def retention_chunked(q, k, v, s0):
    Bsz, L, H, _ = q.shape
    dv = v.shape[-1]
    chunk = RET_CHUNK if L % RET_CHUNK == 0 else L
    n_chunks = L // chunk
    lg = jnp.log1p(-jnp.exp2(-5.0 - jnp.arange(H, dtype=jnp.float32)))
    idx = jnp.arange(chunk, dtype=jnp.float32)
    diff = idx[:, None] - idx[None, :]
    intra = jnp.where(diff >= 0, jnp.exp(lg[:, None, None] * jnp.maximum(diff, 0.0)), 0.0)
    q_dec = jnp.exp(lg[None, :] * (idx[:, None] + 1.0))
    k_dec = jnp.exp(lg[None, :] * (chunk - 1.0 - idx)[:, None])
    c_dec = jnp.exp(lg * chunk)

    def to_chunks(t):
        return jnp.moveaxis(t.reshape(Bsz, n_chunks, chunk, H, t.shape[-1]), 1, 0)

    def step(S, blk):
        qc, kc, vc = blk
        scores = jnp.einsum('bihd,bjhd->bhij', qc, kc) * intra[None]
        inner = jnp.einsum('bhij,bjhv->bihv', scores, vc)
        cross = jnp.einsum('bihd,bhdv->bihv', qc, S) * q_dec[None, :, :, None]
        S_new = S * c_dec[None, :, None, None] + jnp.einsum('bjhd,bjhv->bhdv', kc * k_dec[None, :, :, None], vc)
        return S_new, inner + cross

    s_last, out = lax.scan(step, s0, (to_chunks(q), to_chunks(k), to_chunks(v)))
    out = jnp.moveaxis(out, 0, 1).reshape(Bsz, L, H, dv)
    return out, s_last

def decoder_layer(x, c, pos, h0_re, h0_im, s0, lw):
    (w_ada, b_ada, norm_ffn1, ffn1_w_in, ffn1_w_out, norm_mix, w_in_mix,
     s5_lambda_re, s5_lambda_im, s5_log_dt, s5_b_re, s5_b_im, s5_c_re, s5_c_im, s5_d, s5_w_glu,
     w_out_mix, norm_ffn2, ffn2_w_in, ffn2_w_out) = lw
    f = jnp.float32
    mod = jax.nn.silu(c) @ w_ada + b_ada
    sh1, sc1, g1, sh2, sc2, g2, sh3, sc3, g3 = jnp.split(mod[:, None, :], N_MOD, axis=-1)
    h = modulate(rmsnorm(x, norm_ffn1), sh1, sc1)
    x = x + 0.5 * g1 * swiglu(h, ffn1_w_in, ffn1_w_out)
    h = modulate(rmsnorm(x, norm_mix), sh2, sc2)
    Bsz, L, _ = h.shape
    u, q, k, v, g = jnp.split(h @ w_in_mix, IN_SPLITS, axis=-1)
    y_s5, h_re, h_im = s5_scan(u, s5_lambda_re, s5_lambda_im, s5_log_dt, s5_b_re, s5_b_im,
                               s5_c_re, s5_c_im, s5_d, h0_re, h0_im)
    y_s5 = jax.nn.gelu(y_s5).astype(x.dtype)
    glu_a, glu_b = jnp.split(y_s5 @ s5_w_glu, 2, axis=-1)
    s5_out = glu_a * jax.nn.sigmoid(glu_b)
    qh = rotary(q.astype(f).reshape(Bsz, L, RET_HEADS, RET_DK), pos)
    kh = rotary(k.astype(f).reshape(Bsz, L, RET_HEADS, RET_DK), pos) * (RET_DK ** -0.5)
    vh = v.astype(f).reshape(Bsz, L, RET_HEADS, RET_DV)
    ret, s_new = retention_chunked(qh, kh, vh, s0.astype(f))
    ret_out = jax.nn.silu(g) * head_norm(ret).reshape(Bsz, L, RET_WIDTH).astype(x.dtype)
    x = x + g2 * (jnp.concatenate([s5_out, ret_out], axis=-1) @ w_out_mix)
    h = modulate(rmsnorm(x, norm_ffn2), sh3, sc3)
    x = x + 0.5 * g3 * swiglu(h, ffn2_w_in, ffn2_w_out)
    return x, h_re, h_im, s_new

def final_norm(x, c, w_ada_final, b_ada_final, norm_final):
    shift, scale = jnp.split((jax.nn.silu(c) @ w_ada_final + b_ada_final)[:, None, :], 2, axis=-1)
    return modulate(rmsnorm(x, norm_final), shift, scale)

def setup_inputs(seed: int = 0) -> dict:
    key = jax.random.key(seed)
    ks = jax.random.split(key, 40)
    f = jnp.float32

    def nrm(k, shape, scale):
        return jax.random.normal(k, shape, f) * scale

    lam_im_base = math.pi * jnp.arange(S5_STATE, dtype=f)
    return {
        'x_prompt': nrm(ks[0], (BATCH, SEQ, D_MODEL), 1.0),
        'x_sample': nrm(ks[1], (DEC_BATCH, DEC_SEQ, D_MODEL), 1.0),
        'state_ssm_re': nrm(ks[2], (DEPTH, DEC_BATCH, S5_GROUPS, S5_STATE), 0.3),
        'state_ssm_im': nrm(ks[3], (DEPTH, DEC_BATCH, S5_GROUPS, S5_STATE), 0.3),
        'state_ret': nrm(ks[4], (DEPTH, DEC_BATCH, RET_HEADS, RET_DK, RET_DV), 1.0),
        'c_prompt': nrm(ks[5], (BATCH, D_MODEL), 1.0),
        'c_sample': nrm(ks[6], (DEC_BATCH, D_MODEL), 1.0),
        'w_ada': nrm(ks[7], (DEPTH, D_MODEL, N_MOD * D_MODEL), 0.5 * D_MODEL ** -0.5),
        'b_ada': nrm(ks[8], (DEPTH, N_MOD * D_MODEL), 0.02),
        'norm_ffn1': 1.0 + nrm(ks[9], (DEPTH, D_MODEL), 0.02),
        'ffn1_w_in': nrm(ks[10], (DEPTH, D_MODEL, 2 * D_FF), D_MODEL ** -0.5),
        'ffn1_w_out': nrm(ks[11], (DEPTH, D_FF, D_MODEL), D_FF ** -0.5),
        'norm_mix': 1.0 + nrm(ks[12], (DEPTH, D_MODEL), 0.02),
        'w_in_mix': nrm(ks[13], (DEPTH, D_MODEL, IN_WIDTH), D_MODEL ** -0.5),
        's5_lambda_re': -0.5 + nrm(ks[14], (DEPTH, S5_GROUPS, S5_STATE), 0.01),
        's5_lambda_im': lam_im_base + nrm(ks[15], (DEPTH, S5_GROUPS, S5_STATE), 0.01),
        's5_log_dt': jax.random.uniform(ks[16], (DEPTH, S5_GROUPS), f, math.log(0.001), math.log(0.1)),
        's5_b_re': nrm(ks[17], (DEPTH, S5_GROUPS, S5_STATE, S5_GROUP), (2.0 * S5_GROUP) ** -0.5),
        's5_b_im': nrm(ks[18], (DEPTH, S5_GROUPS, S5_STATE, S5_GROUP), (2.0 * S5_GROUP) ** -0.5),
        's5_c_re': nrm(ks[19], (DEPTH, S5_GROUPS, S5_GROUP, S5_STATE), (2.0 * S5_STATE) ** -0.5),
        's5_c_im': nrm(ks[20], (DEPTH, S5_GROUPS, S5_GROUP, S5_STATE), (2.0 * S5_STATE) ** -0.5),
        's5_d': nrm(ks[21], (DEPTH, S5_WIDTH), 1.0),
        's5_w_glu': nrm(ks[22], (DEPTH, S5_WIDTH, 2 * S5_WIDTH), S5_WIDTH ** -0.5),
        'w_out_mix': nrm(ks[23], (DEPTH, MIX_WIDTH, D_MODEL), MIX_WIDTH ** -0.5),
        'norm_ffn2': 1.0 + nrm(ks[24], (DEPTH, D_MODEL), 0.02),
        'ffn2_w_in': nrm(ks[25], (DEPTH, D_MODEL, 2 * D_FF), D_MODEL ** -0.5),
        'ffn2_w_out': nrm(ks[26], (DEPTH, D_FF, D_MODEL), D_FF ** -0.5),
        'w_ada_final': nrm(ks[27], (D_MODEL, 2 * D_MODEL), 0.5 * D_MODEL ** -0.5),
        'b_ada_final': nrm(ks[28], (2 * D_MODEL,), 0.02),
        'norm_final': 1.0 + nrm(ks[29], (D_MODEL,), 0.02),
    }

def reference(x_prompt, x_sample, state_ssm_re, state_ssm_im, state_ret, c_prompt, c_sample,
              w_ada, b_ada, norm_ffn1, ffn1_w_in, ffn1_w_out, norm_mix, w_in_mix,
              s5_lambda_re, s5_lambda_im, s5_log_dt, s5_b_re, s5_b_im, s5_c_re, s5_c_im, s5_d, s5_w_glu,
              w_out_mix, norm_ffn2, ffn2_w_in, ffn2_w_out, w_ada_final, b_ada_final, norm_final):
    f = jnp.float32
    bp = x_prompt.shape[0]
    pos_prompt = jnp.arange(x_prompt.shape[1], dtype=f)
    pos_sample = PAST_LEN + jnp.arange(x_sample.shape[1], dtype=f)
    xp, xs = x_prompt, x_sample
    p_re, p_im, p_ret, s_re, s_im, s_ret = [], [], [], [], [], []
    for l in range(DEPTH):
        lw = (w_ada[l], b_ada[l], norm_ffn1[l], ffn1_w_in[l], ffn1_w_out[l], norm_mix[l], w_in_mix[l],
              s5_lambda_re[l], s5_lambda_im[l], s5_log_dt[l], s5_b_re[l], s5_b_im[l], s5_c_re[l], s5_c_im[l],
              s5_d[l], s5_w_glu[l], w_out_mix[l], norm_ffn2[l], ffn2_w_in[l], ffn2_w_out[l])
        zero_ssm = jnp.zeros((bp, S5_GROUPS, S5_STATE), f)
        zero_ret = jnp.zeros((bp, RET_HEADS, RET_DK, RET_DV), f)
        xp, hr, hi, sr = decoder_layer(xp, c_prompt, pos_prompt, zero_ssm, zero_ssm, zero_ret, lw)
        p_re.append(hr); p_im.append(hi); p_ret.append(sr)
        xs, hr, hi, sr = decoder_layer(xs, c_sample, pos_sample, state_ssm_re[l], state_ssm_im[l], state_ret[l], lw)
        s_re.append(hr); s_im.append(hi); s_ret.append(sr)
    y_prompt = final_norm(xp, c_prompt, w_ada_final, b_ada_final, norm_final)
    y_sample = final_norm(xs, c_sample, w_ada_final, b_ada_final, norm_final)
    return (y_prompt, y_sample, jnp.stack(p_re), jnp.stack(p_im), jnp.stack(p_ret),
            jnp.stack(s_re), jnp.stack(s_im), jnp.stack(s_ret))


_drawn_inputs = setup_inputs


def setup_inputs(seed=0):
    import zlib

    import numpy as np

    out = dict(_drawn_inputs(seed))
    spreads = {}
    factors = {'norm_ffn1': 8.0,
     's5_lambda_re': 43.617,
     's5_c_re': 22.158,
     's5_c_im': 21.146,
     'norm_ffn2': 23.556,
     'norm_final': 25.059,
     's5_d': 4.522,
     's5_w_glu': 2.846,
     'b_ada_final': 2.778}
    for name, (base, spread) in spreads.items():
        noise = np.random.default_rng([zlib.crc32(name.encode()), seed]).standard_normal(out[name].shape)
        drawn = base * np.exp(spread * noise) if base else spread * noise
        out[name] = __import__('jax').numpy.asarray(drawn.astype(out[name].dtype))
    for name, factor in factors.items():
        out[name] = (out[name] * factor).astype(out[name].dtype)
    return out
```

```python
from contextlib import ExitStack, contextmanager

import numpy as np
import concourse.bass as bass
from concourse import mybir

F32, F32R = mybir.dt.float32, mybir.dt.float32r
ALU, ACT = mybir.AluOpType, mybir.ActivationFunctionType

P = 128
D_MODEL, SEQ, DEC_BATCH, DEC_SEQ, PAST_LEN = 1024, 512, 8, 4, 4096
D_FF = ((8 * D_MODEL // 3 + 255) // 256) * 256
EPS = 1e-6
DT = D_MODEL // P
HALVES = 2
HP, HS = SEQ // 2, DEC_BATCH * DEC_SEQ // 2
HALF = HP + HS
NS = DEC_BATCH * DEC_SEQ
TOK = SEQ + NS
NC_ = 1 + DEC_BATCH
FT = D_FF // P
HT = FT // 2
KMAX = HT
HEADS, DK, DV = 4, P, P
CT, NT, SEG = 4, 16, 128
ADA_BLOCKS, ADA_UNITS, ADA_N = 22, 4, 512
MOD_TILES = ADA_BLOCKS * 4
SH1, SC1, G1, SH2, SC2, G2, SH3, SC3, G3, SHF, SCF = range(0, MOD_TILES, DT)

UP = [(0, HT, DT), (15, HT, DT), (48, HT, DT), (63, HT, DT)]
DOWN = [(11, 4, HT), (26, 4, HT), (59, 4, HT), (74, 4, HT)]
PROJ_U, PROJ_REST, GLU, OUT = (30, 2, DT), (32, 8, DT), (40, 4, 4), (44, 4, DT)
PHASES = [UP[0], DOWN[0], UP[1], DOWN[1], PROJ_U, PROJ_REST, GLU, OUT, UP[2], DOWN[2], UP[3], DOWN[3]]
PAIRS = 78


def k_tiles(pair):
    return next(k for first, n, k in PHASES if first <= pair < first + n)


_two = np.float64(2 * np.pi)
_p0 = 6.28125
_p1 = float(np.float32(np.round((_two - _p0) * 2.0 ** 21) / 2.0 ** 21))
TWO_PI = (_p0, _p1, float(np.float32(_two - _p0 - _p1)))
PI_LOW = 3.1415925

PRM = {}
_at = 0
for _name, _n in (("ident", P), ("mean", P), ("sel", NC_), ("bias", MOD_TILES), ("gain", 4 * DT), ("skip", CT),
                  ("lam", 3 * NT), ("c", DT * NC_)):
    PRM[_name] = (_at, _at + _n)
    _at += _n
PRM_N = _at
HC = {}
_at = 0
for _name, _n in (("mask", SEQ), ("qmask", DEC_BATCH * NS), ("kdec", 5), ("g4", 1), ("smask", NS), ("bmask", DEC_BATCH)):
    HC[_name] = (_at, _at + _n)
    _at += _n
HC_N = _at


class Steps:

    def __init__(self, eng, sem):
        self.eng, self.sem, self.base, self.k = eng, sem, 0, 0

    def mark(self, ins):
        ins.then_inc(self.sem, 1)
        self.k += 1

    def wait(self):
        self.eng.wait_ge(self.sem, self.base + self.k)

    def step(self, ins):
        self.mark(ins)
        self.wait()

    @contextmanager
    def loop(self, start, end, per):
        before = self.base + self.k
        with self.eng.Fori(start, end) as i:
            self.base, self.k = (i - start) * per + before, 0
            yield i
            assert self.k == per, (self.k, per)
        self.base, self.k = before + (end - start) * per, 0


def build(nc, a):
    with ExitStack() as ctx:
        def sb(name, shape, dt=F32):
            return ctx.enter_context(nc.sbuf_tensor(name, shape, dt))

        sems = {}

        def sem(name):
            if name not in sems:
                sems[name] = ctx.enter_context(nc.semaphore(name))
            return sems[name]

        x = sb("x", [P, DT, HALVES, HALF])
        h_hi = sb("h_hi", [P, DT, HALVES, HALF], F32R)
        h_lo = sb("h_lo", [P, DT, HALVES, HALF], F32R)
        w_raw = [sb(f"w_raw{s}", [P, KMAX, P]) for s in range(2)]
        w_hi = [sb(f"w_hi{s}", [P, KMAX, P], F32R) for s in range(2)]
        w_lo = [sb(f"w_lo{s}", [P, KMAX, P], F32R) for s in range(2)]
        mod = sb("mod", [P, MOD_TILES, NC_])
        prm = sb("prm", [P, PRM_N])
        c_split = sb("c_split", [P, DT, 2 * NC_], F32R)
        lb = sb("lb", [P, CT, 2, P])
        lc = sb("lc", [P, NT, 2, 32])
        sumsq, root = (sb(n, [P, HALVES, HALF]) for n in ("sumsq", "root"))
        tmp = [sb(f"tmp{s}", [P, HALVES, HALF]) for s in range(2)]
        h32 = [sb(f"h32_{s}", [P, HALVES, HALF]) for s in range(2)]
        s5r, s5lam, s5beta, s5pow = sb("s5r", [P, NT]), sb("s5lam", [P, 2, NT]), sb("s5beta", [P, 2, NT]), sb("s5pow", [P, 2, 8, NT])
        s5t = sb("s5t", [P, 8, NT])
        stat = sb("stat", [P, 5, 6])
        mv = sb("mv", [P, 5, 2])
        hrstd = sb("hrstd", [P, 5, 1])
        eps_t = sb("eps_t", [P, 1])
        epsm = sb("epsm", [P, 5, 2])
        x_last = sb("x_last", [P, 2, NT])
        carry = sb("carry", [P, 2, 4])
        ct4 = sb("ct4", [P, 4, 4])

        g = nc.sbuf_tensor("hid_hi", [P, HT, HALVES, HALF], F32R)
        hid_hi = g.__enter__()
        g2 = nc.sbuf_tensor("hid_lo", [P, HT, HALVES, HALF], F32R)
        hid_lo = g2.__enter__()
        g2.__exit__(None, None, None)
        g.__exit__(None, None, None)
        proj = sb("proj", [P, 20, TOK])
        bus = sb("bus", [P, 2, NT, NS])

        sb("hid_rest", [P, 2 * HT * TOK - 20 * TOK - 2 * NT * NS])

        with ExitStack() as e_life:
            et = e_life.enter_context(nc.sbuf_tensor("et", [P, 2, NT, SEG], F32))
        with ExitStack() as late:
            def lsb(name, shape):
                return late.enter_context(nc.sbuf_tensor(name, shape, F32))
            xs = lsb("xs", [P, 2, NT, DEC_BATCH, DEC_SEQ])
            vm = lsb("vm", [P, DEC_BATCH, DV])
            gate = lsb("gate", [P, TOK])
            rope = lsb("rope", [P, 2, TOK])
            h0 = lsb("h0", [P, 2, NT, DEC_BATCH])
        sb("et_region", [P, 2 * NT * SEG])

        with ExitStack() as life:
            ada_raw = [life.enter_context(nc.sbuf_tensor(f"ada_raw{u}", [P, 2, ADA_N], F32)) for u in range(ADA_UNITS)]
            ada_hi = [life.enter_context(nc.sbuf_tensor(f"ada_hi{u}", [P, 2, ADA_N], F32R)) for u in range(2)]
            ada_lo = [life.enter_context(nc.sbuf_tensor(f"ada_lo{u}", [P, 2, ADA_N], F32R)) for u in range(2)]
        with ExitStack() as life:
            def rsb(name, shape):
                return life.enter_context(nc.sbuf_tensor(name, shape, F32))
            bu = [rsb(f"bu{s}", [P, 2, 4, SEG]) for s in range(2)]
            z = [rsb(f"z{s}", [P, 2, 4, SEG]) for s in range(2)]
            xc = [rsb(f"xc{s}", [P, 2, 4, SEG]) for s in range(2)]
            lbs = rsb("lbs", [P, 2, 4, P])
            lcs = rsb("lcs", [P, 4, 2, 32])
            us = rsb("us", [P, TOK])
        with ExitStack() as life:
            def rsb(name, shape):
                return life.enter_context(nc.sbuf_tensor(name, shape, F32))
            qs, ks = rsb("qs", [P, TOK]), rsb("ks", [P, TOK])
            vt, kt = rsb("vt", [P, 5, DV]), rsb("kt", [P, 5, DK])
            sc = rsb("sc", [P, 10 * P])
            scs = rsb("scs", [NS, NS])
            hc = rsb("hc", [P, HC_N])
            s0, sn = rsb("s0", [P, DEC_BATCH, DV]), rsb("sn", [P, DEC_BATCH, DV])
            qm = rsb("qm", [P, DEC_BATCH, NS])
            on = rsb("on", [P, 5, DV])
            sp_out = rsb("sp_out", [P, DV])
            xs_last = rsb("xs_last", [P, 2, NT, DEC_BATCH])
        sb("ada_region", [P, 2 * ADA_UNITS * 2 * ADA_N])
        ada_row = h32[1][0:2 * NC_].rearrange("p h n -> p (h n)")[:, 0:ADA_N]
        vs = sumsq[:].rearrange("p h n -> p (h n)")

        acc = [ctx.enter_context(nc.psum_tensor(f"acc{s}", [P, 2, 512], F32)) for s in range(2)]
        pn = ctx.enter_context(nc.psum_tensor("pn", [P, 2, 512], F32))
        pa = ctx.enter_context(nc.psum_tensor("pa", [P, 512], F32))
        pt = ctx.enter_context(nc.psum_tensor("pt", [P, 512], F32))

        def prmv(name):
            return prm[:, PRM[name][0]:PRM[name][1]]

        def hcv(name):
            return hc[:, HC[name][0]:HC[name][1]]

        def prompt(t):
            return t[:, :, 0:HP]

        def sample(t):
            return t[:, :, HP:HALF]

        def sample4(t):
            return sample(t).rearrange("p h (b s) -> p h b s", s=DEC_SEQ)

        def per_seq(t):
            return t.rearrange("p (h b) -> p h b", h=2).unsqueeze(3).broadcast_to([P, 2, 4, DEC_SEQ])

        def flat(t):
            return t[:].rearrange("p h n -> p (h n)")

        def view4(t):
            return flat(t)[:, 0:4 * SEG].rearrange("p (t n) -> p t n", t=4)

        def view(t, n):
            return flat(t)[:, 0:n]

        raw_in = [sem(f"raw_in{s}") for s in range(2)]
        hi_ready = [sem(f"hi_ready{s}") for s in range(2)]
        lo_ready = [sem(f"lo_ready{s}") for s in range(2)]
        acc_ready = [sem(f"acc_ready{s}") for s in range(2)]
        acc_free = [sem(f"acc_free{s}") for s in range(2)]
        ada_in = [sem(f"ada_in{u}") for u in range(ADA_UNITS)]
        ada_hi_ready, ada_lo_ready, ada_used = sem("ada_hi_ready"), sem("ada_lo_ready"), sem("ada_used")
        ada_row_ready, ada_turned, mod_ready = sem("ada_row_ready"), sem("ada_turned"), sem("mod_ready")
        prm_in, x_in, b_in, c_in = sem("prm_in"), sem("x_in"), sem("b_in"), sem("c_in")
        rope_in, h0_in, hc_in, s0_in = sem("rope_in"), sem("h0_in"), sem("hc_in"), sem("s0_in")
        silu_c, c_hi_ready, c_ready = sem("silu_c"), sem("c_hi_ready"), sem("c_ready")
        sumsq_ready, ms_ready, root_ready = sem("sumsq_ready"), sem("ms_ready"), sem("root_ready")
        h32_ready, h_hi_ready, h_lo_ready = sem("h32_ready"), sem("h_hi_ready"), sem("h_lo_ready")
        hid_hi_ready, hid_lo_ready = sem("hid_hi_ready"), sem("hid_lo_ready")
        y_tile = sem("y_tile")
        stored = sem("stored")
        act_step, dve_step, pool_step = sem("act_step"), sem("dve_step"), sem("pool_step")
        s5_angle, s5_exp, s5_trig, bbar_ready, bbar_turned, lb_ready = (sem(n) for n in (
            "s5_angle", "s5_exp", "s5_trig", "bbar_ready", "bbar_turned", "lb_ready"))

        staged, b_done, bs_done = sem("staged"), sem("b_done"), sem("bs_done")
        bu_ready, bus_ready, y_used = sem("bu_ready"), sem("bus_ready"), sem("y_used")
        bu_used, xi_ready, y_ready = sem("bu_used"), sem("xi_ready"), sem("y_ready")
        z_ready, xr_ready, x_last_ready, lbs_clear = (sem(n) for n in ("z_ready", "xr_ready", "x_last_ready", "lbs_clear"))
        xs_ready, xs_last_ready, ys_ready, y_all = (sem(n) for n in ("xs_ready", "xs_last_ready", "ys_ready", "y_all"))
        gelu_ready, g_hi_ready, g_lo_ready, m_hi_ready, m_lo_ready = (sem(n) for n in (
            "gelu_ready", "g_hi_ready", "g_lo_ready", "m_hi_ready", "m_lo_ready"))
        krot_ready, qrot_ready, tv_ready, snp_ready, o_ready, m32_ready = (sem(n) for n in (
            "krot_ready", "qrot_ready", "tv_ready", "snp_ready", "o_ready", "m32_ready"))
        swq_ready, swk_ready, vs_ready, gate_ready, vt_ready, vm_ready = (sem(n) for n in (
            "swq_ready", "swk_ready", "vs_ready", "gate_ready", "vt_ready", "vm_ready"))
        mv_ready, hrstd_ready, on_ready, kt_ready, qm_ready, scm_ready = (sem(n) for n in (
            "mv_ready", "hrstd_ready", "on_ready", "kt_ready", "qm_ready", "scm_ready"))
        tk_ready, scores_ready, spp_ready, sp_ready, sn_ready, ot_ready, head_stored = (sem(n) for n in (
            "tk_ready", "scores_ready", "spp_ready", "sp_ready", "sn_ready", "ot_ready", "head_stored"))
        eps_ready, table_done, pool_settled, dve_settled = (sem(n) for n in (
            "eps_ready", "table_done", "pool_settled", "dve_settled"))

        block = ctx.enter_context(nc.Block())

        @block.sync
        def _(sp):
            sp.dma_start(prm[:], a["prm"]).then_inc(prm_in, 16)

            def source(phase):
                first, n, k = phase
                name = ("up" if phase in UP else "down" if phase in DOWN else
                        {PROJ_U: "w_in", PROJ_REST: "w_in", GLU: "w_glu", OUT: "w_out"}[phase])
                if name in ("up", "down"):
                    j = (UP if name == "up" else DOWN).index(phase)
                    return a[f"ffn{1 + j // 2}_{name}"], (j % 2) * n
                return a[name], 2 if phase == PROJ_REST else 0

            def load_unit(phase, i, s, first_use=False):
                src, off = source(phase)
                k = phase[2]
                if not first_use:
                    sp.wait_ge(lo_ready[s], phase[0] + i)
                sp.dma_start(w_raw[s][:, 0:k, :],
                             src[i + off, s].rearrange("p (k m) -> p k m", k=k)).then_inc(raw_in[s], 16)

            def load_ada(b, u, first_use=False):
                if not first_use:
                    sp.wait_ge(ada_lo_ready, (b - 1) * 4 + u + 1)
                sp.dma_start(ada_raw[u][:], a["ada"][b, u].rearrange("p (k n) -> p k n", k=2)).then_inc(ada_in[u], 16)

            for u in range(ADA_UNITS):
                load_ada(0, u, first_use=True)
            sp.dma_start(x[:], a["x"].rearrange("p (t h n) -> p t h n", t=DT, h=2)).then_inc(x_in, 16)
            with sp.Fori(1, 4) as b:
                for u in range(ADA_UNITS):
                    load_ada(b, u)
            load_unit(UP[0], 0, 0, first_use=True)
            load_unit(UP[0], 0, 1, first_use=True)
            sp.dma_start(lc[:], a["s5_c"].rearrange("p (t r c) -> p t r c", t=NT, r=2)).then_inc(c_in, 16)

            def load_up(phase, block0, done=0):
                n_ada = 9 if block0 else 0
                if n_ada:
                    if done == 0:
                        load_unit(phase, 0, 0)
                    for u in range(ADA_UNITS):
                        load_ada(block0, u)
                    if done == 0:
                        load_unit(phase, 0, 1)
                    with sp.Fori(1, n_ada) as f:
                        load_unit(phase, f, 0)
                        for u in range(ADA_UNITS):
                            load_ada(f + block0, u)
                        load_unit(phase, f, 1)
                with sp.Fori(n_ada, HT) as f:
                    load_unit(phase, f, 0)
                    load_unit(phase, f, 1)

            def load_plain(phase):
                with sp.Fori(0, phase[1]) as i:
                    load_unit(phase, i, 0)
                    load_unit(phase, i, 1)

            load_up(UP[0], 4, done=1)
            load_unit(DOWN[0], 0, 0)
            load_unit(DOWN[0], 0, 1)
            sp.wait_ge(acc_free[1], DOWN[0][0])
            for r in range(2):
                sp.dma_start(flat(tmp[r])[:, 0:NT * 32], a["s5_b"][r]).then_inc(b_in, 16)
            with sp.Fori(1, 4) as i:
                load_unit(DOWN[0], i, 0)
                load_unit(DOWN[0], i, 1)
            load_up(UP[1], 13)
            load_plain(DOWN[1])
            load_plain(PROJ_U)
            load_plain(PROJ_REST)
            load_unit(GLU, 0, 0)
            load_unit(GLU, 0, 1)
            sp.wait_ge(y_used, 16 + 1)
            sp.wait_ge(xi_ready, 16 + 2)
            sp.dma_start(h0[:], a["h0"].rearrange("p (r t b) -> p r t b", r=2, t=NT)).then_inc(h0_in, 16)
            sp.dma_start(rope[:], a["rope"].rearrange("p (r n) -> p r n", r=2)).then_inc(rope_in, 16)
            sp.wait_ge(x_last_ready, 2 * CT)
            sp.dma_start(a["ssm_prompt"], x_last[:].rearrange("p r t -> p (r t)")).then_inc(stored, 16)
            sp.dma_start(hc[:], a["head_consts"][0]).then_inc(hc_in, 16)
            sp.dma_start(s0[:], a["s0"][0].rearrange("p (b v) -> p b v", b=DEC_BATCH)).then_inc(s0_in, 16)
            with sp.Fori(1, 4) as i:
                load_unit(GLU, i, 0)
                load_unit(GLU, i, 1)
            load_unit(OUT, 0, 0)
            load_unit(OUT, 0, 1)
            sp.wait_ge(xs_last_ready, 1)
            sp.dma_start(a["ssm_sample"], xs_last[:].rearrange("p r t b -> p (r t b)")).then_inc(stored, 16)

            def store_head(h):
                sp.wait_ge(sp_ready, h + 1)
                sp.dma_start(a["ret_prompt"][h], sp_out[:]).then_inc(head_stored, 16)
                sp.wait_ge(sn_ready, h + 1)
                sp.dma_start(a["ret_sample"][h], sn[:].rearrange("p b v -> p (b v)")).then_inc(head_stored, 16)
            with sp.Fori(0, HEADS - 1) as h:
                store_head(h)
                sp.wait_ge(o_ready, h + 2)
                sp.wait_ge(vm_ready, h + 1)
                sp.wait_ge(head_stored, 32 * h + 32)
                sp.dma_start(s0[:], a["s0"][h + 1].rearrange("p (b v) -> p b v", b=DEC_BATCH)).then_inc(s0_in, 16)
                sp.dma_start(hc[:], a["head_consts"][h + 1]).then_inc(hc_in, 16)
            store_head(HEADS - 1)
            with sp.Fori(1, 4) as i:
                load_unit(OUT, i, 0)
                load_unit(OUT, i, 1)
            for phase in (UP[2], UP[3]):
                load_up(phase, 0)
                load_plain(DOWN[UP.index(phase)])
            with sp.Fori(0, DT) as m:
                sp.wait_ge(y_tile, m + 1)
                sp.dma_start(a["y"][m].rearrange("p (h n) -> p h n", h=2), x[:, m]).then_inc(stored, 16)
            sp.wait_ge(stored, 16 * (2 + DT))
            sp.wait_ge(head_stored, 16 * 2 * HEADS)

        @block.gpsimd
        def _(pool):
            st = Steps(pool, pool_step)

            def tt(out, in0, in1, op, moving=False):
                if moving:
                    pool.sem_inc(pool_settled, 1)
                return pool.tensor_tensor(out, in0, in1, op)

            def split_lo(pair, s, k):
                pool.wait_ge(hi_ready[s], pair + 1)
                tt(w_lo[s][:, 0:k], w_raw[s][:, 0:k], w_hi[s][:, 0:k].bitcast(F32), ALU.subtract).then_inc(lo_ready[s], 1)

            def split_pairs(phase, start=0):
                first, n, k = phase
                with pool.Fori(start, n) as i:
                    split_lo(i + first, 0, k)
                    split_lo(i + first, 1, k)

            def norm_lo(j):
                with pool.Fori(0, DT // 2) as i:
                    for s in range(2):
                        pool.wait_ge(h_hi_ready, 2 * i + (DT * j + s + 1))
                        tt(h_lo[:, 2 * i + s], h32[s][:], h_hi[:, 2 * i + s].bitcast(F32), ALU.subtract, moving=True)\
                            .then_inc(h_lo_ready, 1)

            def normed_phase(j, phase):
                split_lo(phase[0], 0, phase[2])
                norm_lo(j)
                split_lo(phase[0], 1, phase[2])
                split_pairs(phase, 1)

            pool.wait_ge(x_in, 16)
            st.step(pool.memset(sumsq[:], 0.0))
            with st.loop(0, DT, 2) as m:
                st.step(tt(root[:], x[:, m], x[:, m], ALU.mult, moving=True))
                st.step(tt(sumsq[:], sumsq[:], root[:], ALU.add))
            pool.sem_inc(sumsq_ready, 1)
            normed_phase(0, UP[0])
            split_pairs(DOWN[0])
            split_pairs(UP[1])
            split_pairs(DOWN[1])
            normed_phase(1, PROJ_U)

            pool.sem_inc(xi_ready, 2)

            def segment(ct, j):
                gi, b = 4 * ct + j, j % 2
                er, ei = et[:, 0, bass.ds(4 * ct, 4), :], et[:, 1, bass.ds(4 * ct, 4), :]
                pa_, pb_ = view4(h32[0]), view4(h32[1])
                pool.wait_ge(z_ready, gi + 1)
                pool.wait_ge(y_ready, gi + 1)
                pool.wait_ge(xi_ready, gi + 2)
                st.mark(tt(pa_, z[b][:, 0], ei, ALU.mult, moving=True))
                st.step(tt(pb_, z[b][:, 1], er, ALU.mult))
                tt(xc[b][:, 1], pa_, pb_, ALU.add).then_inc(xi_ready, 1)

            def channel_tile(ct, k_next):
                qa = 2 * ct + PROJ_REST[0]
                split_lo(qa, 1, DT)
                segment(ct, 0)
                split_lo(qa + 1, 0, DT)
                segment(ct, 1)
                split_lo(qa + 1, 1, DT)
                segment(ct, 2)
                split_lo(qa + 2, 0, k_next)
                segment(ct, 3)
                pool.wait_ge(xi_ready, 4 * ct + 4 + 2)
                pool.tensor_copy(x_last[:, 1, bass.ds(4 * ct, 4)], xc[1][:, 1, :, SEG - 1]).then_inc(x_last_ready, 1)

            split_lo(PROJ_REST[0], 0, DT)
            with st.loop(0, CT - 1, 8) as ct:
                channel_tile(ct, DT)
            channel_tile(CT - 1, GLU[2])

            split_lo(GLU[0], 1, GLU[2])
            split_pairs(GLU, 1)
            split_lo(OUT[0], 0, OUT[2])
            split_lo(OUT[0], 1, OUT[2])

            pool.sem_inc(krot_ready, 1)
            pool.wait_ge(rope_in, 16)
            st.step(pool.memset(epsm[:, :, 0:1], EPS))
            st.step(pool.memset(epsm[:, :, 1:2], -0.5))
            with st.loop(0, HEADS, 3) as h:
                k_tile = proj[:, h + 8]
                pool.wait_ge(swk_ready, h + 1)
                pool.wait_ge(o_ready, h + 1)
                st.mark(tt(ks[:], k_tile, rope[:, 0], ALU.mult, moving=True))
                st.step(tt(flat(h32[1]), flat(h32[1]), rope[:, 1], ALU.mult))
                tt(ks[:], ks[:], flat(h32[1]), ALU.add).then_inc(krot_ready, 1)
                pool.wait_ge(vt_ready, h + 1)
                pool.wait_ge(hc_in, 16 * h + 16)
                pool.wait_ge(snp_ready, h + 1)
                tt(vm[0:NS], vt[0:NS, 4, :].unsqueeze(1).broadcast_to([NS, DEC_BATCH, DV]),
                   hcv("bmask")[0:NS].unsqueeze(2).broadcast_to([NS, DEC_BATCH, DV]), ALU.mult).then_inc(vm_ready, 1)
                pool.wait_ge(mv_ready, h + 1)
                st.step(tt(hrstd[:], mv[:, :, 1:2], epsm[:, :, 0:1], ALU.add))
                tt(hrstd[:], hrstd[:], epsm[:, :, 1:2], ALU.pow).then_inc(hrstd_ready, 1)
            split_pairs(OUT, 1)
            normed_phase(2, UP[2])
            split_pairs(DOWN[2])
            split_pairs(UP[3])
            split_pairs(DOWN[3])

        @block.scalar
        def _(act):
            st = Steps(act, act_step)

            def copy(out, in_, scale=1.0):
                return nc.scalar.activation(out, in_, ACT.Copy, scale=scale)

            def split_hi(pair, s, k, first_use=False):
                act.wait_ge(raw_in[s], 16 * pair + 16)
                if not first_use:
                    act.wait_ge(acc_ready[s], pair)
                copy(w_hi[s][:, 0:k], w_raw[s][:, 0:k]).then_inc(hi_ready[s], 1)

            def ada_split(b, u):
                act.wait_ge(ada_in[u], 16 * b + 16)
                if not (isinstance(b, int) and b == 0 and u < 2):
                    act.wait_ge(ada_used, 4 * b + (u - 1))
                copy(ada_hi[u % 2][:], ada_raw[u][:]).then_inc(ada_hi_ready, 1)

            def ada_read(b):
                act.wait_ge(ada_used, 4 * b + 4)
                if not (isinstance(b, int) and b == 0):
                    act.wait_ge(ada_turned, b)
                copy(ada_row, pa[0:2 * NC_, :]).then_inc(ada_row_ready, 1)

            act.wait_ge(prm_in, 16)
            act_c = h32[0][:, 0, 0:DT * NC_]
            nc.scalar.activation(act_c, prmv("c"), ACT.Silu).then_inc(silu_c, 1)
            act.wait_ge(silu_c, 1)
            copy(c_split[:, :, 0:NC_], act_c.rearrange("p (t n) -> p t n", n=NC_)).then_inc(c_hi_ready, 1)
            for u in range(2):
                ada_split(0, u)
            lam = prmv("lam").rearrange("p (a t) -> p a t", a=3)
            nc.scalar.activation(s5t[:, 0], lam[:, 2], ACT.Exp).then_inc(s5_exp, 1)
            for u in range(2, 4):
                ada_split(0, u)
            ada_read(0)
            act.wait_ge(s5_angle, 1)
            nc.scalar.activation(s5r[:], s5t[:, 1], ACT.Exp)
            nc.scalar.activation(s5pow[:, 1, 0], s5t[:, 2], ACT.Sin)
            nc.scalar.activation(s5pow[:, 0, 0], s5t[:, 3], ACT.Sin).then_inc(s5_trig, 1)
            with act.Fori(1, 4) as b:
                for u in range(4):
                    ada_split(b, u)
                ada_read(b)
            split_hi(UP[0][0], 0, DT, first_use=True)

            def norm_root(j):
                act.wait_ge(ms_ready, j + 1)
                nc.scalar.activation(root[:], pn[:, :, 0:HALF], ACT.Sqrt, bias=eps_t[:]).then_inc(root_ready, 1)

            def norm_hi(j):
                with act.Fori(0, DT // 2) as i:
                    for s in range(2):
                        act.wait_ge(h32_ready, 2 * i + (DT * j + s + 1))
                        copy(h_hi[:, 2 * i + s], h32[s][:]).then_inc(h_hi_ready, 1)

            def up(phase, block0):
                first = phase[0]

                def hidden(f, ada, first_use=False, k_next=DT):
                    pair = f + first
                    b = f + block0
                    split_hi(pair, 1, DT, first_use)
                    if ada:
                        ada_split(b, 0)
                        ada_split(b, 1)
                    act.wait_ge(acc_ready[0], pair + 1)
                    if not first_use:
                        act.wait_ge(acc_free[1], pair)
                    nc.scalar.activation(tmp[0][:], acc[0][:, :, 0:HALF], ACT.Silu).then_inc(acc_free[0], 1)
                    split_hi(pair + 1, 0, k_next)
                    if ada:
                        ada_split(b, 2)
                        ada_split(b, 3)
                    act.wait_ge(acc_free[1], pair + 1)
                    copy(hid_hi[:, f], h32[0][:]).then_inc(hid_hi_ready, 1)
                    if ada:
                        ada_read(b)

                n_ada = 9 if block0 else 0
                if block0:
                    hidden(0, True, first_use=(first == 0))
                    with act.Fori(1, n_ada) as f:
                        hidden(f, True)
                with act.Fori(n_ada, HT - 1) as f:
                    hidden(f, False)
                hidden(HT - 1, False, k_next=KMAX)

            def splits(phase, start=0):
                first, n, k = phase
                with act.Fori(start, n - 1) as i:
                    split_hi(i + first, 1, k)
                    split_hi(i + (first + 1), 0, k)
                split_hi(first + n - 1, 1, k)
                if first + n < PAIRS:
                    split_hi(first + n, 0, k_tiles(first + n))

            act.wait_ge(eps_ready, 1)
            norm_root(0)
            norm_hi(0)
            up(UP[0], 4)
            act.wait_ge(c_in, 16)
            st.step(nc.scalar.activation(lc[:, :, 1, :], lc[:, :, 1, :], ACT.Copy, scale=-1.0))
            splits(DOWN[0])
            act.wait_ge(bbar_turned, 1)
            copy(lb[:], pn[:].rearrange("p r (t n) -> p t r n", t=CT)).then_inc(lb_ready, 1)
            act.wait_ge(table_done, 1)
            up(UP[1], 13)
            splits(DOWN[1])
            norm_root(1)
            norm_hi(1)

            def read_proj(pair, s, m):
                act.wait_ge(acc_ready[s], pair + 1)
                copy(proj[:, m, 0:SEQ].rearrange("p (h n) -> p h n", h=2), prompt(acc[s]))
                copy(proj[:, m, SEQ:TOK].rearrange("p (h n) -> p h n", h=2), sample(acc[s])).then_inc(acc_free[s], 1)

            for i in range(PROJ_U[1]):
                pair = PROJ_U[0] + i
                split_hi(pair, 1, DT)
                read_proj(pair, 0, 2 * i)
                split_hi(pair + 1, 0, DT)
                read_proj(pair, 1, 2 * i + 1)

            act.sem_inc(bu_ready, 1)
            act.sem_inc(bus_ready, 1)
            act.wait_ge(lbs_clear, 1)
            for s in range(2):
                act.wait_ge(acc_free[s], PROJ_REST[0])
            act.wait_ge(lb_ready, 1)

            def channel_tile(ct, k_next, first=False):
                qa = 2 * ct + PROJ_REST[0]
                if not first:
                    act.wait_ge(y_ready, 4 * ct + 2)
                for i in range(4):
                    r = slice(32 * i, 32 * i + 32)
                    copy(lbs[r, :, i, :], lb[r, ct])
                copy(lcs[:], lc[:, bass.ds(4 * ct, 4)])
                copy(us[:], proj[:, ct]).then_inc(staged, 1)

                def read_bu(j):
                    gi = 4 * ct + j
                    act.wait_ge(b_done, gi + 1)
                    act.wait_ge(bu_used, gi + 1)
                    copy(bu[j % 2][:], pn[:].rearrange("p r (t n) -> p r t n", t=4)).then_inc(bu_ready, 1)

                split_hi(qa, 1, DT)
                read_bu(0)
                act.wait_ge(bs_done, ct + 1)
                copy(bus[:, :, bass.ds(4 * ct, 4), :],
                     pt[:, 0:2 * 4 * NS].rearrange("p (r t n) -> p r t n", r=2, t=4)).then_inc(bus_ready, 1)
                read_proj(qa, 0, 4 * ct + 4)
                split_hi(qa + 1, 0, DT)
                read_bu(1)
                read_proj(qa, 1, 4 * ct + 5)
                split_hi(qa + 1, 1, DT)
                read_bu(2)
                read_proj(qa + 1, 0, 4 * ct + 6)
                split_hi(qa + 2, 0, k_next)
                read_bu(3)
                read_proj(qa + 1, 1, 4 * ct + 7)

            channel_tile(0, DT, first=True)
            with act.Fori(1, CT - 1) as ct:
                channel_tile(ct, DT)
            channel_tile(CT - 1, GLU[2])

            act.wait_ge(y_all, 1)
            for m in range(CT):
                nc.scalar.activation(proj[:, m], proj[:, m], ACT.Gelu_apprx_tanh).then_inc(gelu_ready, 1)
            for m in range(CT):
                act.wait_ge(gelu_ready, m + 1)
                copy(prompt(h_hi[:, 4 + m]), proj[:, m, 0:SEQ].rearrange("p (h n) -> p h n", h=2))
                copy(sample(h_hi[:, 4 + m]), proj[:, m, SEQ:TOK].rearrange("p (h n) -> p h n", h=2)).then_inc(g_hi_ready, 1)

            def glu_tile(i, k_next):
                pair = i + GLU[0]
                split_hi(pair, 1, GLU[2])
                act.wait_ge(acc_ready[1], pair + 1)
                act.wait_ge(acc_free[0], pair)
                nc.scalar.activation(tmp[0][:], acc[1][:, :, 0:HALF], ACT.Sigmoid).then_inc(acc_free[1], 1)
                split_hi(pair + 1, 0, k_next)
                act.wait_ge(acc_free[0], pair + 1)
                copy(h_hi[:, i], h32[0][:]).then_inc(m_hi_ready, 1)

            with act.Fori(0, GLU[1] - 1) as i:
                glu_tile(i, GLU[2])
            glu_tile(GLU[1] - 1, OUT[2])
            split_hi(OUT[0], 1, OUT[2])

            with act.Fori(0, HEADS) as h:
                half = P // 2
                act.wait_ge(qrot_ready, h + 1)
                copy(flat(h32[0])[0:half], proj[half:P, h + 4])
                copy(flat(h32[0])[half:P], proj[0:half, h + 4]).then_inc(swq_ready, 1)
                act.wait_ge(krot_ready, h + 1)
                copy(flat(h32[1])[0:half], proj[half:P, h + 8])
                copy(flat(h32[1])[half:P], proj[0:half, h + 8]).then_inc(swk_ready, 1)
                act.wait_ge(tv_ready, h + 1)
                copy(vs, proj[:, h + 12]).then_inc(vs_ready, 1)
                act.wait_ge(m32_ready, h + 1)
                nc.scalar.activation(gate[:], proj[:, h + 16], ACT.Silu).then_inc(gate_ready, 1)
                act.wait_ge(tv_ready, h + 2)
                act.wait_ge(snp_ready, h + 1)
                copy(vt[:, 0:4], pt[:].rearrange("p (t n) -> p t n", t=4))
                copy(vt[0:NS, 4], pa[0:NS, 0:DV]).then_inc(vt_ready, 1)
                act.wait_ge(m32_ready, h + 2)
                copy(prompt(h_hi[:, h + 4]), prompt(tmp[1]))
                copy(sample(h_hi[:, h + 4]), sample(tmp[1])).then_inc(m_hi_ready, 1)
            with act.Fori(1, OUT[1]) as i:
                split_hi(i + OUT[0], 0, DT)
                split_hi(i + OUT[0], 1, DT)
            split_hi(UP[2][0], 0, DT)
            norm_root(2)
            norm_hi(2)
            up(UP[2], 0)
            splits(DOWN[2])
            up(UP[3], 0)
            splits(DOWN[3])
            norm_root(3)

        @block.vector
        def _(dve):
            st = Steps(dve, dve_step)
            v = nc.vector
            tt = v.tensor_tensor

            def ada_lo_split(b, u):
                dve.wait_ge(ada_hi_ready, 4 * b + (u + 1))
                tt(ada_lo[u % 2][:], ada_raw[u][:], ada_hi[u % 2][:].bitcast(F32), ALU.subtract).then_inc(ada_lo_ready, 1)

            def read_mod(b):
                dve.wait_ge(ada_turned, b + 1)
                tt(mod[:, bass.ds(4 * b, 4), :], pt[:, 0:4 * NC_].rearrange("p (t n) -> p t n", n=NC_),
                   prmv("bias")[:, bass.ds(4 * b, 4)].unsqueeze(2).broadcast_to([P, 4, NC_]), ALU.add).then_inc(mod_ready, 1)

            def scale_mod(j, sc, blocks):
                dve.wait_ge(mod_ready, blocks)
                gain = prmv("gain")[:, DT * j:DT * j + DT].unsqueeze(2).broadcast_to([P, DT, NC_])
                st.step(v.scalar_tensor_tensor(out=mod[:, sc:sc + DT, :], in0=mod[:, sc:sc + DT, :], scalar=1.0, in1=gain,
                                               op0=ALU.add, op1=ALU.mult))

            def halve_gate(g_, blocks):
                dve.wait_ge(mod_ready, blocks)
                st.step(v.tensor_scalar(mod[:, g_:g_ + DT, :], mod[:, g_:g_ + DT, :], 0.5, None, ALU.mult))

            def modulated(m, s, out, sc, sh):
                st.step(tt(tmp[s][:], x[:, m], root[:], ALU.mult))
                v.tensor_scalar(prompt(out), prompt(tmp[s]), mod[:, m + sc, 0:1], mod[:, m + sh, 0:1], ALU.mult, ALU.add)
                st.step(tt(sample4(out), sample4(tmp[s]), per_seq(mod[:, m + sc, 1:NC_]), ALU.mult))
                return tt(sample4(out), sample4(out), per_seq(mod[:, m + sh, 1:NC_]), ALU.add)

            def norm_rstd(j):
                dve.wait_ge(root_ready, j + 1)
                st.step(v.reciprocal(root[:], root[:]))

            def norm(j, sc, sh):
                norm_rstd(j)

                def two(i, wait=True):
                    for s in range(2):
                        if wait:
                            dve.wait_ge(h_lo_ready, 2 * i + (DT * j + s - 1))
                        modulated(2 * i + s, s, h32[s], sc, sh).then_inc(h32_ready, 1)
                if j == 0:
                    two(0, wait=False)
                with st.loop(1 if j == 0 else 0, DT // 2, 4) as i:
                    two(i)

            def up(phase, block0):
                first = phase[0]

                def hidden(f, ada, turned=None):
                    pair = f + first
                    b = f + block0
                    if ada:
                        ada_lo_split(b, 0)
                        ada_lo_split(b, 1)
                        if not (isinstance(f, int) and f == 0):
                            read_mod(b - 1)
                        ada_lo_split(b, 2)
                        ada_lo_split(b, 3)
                    if turned is not None:
                        read_mod(turned)
                    dve.wait_ge(acc_free[0], pair + 1)
                    dve.wait_ge(acc_ready[1], pair + 1)
                    if not (isinstance(f, int) and f == 0):
                        dve.wait_ge(hid_lo_ready, f + HT * UP.index(phase))
                    tt(h32[0][:], tmp[0][:], acc[1][:, :, 0:HALF], ALU.mult).then_inc(acc_free[1], 1)
                    dve.wait_ge(acc_free[1], pair + 1)
                    dve.wait_ge(hid_hi_ready, f + (HT * UP.index(phase) + 1))
                    tt(hid_lo[:, f], h32[0][:], hid_hi[:, f].bitcast(F32), ALU.subtract).then_inc(hid_lo_ready, 1)

                if block0:
                    hidden(0, True)
                    with dve.Fori(1, 9) as f:
                        hidden(f, True)
                    hidden(9, False, turned=block0 + 8)
                    hidden(10, False)
                else:
                    with dve.Fori(0, HT) as f:
                        hidden(f, False)

            def residual(pair, s, m, gate_, square):
                dve.wait_ge(acc_ready[s], pair + 1)
                st.mark(v.scalar_tensor_tensor(out=prompt(x[:, m]), in0=prompt(acc[s]), scalar=mod[:, m + gate_, 0:1],
                                               in1=prompt(x[:, m]), op0=ALU.mult, op1=ALU.add))
                tt(sample4(h32[s]), sample4(acc[s]), per_seq(mod[:, m + gate_, 1:NC_]), ALU.mult).then_inc(acc_free[s], 1)
                dve.wait_ge(acc_free[s], pair + 1)
                st.step(tt(sample(x[:, m]), sample(x[:, m]), sample(h32[s]), ALU.add))
                if square:
                    st.step(tt(tmp[s][:], x[:, m], x[:, m], ALU.mult))
                    st.step(tt(sumsq[:], sumsq[:], tmp[s][:], ALU.add))

            def residuals(phase, gate_, square, extra=None, extra_steps=0):
                if phase in DOWN:
                    dve.wait_ge(hid_lo_ready, HT * (DOWN.index(phase) + 1))
                else:
                    dve.wait_ge(m_lo_ready, GLU[1] + HEADS)
                if square:
                    st.step(v.memset(sumsq[:], 0.0))
                with st.loop(0, 4, (8 if square else 4) + extra_steps) as i:
                    for s in range(2):
                        residual(i + phase[0], s, 2 * i + s, gate_, square)
                    if extra:
                        extra(i)
                if square:
                    dve.sem_inc(sumsq_ready, 1)

            v.memset(eps_t[:], EPS).then_inc(eps_ready, 1)
            dve.wait_ge(c_hi_ready, 1)
            tt(c_split[:, :, NC_:2 * NC_], h32[0][:, 0, 0:DT * NC_].rearrange("p (t n) -> p t n", n=NC_),
               c_split[:, :, 0:NC_].bitcast(F32), ALU.subtract).then_inc(c_ready, 1)
            ada_lo_split(0, 0)
            ada_lo_split(0, 1)
            lam = prmv("lam").rearrange("p (a t) -> p a t", a=3)
            dve.wait_ge(s5_exp, 1)
            st.mark(tt(s5t[:, 1], lam[:, 0], s5t[:, 0], ALU.mult))
            st.step(tt(s5t[:, 2], lam[:, 1], s5t[:, 0], ALU.mult))
            magic = 1.5 * 2.0 ** 23
            st.step(v.tensor_scalar(s5t[:, 4], s5t[:, 2], float(1 / (2 * np.pi)), magic, ALU.mult, ALU.add))
            st.step(v.tensor_scalar(s5t[:, 4], s5t[:, 4], magic, None, ALU.subtract))
            for part in TWO_PI:
                st.step(v.scalar_tensor_tensor(out=s5t[:, 2], in0=s5t[:, 4], scalar=-part, in1=s5t[:, 2],
                                               op0=ALU.mult, op1=ALU.add))
            st.step(v.tensor_scalar(s5t[:, 2], s5t[:, 2], PI_LOW, -PI_LOW, ALU.min, ALU.max))
            st.step(v.tensor_scalar(s5t[:, 5], s5t[:, 2], -1.0, None, ALU.mult))
            st.step(tt(s5t[:, 3], s5t[:, 2], s5t[:, 5], ALU.max))
            v.tensor_scalar(s5t[:, 3], s5t[:, 3], -1.0, float(np.pi / 2), ALU.mult, ALU.add).then_inc(s5_angle, 1)
            ada_lo_split(0, 2)
            ada_lo_split(0, 3)
            with dve.Fori(1, 4) as b:
                ada_lo_split(b, 0)
                ada_lo_split(b, 1)
                read_mod(b - 1)
                ada_lo_split(b, 2)
                ada_lo_split(b, 3)
            read_mod(3)
            scale_mod(0, SC1, 4)

            norm(0, SC1, SH1)
            up(UP[0], 4)
            halve_gate(G1, 13)

            dve.wait_ge(s5_trig, 1)
            pr, pi = s5pow[:, 0], s5pow[:, 1]
            t0, t1, t2, t3 = (s5t[:, n] for n in (4, 5, 6, 7))

            def unit_length(k):
                st.mark(tt(t0, pr[:, k], pr[:, k], ALU.mult))
                st.step(tt(t1, pi[:, k], pi[:, k], ALU.mult))
                st.step(tt(t0, t0, t1, ALU.add))
                st.step(v.tensor_scalar(t0, t0, -0.5, 1.5, ALU.mult, ALU.add))
                st.mark(tt(pr[:, k], pr[:, k], t0, ALU.mult))
                st.step(tt(pi[:, k], pi[:, k], t0, ALU.mult))

            for k in range(8):
                if k:
                    st.mark(tt(t0, pr[:, k - 1], pr[:, k - 1], ALU.mult))
                    st.mark(tt(t1, pi[:, k - 1], pi[:, k - 1], ALU.mult))
                    st.step(tt(t2, pr[:, k - 1], pi[:, k - 1], ALU.mult))
                    st.mark(tt(pr[:, k], t0, t1, ALU.subtract))
                    st.step(v.tensor_scalar(pi[:, k], t2, 2.0, None, ALU.mult))
                unit_length(k)
            st.mark(tt(s5lam[:, 0], s5r[:], pr[:, 0], ALU.mult))
            st.step(tt(s5lam[:, 1], s5r[:], pi[:, 0], ALU.mult))
            st.mark(tt(t0, lam[:, 0], lam[:, 0], ALU.mult))
            st.mark(tt(t1, lam[:, 1], lam[:, 1], ALU.mult))
            st.step(v.tensor_scalar(t2, s5lam[:, 0], 1.0, None, ALU.subtract))
            st.step(tt(t0, t0, t1, ALU.add))
            st.step(v.reciprocal(t3, t0))
            st.mark(tt(t0, t2, lam[:, 0], ALU.mult))
            st.step(tt(t1, s5lam[:, 1], lam[:, 1], ALU.mult))
            st.step(tt(t0, t0, t1, ALU.add))
            st.step(tt(s5beta[:, 0], t0, t3, ALU.mult))
            st.mark(tt(t0, s5lam[:, 1], lam[:, 0], ALU.mult))
            st.step(tt(t1, t2, lam[:, 1], ALU.mult))
            st.step(tt(t0, t0, t1, ALU.subtract))
            st.step(tt(s5beta[:, 1], t0, t3, ALU.mult))
            dve.wait_ge(b_in, 32)

            def by_tile(t):
                return flat(t)[:, 0:NT * 32].rearrange("p (t c) -> p t c", t=NT)
            br, bi = by_tile(tmp[0]), by_tile(tmp[1])
            beta_r, beta_i = (s5beta[:, n].unsqueeze(2).broadcast_to([P, NT, 32]) for n in range(2))
            st.mark(tt(by_tile(h32[0]), br, beta_r, ALU.mult))
            st.step(tt(by_tile(root), bi, beta_i, ALU.mult))
            st.mark(tt(by_tile(h32[0]), by_tile(h32[0]), by_tile(root), ALU.subtract))
            st.mark(tt(by_tile(h32[1]), br, beta_i, ALU.mult))
            st.step(tt(by_tile(sumsq), bi, beta_r, ALU.mult))
            tt(by_tile(h32[1]), by_tile(h32[1]), by_tile(sumsq), ALU.add).then_inc(bbar_ready, 1)
            st.mark(v.memset(et[:, 0, :, 0:1], 1.0))
            st.step(v.memset(et[:, 1, :, 0:1], 0.0))

            def table(i):
                for k in range(7):
                    n = 2 ** k
                    er, ei = (et[:, r, bass.ds(4 * i, 4), 0:n] for r in range(2))
                    o_r, o_i = (et[:, r, bass.ds(4 * i, 4), n:2 * n] for r in range(2))
                    qr, qi = (s5pow[:, r, k, bass.ds(4 * i, 4)].unsqueeze(2).broadcast_to([P, 4, n]) for r in range(2))
                    u0, u1, u2, u3 = (view4(t)[:, :, 0:n] for t in (tmp[0], tmp[1], root, sumsq))
                    st.mark(tt(u0, er, qr, ALU.mult))
                    st.mark(tt(u1, ei, qi, ALU.mult))
                    st.mark(tt(u2, er, qi, ALU.mult))
                    st.step(tt(u3, ei, qr, ALU.mult))
                    st.mark(tt(o_r, u0, u1, ALU.subtract))
                    st.step(tt(o_i, u2, u3, ALU.add))

            dve.wait_ge(bbar_turned, 1)
            residuals(DOWN[0], G1, False, extra=table, extra_steps=42)
            dve.sem_inc(table_done, 1)
            up(UP[1], 13)
            halve_gate(G3, 22)
            scale_mod(1, SC2, 22)
            scale_mod(2, SC3, 22)
            scale_mod(3, SCF, 22)
            residuals(DOWN[1], G1, True)
            norm(1, SC2, SH2)

            v.memset(lbs[:], 0.0).then_inc(lbs_clear, 1)
            dve.sem_inc(bu_used, 2)
            dve.sem_inc(y_used, 1)

            def read_y(ct, j):
                gi = 4 * ct + j
                dve.wait_ge(y_ready, gi + 3)
                v.scalar_tensor_tensor(out=proj[:, ct, SEG * j:SEG * (j + 1)], in0=proj[:, ct, SEG * j:SEG * (j + 1)],
                                       scalar=prm[:, bass.ds(ct + PRM["skip"][0], 1)], in1=pa[:, 0:SEG],
                                       op0=ALU.mult, op1=ALU.add).then_inc(y_used, 1)

            def segment(ct, j):
                gi, b = 4 * ct + j, j % 2
                er, ei = et[:, 0, bass.ds(4 * ct, 4), :], et[:, 1, bass.ds(4 * ct, 4), :]
                u0, u1 = view4(tmp[0]), view4(tmp[1])
                dve.wait_ge(bu_ready, gi + 2)
                dve.wait_ge(xi_ready, gi + 1)
                bur, bui = bu[b][:, 0], bu[b][:, 1]
                st.mark(tt(u0, bur, er, ALU.mult))
                st.step(tt(u1, bui, ei, ALU.mult))
                st.step(tt(z[b][:, 0], u0, u1, ALU.add))
                st.mark(tt(u0, bui, er, ALU.mult))
                tt(u1, bur, ei, ALU.mult).then_inc(bu_used, 1)
                dve.wait_ge(bu_used, gi + 3)
                st.step(tt(z[b][:, 1], u0, u1, ALU.subtract))
                for r in range(2):
                    for t in range(4):
                        first = 0.0 if j == 0 else carry[:, r, t:t + 1]
                        ins = v.tensor_tensor_scan(z[b][:, r, t], s5r[:, bass.ds(4 * ct + t, 1)].broadcast_to([P, SEG]),
                                                   z[b][:, r, t], first, ALU.mult, ALU.add)
                ins.then_inc(z_ready, 1)
                dve.wait_ge(z_ready, gi + 1)
                st.mark(tt(u0, z[b][:, 0], er, ALU.mult))
                st.step(tt(u1, z[b][:, 1], ei, ALU.mult))
                dve.wait_ge(y_ready, gi + 1)
                tt(xc[b][:, 0], u0, u1, ALU.subtract).then_inc(xr_ready, 1)
                if j < 3:
                    qr, qi = (s5pow[:, r, 7, bass.ds(4 * ct, 4)] for r in range(2))
                    zr, zi = z[b][:, 0, :, SEG - 1], z[b][:, 1, :, SEG - 1]
                    st.mark(tt(ct4[:, 0], zr, qr, ALU.mult))
                    st.mark(tt(ct4[:, 1], zi, qi, ALU.mult))
                    st.mark(tt(ct4[:, 2], zr, qi, ALU.mult))
                    st.step(tt(ct4[:, 3], zi, qr, ALU.mult))
                    st.mark(tt(carry[:, 0], ct4[:, 0], ct4[:, 1], ALU.subtract))
                    st.step(tt(carry[:, 1], ct4[:, 2], ct4[:, 3], ALU.add))
                else:
                    dve.wait_ge(xr_ready, gi + 1)
                    v.tensor_copy(x_last[:, 0, bass.ds(4 * ct, 4)], xc[1][:, 0, :, SEG - 1]).then_inc(x_last_ready, 1)
                if j:
                    read_y(ct, j - 1)

            with st.loop(0, CT, 4 * 7 + 3 * 6) as ct:
                for j in range(4):
                    segment(ct, j)
                read_y(ct, 3)

            dve.wait_ge(h0_in, 16)
            dve.wait_ge(bus_ready, CT + 1)
            bus5 = bus[:].rearrange("p r t (b s) -> p r t b s", s=DEC_SEQ)
            w = [view(t, NT * DEC_BATCH).rearrange("p (t b) -> p t b", t=NT) for t in (tmp[0], tmp[1], h32[0], h32[1])]
            lr, li = (s5lam[:, r].unsqueeze(2).broadcast_to([P, NT, DEC_BATCH]) for r in range(2))
            for s in range(DEC_SEQ):
                qr, qi = (h0[:, r] if s == 0 else xs[:, r, :, :, s - 1] for r in range(2))
                st.mark(tt(w[0], qr, lr, ALU.mult))
                st.mark(tt(w[1], qi, li, ALU.mult))
                st.mark(tt(w[2], qr, li, ALU.mult))
                st.step(tt(w[3], qi, lr, ALU.mult))
                st.mark(tt(w[0], w[0], w[1], ALU.subtract))
                st.step(tt(w[2], w[2], w[3], ALU.add))
                st.mark(tt(xs[:, 0, :, :, s], w[0], bus5[:, 0, :, :, s], ALU.add))
                st.step(tt(xs[:, 1, :, :, s], w[2], bus5[:, 1, :, :, s], ALU.add))
            dve.sem_inc(xs_ready, 1)
            v.tensor_copy(xs_last[:], xs[:, :, :, :, DEC_SEQ - 1]).then_inc(xs_last_ready, 1)
            skip = prmv("skip").unsqueeze(2).broadcast_to([P, CT, NS])
            u_s = proj[:, 0:CT, SEQ:TOK]
            st.step(tt(u_s, u_s, skip, ALU.mult))
            dve.wait_ge(ys_ready, 1)
            st.step(tt(u_s, u_s, pa[:, 0:CT * NS].rearrange("p (t n) -> p t n", t=CT), ALU.add))
            dve.wait_ge(y_used, 17)
            dve.sem_inc(y_all, 1)
            for m in range(CT):
                dve.wait_ge(g_hi_ready, m + 1)
                tt(prompt(h_lo[:, 4 + m]), proj[:, m, 0:SEQ].rearrange("p (h n) -> p h n", h=2),
                   prompt(h_hi[:, 4 + m]).bitcast(F32), ALU.subtract)
                tt(sample(h_lo[:, 4 + m]), proj[:, m, SEQ:TOK].rearrange("p (h n) -> p h n", h=2),
                   sample(h_hi[:, 4 + m]).bitcast(F32), ALU.subtract).then_inc(g_lo_ready, 1)

            def glu_tile(i, first=False):
                pair = i + GLU[0]
                if not first:
                    dve.wait_ge(m_lo_ready, i)
                dve.wait_ge(acc_free[1], pair + 1)
                dve.wait_ge(acc_ready[0], pair + 1)
                tt(h32[0][:], tmp[0][:], acc[0][:, :, 0:HALF], ALU.mult).then_inc(acc_free[0], 1)
                dve.wait_ge(acc_free[0], pair + 1)
                dve.wait_ge(m_hi_ready, i + 1)
                tt(h_lo[:, i], h32[0][:], h_hi[:, i].bitcast(F32), ALU.subtract).then_inc(m_lo_ready, 1)

            glu_tile(0, first=True)
            with dve.Fori(1, GLU[1]) as i:
                glu_tile(i)

            st.step(v.memset(mv[:], 1.0))
            dve.sem_inc(qrot_ready, 1)
            dve.sem_inc(m32_ready, 1)
            dve.wait_ge(rope_in, 16)
            with st.loop(0, HEADS, 2 + 5 + 1) as h:
                dve.wait_ge(swq_ready, h + 1)
                dve.wait_ge(o_ready, h + 1)
                st.mark(tt(qs[:], proj[:, h + 4], rope[:, 0], ALU.mult))
                st.step(tt(flat(h32[0]), flat(h32[0]), rope[:, 1], ALU.mult))
                tt(qs[:], qs[:], flat(h32[0]), ALU.add).then_inc(qrot_ready, 1)
                dve.wait_ge(hc_in, 16 * h + 16)
                dve.wait_ge(qrot_ready, h + 2)
                tt(qm[:], qs[:, SEQ:TOK].unsqueeze(1).broadcast_to([P, DEC_BATCH, NS]),
                   hcv("qmask").rearrange("p (b n) -> p b n", b=DEC_BATCH), ALU.mult).then_inc(qm_ready, 1)
                dve.wait_ge(tk_ready, h + 1)
                dve.wait_ge(snp_ready, h + 1)
                tt(kt[:, 0:4], pn[:, 0].rearrange("p (t n) -> p t n", t=4),
                   hcv("kdec")[:, 0:4].unsqueeze(2).broadcast_to([P, 4, DK]), ALU.mult)
                v.tensor_scalar(kt[0:NS, 4], pn[0:NS, 1, 0:DK], hcv("kdec")[0:NS, 4:5], None, ALU.mult).then_inc(kt_ready, 1)
                dve.wait_ge(scores_ready, h + 1)
                at = 0
                for t in range(4):
                    n = SEQ - P * t
                    tt(sc[:, at:at + n], acc[t // 2][:, t % 2, 0:n], hcv("mask")[:, 0:n], ALU.mult)
                    at += n
                tt(scs[:], acc[1][0:NS, 1, P:P + NS], hcv("smask")[0:NS], ALU.mult).then_inc(scm_ready, 1)
                dve.wait_ge(spp_ready, h + 1)
                v.tensor_copy(sp_out[:], pn[:, 0, 0:DV]).then_inc(sp_ready, 1)
                dve.wait_ge(o_ready, h + 2)
                for t in range(5):
                    rows = P if t < 4 else NS
                    src = pt[:, DV * t:DV * t + DV] if t < 4 else pa[0:NS, 0:DV]
                    st.step(v.bn_stats(stat[0:rows, t], src))
                dve.sem_inc(dve_settled, 1)
                for t in range(4):
                    v.bn_aggr(mv[:, t], stat[:, t])
                v.bn_aggr(mv[0:NS, 4], stat[0:NS, 4]).then_inc(mv_ready, 1)
                dve.wait_ge(snp_ready, h + 2)
                v.scalar_tensor_tensor(out=sn[:].rearrange("p (c b) v -> p c (b v)", c=2),
                                       in0=s0[:].rearrange("p (c b) v -> p c (b v)", c=2), scalar=hcv("g4"), in1=acc[0][:],
                                       op0=ALU.mult, op1=ALU.add).then_inc(sn_ready, 1)
                dve.wait_ge(hrstd_ready, h + 1)
                for t in range(5):
                    rows = P if t < 4 else NS
                    src = pt[:, DV * t:DV * t + DV] if t < 4 else pa[0:NS, 0:DV]
                    ins = v.tensor_scalar(on[0:rows, t], src, mv[0:rows, t, 0:1], hrstd[0:rows, t], ALU.subtract, ALU.mult)
                ins.then_inc(on_ready, 1)
                dve.wait_ge(ot_ready, h + 1)
                dve.wait_ge(gate_ready, h + 1)
                st.mark(tt(prompt(tmp[1]), acc[1][:, 0].rearrange("p (h n) -> p h n", h=2),
                           gate[:, 0:SEQ].rearrange("p (h n) -> p h n", h=2), ALU.mult))
                tt(sample(tmp[1]), acc[1][:, 1, 0:NS].rearrange("p (h n) -> p h n", h=2),
                   gate[:, SEQ:TOK].rearrange("p (h n) -> p h n", h=2), ALU.mult).then_inc(m32_ready, 1)
                dve.wait_ge(m_hi_ready, h + (GLU[1] + 1))
                tt(h_lo[:, h + 4], tmp[1][:], h_hi[:, h + 4].bitcast(F32), ALU.subtract).then_inc(m_lo_ready, 1)
            residuals(OUT, G2, True)
            norm(2, SC3, SH3)
            up(UP[2], 0)
            residuals(DOWN[2], G3, False)
            up(UP[3], 0)
            residuals(DOWN[3], G3, True)
            norm_rstd(3)
            with st.loop(0, DT // 2, 4) as i:
                for s in range(2):
                    modulated(2 * i + s, s, x[:, 2 * i + s], SCF, SHF).then_inc(y_tile, 1)

        @block.tensor
        def _(pe):
            mm = nc.tensor.matmul

            def unit(pair, s, k, r_hi, r_lo, first_use=False, ready=None, at=0):
                pe.wait_ge(hi_ready[s], pair + 1)
                if not first_use:
                    pe.wait_ge(acc_free[s], pair)
                for t in range(k):
                    if ready:
                        pe.wait_ge(ready[0], ready[1] + t + 1)
                    for r in (r_hi, r_lo):
                        for c in range(2):
                            mm(acc[s][:, c, 0:HALF], w_hi[s][:, t], r[:, at + t, c], start=(t == 0 and r is r_hi), stop=False)
                pe.wait_ge(lo_ready[s], pair + 1)
                for t in range(k):
                    for c in range(2):
                        ins = mm(acc[s][:, c, 0:HALF], w_lo[s][:, t], r_hi[:, at + t, c], start=False, stop=(t == k - 1))
                ins.then_inc(acc_ready[s], 1)

            def ada_unit(b, u):
                pe.wait_ge(ada_lo_ready, 4 * b + (u + 1))
                if u == 0 and not (isinstance(b, int) and b == 0):
                    pe.wait_ge(ada_row_ready, b)
                for w, part in ((ada_hi[u % 2], 0), (ada_lo[u % 2], 1)):
                    for k in range(2):
                        ins = mm(pa[0:2 * NC_, :], c_split[:, 2 * u + k], w[:, k],
                                 start=(u == 0 and part == 0 and k == 0), stop=(u == 3 and part == 1 and k == 1))
                ins.then_inc(ada_used, 1)

            def ada_turn(b):
                pe.wait_ge(ada_row_ready, b + 1)
                if not (isinstance(b, int) and b == 0):
                    pe.wait_ge(mod_ready, b)
                for t in range(4):
                    ins = mm(pt[:, NC_ * t:NC_ * (t + 1)], ada_row[:, P * t:P * (t + 1)], prmv("sel")[0:2 * NC_],
                             start=True, stop=True)
                ins.then_inc(ada_turned, 1)

            def mean_square(j):
                pe.wait_ge(sumsq_ready, j + 1)
                for c in range(2):
                    ins = mm(pn[:, c, 0:HALF], prmv("mean"), sumsq[:, c], start=True, stop=True)
                ins.then_inc(ms_ready, 1)

            def up(phase, block0, j=None):
                first, n, k = phase

                def hidden(f, ada, first_use=False, ready=None, turned=None):
                    unit(f + first, 0, k, h_hi, h_lo, first_use, ready)
                    if ada:
                        if not (isinstance(f, int) and f == 0):
                            ada_turn(f + (block0 - 1))
                        ada_unit(f + block0, 0)
                        ada_unit(f + block0, 1)
                    if turned is not None:
                        ada_turn(turned)
                    unit(f + first, 1, k, h_hi, h_lo, first_use)
                    if ada:
                        ada_unit(f + block0, 2)
                        ada_unit(f + block0, 3)

                ready = None if j is None else (h_lo_ready, DT * j)
                if block0:
                    hidden(0, True, first_use=(first == 0), ready=ready)
                    with pe.Fori(1, 9) as f:
                        hidden(f, True)
                    hidden(9, False, turned=block0 + 8)
                    hidden(10, False)
                else:
                    hidden(0, False, ready=ready)
                    with pe.Fori(1, n) as f:
                        hidden(f, False)

            def down(phase):
                first, n, k = phase
                unit(first, 0, k, hid_hi, hid_lo, ready=(hid_lo_ready, HT * DOWN.index(phase)))
                unit(first, 1, k, hid_hi, hid_lo)
                with pe.Fori(1, n) as i:
                    unit(i + first, 0, k, hid_hi, hid_lo)
                    unit(i + first, 1, k, hid_hi, hid_lo)

            pe.wait_ge(prm_in, 16)
            pe.wait_ge(c_ready, 1)
            pe.wait_ge(c_hi_ready, 1)
            for u in range(4):
                ada_unit(0, u)
            with pe.Fori(1, 4) as b:
                ada_unit(b, 0)
                ada_unit(b, 1)
                ada_turn(b - 1)
                ada_unit(b, 2)
                ada_unit(b, 3)
            ada_turn(3)
            mean_square(0)
            up(UP[0], 4, j=0)
            pe.wait_ge(bbar_ready, 1)
            for r in range(2):
                for t in range(CT):
                    ins = nc.tensor.transpose(pn[:, r, P * t:P * (t + 1)], flat(h32[r])[:, P * t:P * (t + 1)], prmv("ident"))
            ins.then_inc(bbar_turned, 1)
            down(DOWN[0])
            up(UP[1], 13)
            down(DOWN[1])
            mean_square(1)

            unit(PROJ_U[0], 0, DT, h_hi, h_lo, ready=(h_lo_ready, DT))
            unit(PROJ_U[0], 1, DT, h_hi, h_lo)
            unit(PROJ_U[0] + 1, 0, DT, h_hi, h_lo)
            unit(PROJ_U[0] + 1, 1, DT, h_hi, h_lo)
            pe.sem_inc(y_ready, 2)
            with pe.Fori(0, CT) as ct:
                qa = 2 * ct + PROJ_REST[0]

                def b_u(j):
                    pe.wait_ge(bu_ready, 4 * ct + (j + 1))
                    for r in range(2):
                        for t in range(4):
                            ins = mm(pn[:, r, SEG * t:SEG * (t + 1)], lbs[:, r, t], us[:, SEG * j:SEG * (j + 1)],
                                     start=True, stop=True)
                    ins.then_inc(b_done, 1)

                def c_x(j):
                    b = j % 2
                    pe.wait_ge(xr_ready, 4 * ct + (j + 1))
                    pe.wait_ge(xi_ready, 4 * ct + (j + 3))
                    pe.wait_ge(y_used, 4 * ct + (j + 1))
                    for t in range(4):
                        for r in range(2):
                            ins = mm(pa[32 * t:32 * t + 32, 0:SEG], lcs[:, t, r], xc[b][:, r, t], start=(r == 0), stop=(r == 1))
                    ins.then_inc(y_ready, 1)

                pe.wait_ge(staged, ct + 1)
                b_u(0)
                pe.wait_ge(bus_ready, ct + 1)
                for r in range(2):
                    for t in range(4):
                        ins = mm(pt[:, (4 * r + t) * NS:(4 * r + t + 1) * NS], lbs[:, r, t], us[:, SEQ:TOK], start=True, stop=True)
                ins.then_inc(bs_done, 1)
                unit(qa, 0, DT, h_hi, h_lo)
                b_u(1)
                c_x(0)
                unit(qa, 1, DT, h_hi, h_lo)
                b_u(2)
                c_x(1)
                unit(qa + 1, 0, DT, h_hi, h_lo)
                b_u(3)
                c_x(2)
                unit(qa + 1, 1, DT, h_hi, h_lo)
                c_x(3)

            pe.wait_ge(xs_ready, 1)
            pe.wait_ge(y_used, 17)
            for ct in range(CT):
                for t in range(4):
                    for r in range(2):
                        ins = mm(pa[32 * t:32 * t + 32, NS * ct:NS * (ct + 1)], lc[:, 4 * ct + t, r],
                                 xs[:, r, 4 * ct + t].rearrange("p b s -> p (b s)"), start=(r == 0), stop=(r == 1))
            ins.then_inc(ys_ready, 1)

            unit(GLU[0], 0, GLU[2], h_hi, h_lo, ready=(g_lo_ready, 0), at=4)
            unit(GLU[0], 1, GLU[2], h_hi, h_lo, at=4)
            with pe.Fori(1, GLU[1]) as i:
                unit(i + GLU[0], 0, GLU[2], h_hi, h_lo, at=4)
                unit(i + GLU[0], 1, GLU[2], h_hi, h_lo, at=4)

            for free in (tv_ready, snp_ready, o_ready):
                pe.sem_inc(free, 1)
            for s in range(2):
                pe.wait_ge(acc_free[s], OUT[0])
            with pe.Fori(0, HEADS) as h:
                ident = prmv("ident")
                pe.wait_ge(vs_ready, h + 1)
                pe.wait_ge(m32_ready, h + 1)
                for t in range(4):
                    nc.tensor.transpose(pt[:, DV * t:DV * (t + 1)], vs[:, P * t:P * (t + 1)], ident)
                nc.tensor.transpose(pa[0:NS, 0:DV], vs[:, SEQ:TOK], ident).then_inc(tv_ready, 1)
                pe.wait_ge(krot_ready, h + 2)
                for t in range(4):
                    nc.tensor.transpose(pn[:, 0, DK * t:DK * (t + 1)], ks[:, P * t:P * (t + 1)], ident)
                nc.tensor.transpose(pn[0:NS, 1, 0:DK], ks[:, SEQ:TOK], ident).then_inc(tk_ready, 1)
                pe.wait_ge(qrot_ready, h + 2)
                for t in range(4):
                    n = SEQ - P * t
                    mm(acc[t // 2][:, t % 2, 0:n], ks[:, P * t:P * (t + 1)], qs[:, P * t:SEQ], start=True, stop=True)
                mm(acc[1][0:NS, 1, P:P + NS], ks[:, SEQ:TOK], qs[:, SEQ:TOK], start=True, stop=True).then_inc(scores_ready, 1)
                pe.wait_ge(kt_ready, h + 1)
                pe.wait_ge(vt_ready, h + 1)
                for t in range(4):
                    ins = mm(pn[:, 0, 0:DV], kt[:, t], vt[:, t], start=(t == 0), stop=(t == 3))
                ins.then_inc(spp_ready, 1)
                pe.wait_ge(scm_ready, h + 1)
                for qt in range(4):
                    for t in range(qt + 1):
                        at = sum(SEQ - P * n for n in range(t)) + P * (qt - t)
                        mm(pt[:, DV * qt:DV * (qt + 1)], sc[:, at:at + P], vt[:, t], start=(t == 0), stop=(t == qt))
                pe.wait_ge(qm_ready, h + 1)
                pe.wait_ge(s0_in, 16 * h + 16)
                for b in range(DEC_BATCH):
                    mm(pa[0:NS, 0:DV], qm[:, b], s0[:, b], start=(b == 0), stop=False)
                mm(pa[0:NS, 0:DV], scs[:], vt[0:NS, 4], start=False, stop=True).then_inc(o_ready, 1)
                pe.wait_ge(vm_ready, h + 1)
                for c in range(2):
                    ins = mm(acc[0][:, c], kt[0:NS, 4], vm[0:NS, 4 * c:4 * c + 4].rearrange("p b v -> p (b v)"),
                             start=True, stop=True)
                ins.then_inc(snp_ready, 1)
                pe.wait_ge(on_ready, h + 1)
                for t in range(4):
                    nc.tensor.transpose(acc[1][:, 0, P * t:P * (t + 1)], on[:, t], ident)
                nc.tensor.transpose(acc[1][:, 1, 0:NS], on[0:NS, 4], prmv("ident")[0:NS, 0:NS]).then_inc(ot_ready, 1)

            unit(OUT[0], 0, DT, h_hi, h_lo, ready=(m_lo_ready, 0))
            unit(OUT[0], 1, DT, h_hi, h_lo)
            with pe.Fori(1, OUT[1]) as i:
                unit(i + OUT[0], 0, DT, h_hi, h_lo)
                unit(i + OUT[0], 1, DT, h_hi, h_lo)
            mean_square(2)
            up(UP[2], 0, j=2)
            down(DOWN[2])
            up(UP[3], 0)
            down(DOWN[3])
            mean_square(3)


def head_constants():
    out = np.zeros((HEADS, P, HC_N), np.float32)
    scale = np.float32(DK) ** np.float32(-0.5)
    i = np.arange(P)
    for h in range(HEADS):
        lg = np.log1p(-np.exp2(-5.0 - h))
        d = np.arange(SEQ)[None, :] - i[:, None]
        out[h, :, slice(*HC["mask"])] = np.where(d >= 0, np.exp(lg * np.maximum(d, 0)), 0.0) * scale
        n = np.arange(NS)
        seq, s = n // DEC_SEQ, n % DEC_SEQ
        qmask = (seq[None, :] == np.arange(DEC_BATCH)[:, None]) * np.exp(lg * (s + 1.0))[None, :]
        out[h, :, slice(*HC["qmask"])] = qmask.reshape(1, -1)
        kdec = np.zeros((P, 5))
        for t in range(4):
            kdec[:, t] = np.exp(lg * (SEQ - 1.0 - (P * t + i))) * scale
        kdec[:NS, 4] = np.exp(lg * (DEC_SEQ - 1.0 - s)) * scale
        out[h, :, slice(*HC["kdec"])] = kdec
        out[h, :, slice(*HC["g4"])] = np.exp(lg * DEC_SEQ)
        same = (seq[:, None] == seq[None, :]) & (s[None, :] >= s[:, None])
        out[h, :NS, slice(*HC["smask"])] = np.where(same, np.exp(lg * np.maximum(s[None, :] - s[:, None], 0)), 0.0) * scale
        out[h, :NS, slice(*HC["bmask"])] = seq[:, None] == np.arange(DEC_BATCH)[None, :]
    return out


def rope_table():
    half = DK // 2
    inv = (np.float32(10000.0) ** (-np.arange(half, dtype=np.float32) / np.float32(half))).astype(np.float32)
    pos = np.concatenate([np.arange(SEQ), PAST_LEN + np.tile(np.arange(DEC_SEQ), DEC_BATCH)]).astype(np.float32)
    ang = (pos[None, :] * inv[:, None]).astype(np.float32).astype(np.float64)
    cos, sin = np.cos(ang), np.sin(ang)
    return np.stack([np.concatenate([cos, cos]), np.concatenate([-sin, sin])], 1).astype(np.float32).reshape(P, 2 * TOK)


_OUTS = {"y": (DT, P, TOK), "ssm_prompt": (P, 2 * NT), "ssm_sample": (P, 2 * NT * DEC_BATCH),
         "ret_prompt": (HEADS, DK, DV), "ret_sample": (HEADS, DK, DEC_BATCH * DV)}


def kernel(**inputs):
    import concourse.bacc as bacc
    from concourse.bass_utils import run_bass_kernel_spmd

    v = {n: np.asarray(t) for n, t in inputs.items()}
    one = {n: t[0] if t.shape[0] == 1 and n not in ("x_prompt", "c_prompt") else t for n, t in v.items()}

    def tiled(w, k, m, order):
        return np.ascontiguousarray(w.reshape(k + m).transpose(order))

    feeds = {}
    xp = v["x_prompt"].reshape(HALVES, HP, D_MODEL)
    xs_ = v["x_sample"].reshape(HALVES, HS, D_MODEL)
    xt = np.concatenate([xp, xs_], 1)
    feeds["x"] = np.ascontiguousarray(xt.reshape(HALVES, HALF, DT, P).transpose(3, 2, 0, 1)).reshape(P, -1)
    for n in (1, 2):
        w = one[f"ffn{n}_w_in"]
        feeds[f"ffn{n}_up"] = tiled(w, (DT, P), (2, FT, P), (3, 2, 1, 0, 4)).reshape(FT, 2, P, DT * P)
        w = one[f"ffn{n}_w_out"]
        feeds[f"ffn{n}_down"] = np.ascontiguousarray(
            w.reshape(2, HT, P, DT, P).transpose(0, 3, 2, 1, 4)).reshape(2 * 4, 2, P, HT * P)
    feeds["w_in"] = tiled(one["w_in_mix"], (DT, P), (20, P), (2, 1, 0, 3)).reshape(10, 2, P, DT * P)
    feeds["w_glu"] = tiled(one["s5_w_glu"], (4, P), (2, 4, P), (3, 2, 1, 0, 4)).reshape(4, 2, P, 4 * P)
    feeds["w_out"] = tiled(one["w_out_mix"], (DT, P), (DT, P), (2, 1, 0, 3)).reshape(4, 2, P, DT * P)
    wa = np.concatenate([one["w_ada"], v["w_ada_final"]], 1)
    feeds["ada"] = tiled(wa, (4, 2, P), (ADA_BLOCKS, ADA_N), (3, 0, 2, 1, 4)).reshape(ADA_BLOCKS, 4, P, 2 * ADA_N)

    prm = np.zeros((P, PRM_N), np.float32)

    def put(name, t):
        prm[:, slice(*PRM[name])] = t.reshape(P, -1)

    put("ident", np.eye(P, dtype=np.float32))
    put("mean", np.full((P, P), 1.0 / D_MODEL, np.float32))
    sel = np.zeros((P, NC_), np.float32)
    sel[np.arange(2 * NC_), np.arange(2 * NC_) % NC_] = 1.0
    put("sel", sel)
    put("bias", np.concatenate([one["b_ada"], v["b_ada_final"]]).reshape(MOD_TILES, P).T)
    put("gain", np.concatenate([one[n] for n in ("norm_ffn1", "norm_mix", "norm_ffn2")] + [v["norm_final"]]).reshape(4 * DT, P).T)
    put("skip", one["s5_d"].reshape(CT, P).T)

    def states(t):
        return np.moveaxis(t.reshape((NT, P) + t.shape[2:]), 0, 1)

    log_dt = np.repeat(one["s5_log_dt"][:, None], 64, 1)
    put("lam", np.stack([states(one["s5_lambda_re"]), states(one["s5_lambda_im"]), states(log_dt)], 1))
    c_all = np.concatenate([v["c_prompt"], v["c_sample"]], 0)
    put("c", c_all.reshape(NC_, DT, P).transpose(2, 1, 0))
    feeds["prm"] = prm

    def block_diagonal(t):
        out = np.zeros((P, NT, 32), np.float32)
        out[:64, :, :16] = t[:64]
        out[64:, :, 16:] = t[64:]
        return out

    feeds["s5_b"] = np.stack([block_diagonal(states(one[n])).reshape(P, -1) for n in ("s5_b_re", "s5_b_im")])
    feeds["s5_c"] = np.ascontiguousarray(np.stack(
        [block_diagonal(states(one[n].transpose(0, 2, 1))) for n in ("s5_c_re", "s5_c_im")], 2)).reshape(P, -1)
    h0 = [np.moveaxis(one[n].reshape(DEC_BATCH, NT, P), (0, 1, 2), (2, 1, 0)) for n in ("state_ssm_re", "state_ssm_im")]
    feeds["h0"] = np.ascontiguousarray(np.stack(h0, 1)).reshape(P, -1)
    feeds["s0"] = np.ascontiguousarray(one["state_ret"].transpose(1, 2, 0, 3)).reshape(HEADS, DK, -1)
    feeds["rope"] = rope_table()
    feeds["head_consts"] = head_constants()

    nc = bacc.Bacc("TRN2", target_bir_lowering=False, num_devices=1)
    aps = {n: nc.dram_tensor(f"in_{n}", t.shape, F32, kind="ExternalInput").ap() for n, t in feeds.items()}
    aps |= {n: nc.dram_tensor(f"out_{n}", s, F32, kind="ExternalOutput").ap() for n, s in _OUTS.items()}
    build(nc, aps)
    r = run_bass_kernel_spmd(nc, [{f"in_{n}": t for n, t in feeds.items()}], core_ids=[0]).results[0]
    out = {n: np.asarray(r[f"out_{n}"]) for n in _OUTS}

    y = out["y"].reshape(DT, P, HALVES, HALF).transpose(2, 3, 0, 1).reshape(HALVES, HALF, D_MODEL)
    y_prompt = np.ascontiguousarray(y[:, :HP]).reshape(1, SEQ, D_MODEL)
    y_sample = np.ascontiguousarray(y[:, HP:]).reshape(DEC_BATCH, DEC_SEQ, D_MODEL)
    sp = out["ssm_prompt"].reshape(P, 2, NT).transpose(1, 2, 0).reshape(2, 1, 1, 32, 64)
    ss = out["ssm_sample"].reshape(P, 2, NT, DEC_BATCH).transpose(1, 3, 2, 0).reshape(2, 1, DEC_BATCH, 32, 64)
    ret_p = out["ret_prompt"].reshape(1, 1, HEADS, DK, DV)
    ret_s = np.ascontiguousarray(out["ret_sample"].reshape(HEADS, DK, DEC_BATCH, DV).transpose(2, 0, 1, 3))[None]
    return (y_prompt, y_sample, np.ascontiguousarray(sp[0]), np.ascontiguousarray(sp[1]), ret_p,
            np.ascontiguousarray(ss[0]), np.ascontiguousarray(ss[1]), ret_s)
```

```python
from contextlib import ExitStack, contextmanager

import numpy as np
import concourse.bass as bass
from concourse import mybir

F32, F32R = mybir.dt.float32, mybir.dt.float32r
ALU, ACT = mybir.AluOpType, mybir.ActivationFunctionType

P = 128
D_MODEL, SEQ, DEC_BATCH, DEC_SEQ, PAST_LEN = 1024, 512, 8, 4, 4096
D_FF = ((8 * D_MODEL // 3 + 255) // 256) * 256
EPS = 1e-6
DT = D_MODEL // P
HALVES = 2
HP, HS = SEQ // 2, DEC_BATCH * DEC_SEQ // 2
HALF = HP + HS
NS = DEC_BATCH * DEC_SEQ
TOK = SEQ + NS
NC_ = 1 + DEC_BATCH
FT = D_FF // P
HT = FT // 2
KMAX = HT
HEADS, DK, DV = 4, P, P
CT, NT, SEG = 4, 16, 128
ADA_BLOCKS, ADA_UNITS, ADA_N = 22, 4, 512
MOD_TILES = ADA_BLOCKS * 4
SH1, SC1, G1, SH2, SC2, G2, SH3, SC3, G3, SHF, SCF = range(0, MOD_TILES, DT)

UP = [(0, HT, DT), (15, HT, DT), (48, HT, DT), (63, HT, DT)]
DOWN = [(11, 4, HT), (26, 4, HT), (59, 4, HT), (74, 4, HT)]
PROJ_U, PROJ_REST, GLU, OUT = (30, 2, DT), (32, 8, DT), (40, 4, 4), (44, 4, DT)
PHASES = [UP[0], DOWN[0], UP[1], DOWN[1], PROJ_U, PROJ_REST, GLU, OUT, UP[2], DOWN[2], UP[3], DOWN[3]]
PAIRS = 78


def k_tiles(pair):
    return next(k for first, n, k in PHASES if first <= pair < first + n)


_two = np.float64(2 * np.pi)
_p0 = 6.28125
_p1 = float(np.float32(np.round((_two - _p0) * 2.0 ** 21) / 2.0 ** 21))
TWO_PI = (_p0, _p1, float(np.float32(_two - _p0 - _p1)))
PI_LOW = 3.1415925

PRM = {}
_at = 0
for _name, _n in (("ident", P), ("mean", P), ("sel", NC_), ("bias", MOD_TILES), ("gain", 4 * DT), ("skip", CT),
                  ("lam", 3 * NT), ("c", DT * NC_)):
    PRM[_name] = (_at, _at + _n)
    _at += _n
PRM_N = _at
HC = {"mask": (0, SEQ), "qmask": (SEQ, SEQ + DEC_BATCH * NS)}
HC_N = SEQ + DEC_BATCH * NS
HS_C = {}
_at = 0
for _name, _n in (("kdec", 5), ("g4", 1), ("smask", NS), ("bmask", DEC_BATCH)):
    HS_C[_name] = (_at, _at + _n)
    _at += _n
HS_N = _at


class Steps:

    def __init__(self, eng, sem):
        self.eng, self.sem, self.base, self.k = eng, sem, 0, 0

    def mark(self, ins):
        ins.then_inc(self.sem, 1)
        self.k += 1

    def wait(self):
        self.eng.wait_ge(self.sem, self.base + self.k)

    def step(self, ins):
        self.mark(ins)
        self.wait()

    @contextmanager
    def loop(self, start, end, per):
        before = self.base + self.k
        with self.eng.Fori(start, end) as i:
            self.base, self.k = (i - start) * per + before, 0
            yield i
            assert self.k == per, (self.k, per)
        self.base, self.k = before + (end - start) * per, 0


def build(nc, a):
    with ExitStack() as ctx:
        def sb(name, shape, dt=F32):
            return ctx.enter_context(nc.sbuf_tensor(name, shape, dt))

        sems = {}

        def sem(name):
            if name not in sems:
                sems[name] = ctx.enter_context(nc.semaphore(name))
            return sems[name]

        x = sb("x", [P, DT, HALVES, HALF])
        h_hi = sb("h_hi", [P, DT, HALVES, HALF], F32R)
        h_lo = sb("h_lo", [P, DT, HALVES, HALF], F32R)
        w_raw = [sb(f"w_raw{s}", [P, KMAX, P]) for s in range(2)]
        w_hi = [sb(f"w_hi{s}", [P, KMAX, P], F32R) for s in range(2)]
        w_lo = [sb(f"w_lo{s}", [P, KMAX, P], F32R) for s in range(2)]
        mod = sb("mod", [P, MOD_TILES, NC_])
        prm = sb("prm", [P, PRM_N])
        c_split = sb("c_split", [P, DT, 2 * NC_], F32R)
        lb = sb("lb", [P, CT, 2, P])
        lc = sb("lc", [P, NT, 2, 32])
        sumsq, root = (sb(n, [P, HALVES, HALF]) for n in ("sumsq", "root"))
        rms = sb("rms", [P, 6])
        hs32 = root[:].rearrange("p h n -> p (h n)")[:, 0:DT * NS].rearrange("p (t h n) -> p t h n", t=DT, h=HALVES)
        gs = [sb(f"gs{s}", [P, HALVES, HS]) for s in range(2)]
        tmp = [sb(f"tmp{s}", [P, HALVES, HALF]) for s in range(2)]
        h32 = [sb(f"h32_{s}", [P, HALVES, HALF]) for s in range(2)]
        s5r, s5lam, s5beta, s5pow = sb("s5r", [P, NT]), sb("s5lam", [P, 2, NT]), sb("s5beta", [P, 2, NT]), sb("s5pow", [P, 2, 8, NT])
        s5t = sb("s5t", [P, 8, NT])
        stat = sb("stat", [P, 5, 6])
        mv = sb("mv", [P, 5, 2])
        hrstd = sb("hrstd", [P, 5, 1])
        eps_t = sb("eps_t", [P, 1])
        epsm = sb("epsm", [P, 5, 2])
        x_last = sb("x_last", [P, 2, NT])
        carry = sb("carry", [P, 2, 4])
        ct4 = sb("ct4", [P, 4, 4])

        g = nc.sbuf_tensor("hid_hi", [P, HT, HALVES, HALF], F32R)
        hid_hi = g.__enter__()
        g2 = nc.sbuf_tensor("hid_lo", [P, HT, HALVES, HALF], F32R)
        hid_lo = g2.__enter__()
        glu_hi, glu_lo = hid_hi[:, 4:4 + CT], hid_lo[:, 0:CT]
        g2.__exit__(None, None, None)
        g.__exit__(None, None, None)
        proj = sb("proj", [P, 20, TOK])
        bus = sb("bus", [P, 2, NT, NS])

        norm_tmp, norm_out = (proj[:, n:n + DT].rearrange("p t (h c) -> p t h c", h=HALVES) for n in (DT, 0))

        sb("hid_rest", [P, 2 * HT * TOK - 20 * TOK - 2 * NT * NS])

        with ExitStack() as e_life:
            et = e_life.enter_context(nc.sbuf_tensor("et", [P, 2, NT, SEG], F32))
        with ExitStack() as late:
            def lsb(name, shape):
                return late.enter_context(nc.sbuf_tensor(name, shape, F32))
            xs = lsb("xs", [P, 2, NT, DEC_BATCH, DEC_SEQ])
            vm = lsb("vm", [P, DEC_BATCH, DV])
            hsm = lsb("hsm", [P, HEADS, HS_N])
            h0 = lsb("h0", [P, 2, NT, DEC_BATCH])
        sb("et_region", [P, 2 * NT * SEG])

        with ExitStack() as life:
            ada_raw = [life.enter_context(nc.sbuf_tensor(f"ada_raw{u}", [P, 2, ADA_N], F32)) for u in range(ADA_UNITS)]
            ada_hi = [life.enter_context(nc.sbuf_tensor(f"ada_hi{u}", [P, 2, ADA_N], F32R)) for u in range(2)]
            ada_lo = [life.enter_context(nc.sbuf_tensor(f"ada_lo{u}", [P, 2, ADA_N], F32R)) for u in range(2)]
        with ExitStack() as life:
            def rsb(name, shape):
                return life.enter_context(nc.sbuf_tensor(name, shape, F32))
            bu = [rsb(f"bu{s}", [P, 2, 4, SEG]) for s in range(2)]
            z = [rsb(f"z{s}", [P, 2, 4, SEG]) for s in range(2)]
            xc = [rsb(f"xc{s}", [P, 2, 4, SEG]) for s in range(2)]
            lbs = rsb("lbs", [P, 2, 4, P])
            lcs = rsb("lcs", [P, 4, 2, 32])
            swap = rsb("swap", [P, TOK])
        with ExitStack() as life:
            def rsb(name, shape):
                return life.enter_context(nc.sbuf_tensor(name, shape, F32))
            ks = rsb("ks", [P, TOK])
            vt, kt = rsb("vt", [P, 5, DV]), rsb("kt", [P, 5, DK])
            sc = rsb("sc", [P, 10 * P])
            scs = rsb("scs", [NS, NS])
            hc = rsb("hc", [P, HC_N])
            s0, sn = rsb("s0", [P, DEC_BATCH, DV]), rsb("sn", [P, DEC_BATCH, DV])
            qm = rsb("qm", [P, DEC_BATCH, NS])
            on = rsb("on", [P, 5, DV])
            sp_out = rsb("sp_out", [P, DV])
            xs_last = rsb("xs_last", [P, 2, NT, DEC_BATCH])
        sb("ada_region", [P, 2 * ADA_UNITS * 2 * ADA_N])
        ada_row = h32[1][0:2 * NC_].rearrange("p h n -> p (h n)")[:, 0:ADA_N]
        rope = [t[:].rearrange("p h n -> p (h n)") for t in (sumsq, root)]
        vs = rope[0]

        acc = [ctx.enter_context(nc.psum_tensor(f"acc{s}", [P, 2, 512], F32)) for s in range(2)]
        pn = ctx.enter_context(nc.psum_tensor("pn", [P, 2, 512], F32))
        pa = ctx.enter_context(nc.psum_tensor("pa", [P, 512], F32))
        pt = ctx.enter_context(nc.psum_tensor("pt", [P, 512], F32))

        def prmv(name):
            return prm[:, PRM[name][0]:PRM[name][1]]

        def hcv(name):
            return hc[:, HC[name][0]:HC[name][1]]

        def hsv(h, name):
            return hsm[:, h, HS_C[name][0]:HS_C[name][1]]

        def prompt(t):
            return t[:, :, 0:HP]

        def sample(t):
            return t[:, :, HP:HALF]

        def sample4(t):
            return sample(t).rearrange("p h (b s) -> p h b s", s=DEC_SEQ)

        def per_seq(t):
            return t.rearrange("p (h b) -> p h b", h=2).unsqueeze(3).broadcast_to([P, 2, 4, DEC_SEQ])

        def flat(t):
            return t[:].rearrange("p h n -> p (h n)")

        def view4(t):
            return flat(t)[:, 0:4 * SEG].rearrange("p (t n) -> p t n", t=4)

        def view(t, n):
            return flat(t)[:, 0:n]

        def scores_at(t):
            return (acc[0][:, 0, 0:SEQ], acc[0][:, 1, 0:3 * P], acc[1][:, 0, 0:2 * P], acc[0][:, 1, 3 * P:4 * P])[t]

        raw_in = [sem(f"raw_in{s}") for s in range(2)]
        hi_ready = [sem(f"hi_ready{s}") for s in range(2)]
        lo_ready = [sem(f"lo_ready{s}") for s in range(2)]
        acc_ready = [sem(f"acc_ready{s}") for s in range(2)]
        acc_free = [sem(f"acc_free{s}") for s in range(2)]
        ada_in = [sem(f"ada_in{u}") for u in range(ADA_UNITS)]
        ada_hi_ready, ada_lo_ready, ada_used = sem("ada_hi_ready"), sem("ada_lo_ready"), sem("ada_used")
        ada_row_ready, ada_turned, mod_ready = sem("ada_row_ready"), sem("ada_turned"), sem("mod_ready")
        prm_in, x_in, b_in, c_in = sem("prm_in"), sem("x_in"), sem("b_in"), sem("c_in")
        rope_in, h0_in, hc_in, s0_in, hsm_in = sem("rope_in"), sem("h0_in"), sem("hc_in"), sem("s0_in"), sem("hsm_in")
        silu_c, c_hi_ready, c_ready = sem("silu_c"), sem("c_hi_ready"), sem("c_ready")
        sumsq_ready, ms_ready, root_ready = sem("sumsq_ready"), sem("ms_ready"), sem("root_ready")
        diag_ready, rstd_ready = sem("diag_ready"), sem("rstd_ready")
        tile_ready = [sem("tile_even"), sem("tile_odd")]
        h_hi_ready = [sem("h_hi_even"), sem("h_hi_odd")]
        h_lo_ready = [sem("h_lo_even"), sem("h_lo_odd")]
        hs_ready, hs_hi_ready, hs_lo_ready, scaled = sem("hs_ready"), sem("hs_hi_ready"), sem("hs_lo_ready"), sem("scaled")
        hid_hi_ready, hid_lo_ready = sem("hid_hi_ready"), sem("hid_lo_ready")
        y_even, y_odd = sem("y_even"), sem("y_odd")
        stored = sem("stored")
        act_step, dve_step, pool_step = sem("act_step"), sem("dve_step"), sem("pool_step")
        s5_angle, s5_exp, s5_trig, bbar_ready, bbar_turned, lb_ready = (sem(n) for n in (
            "s5_angle", "s5_exp", "s5_trig", "bbar_ready", "bbar_turned", "lb_ready"))

        staged, b_done, bs_done = sem("staged"), sem("b_done"), sem("bs_done")
        bu_ready, bus_ready, y_used = sem("bu_ready"), sem("bus_ready"), sem("y_used")
        bu_used, xi_ready, y_ready = sem("bu_used"), sem("xi_ready"), sem("y_ready")
        z_ready, xr_ready, x_last_ready, lbs_clear = (sem(n) for n in ("z_ready", "xr_ready", "x_last_ready", "lbs_clear"))
        xs_ready, xs_last_ready, ys_ready, y_all = (sem(n) for n in ("xs_ready", "xs_last_ready", "ys_ready", "y_all"))
        gelu_ready, g_hi_ready, g_lo_ready, m_hi_ready, m_lo_ready = (sem(n) for n in (
            "gelu_ready", "g_hi_ready", "g_lo_ready", "m_hi_ready", "m_lo_ready"))
        lcs_staged, krot_ready, qrot_ready, qsw_ready, ksw_ready = (sem(n) for n in (
            "lcs_staged", "krot_ready", "qrot_ready", "qsw_ready", "ksw_ready"))
        m32_ready, r_lo_ready = sem("m32_ready"), sem("r_lo_ready")
        tv_ready, snp_ready, o_ready, ks_ready, r_hi_ready = (sem(n) for n in (
            "tv_ready", "snp_ready", "o_ready", "ks_ready", "r_hi_ready"))
        vs_ready, vt_ready, vm_ready = (sem(n) for n in ("vs_ready", "vt_ready", "vm_ready"))
        mv_ready, hrstd_ready, on_ready, kt_ready, qm_ready, scm_ready = (sem(n) for n in (
            "mv_ready", "hrstd_ready", "on_ready", "kt_ready", "qm_ready", "scm_ready"))
        tk_ready, scores_ready, spp_ready, sp_ready, sn_ready, ot_ready, head_stored = (sem(n) for n in (
            "tk_ready", "scores_ready", "spp_ready", "sp_ready", "sn_ready", "ot_ready", "head_stored"))
        eps_ready, table_done, pool_settled, dve_settled = (sem(n) for n in (
            "eps_ready", "table_done", "pool_settled", "dve_settled"))

        block = ctx.enter_context(nc.Block())

        @block.sync
        def _(sp):
            sp.dma_start(prm[:], a["prm"]).then_inc(prm_in, 16)

            def source(phase):
                first, n, k = phase
                name = ("up" if phase in UP else "down" if phase in DOWN else
                        {PROJ_U: "w_in", PROJ_REST: "w_in", GLU: "w_glu", OUT: "w_out"}[phase])
                if name in ("up", "down"):
                    j = (UP if name == "up" else DOWN).index(phase)
                    return a[f"ffn{1 + j // 2}_{name}"], (j % 2) * n
                return a[name], 2 if phase == PROJ_REST else 0

            def load_unit(phase, i, s, first_use=False):
                src, off = source(phase)
                k = phase[2]
                if not first_use:
                    sp.wait_ge(lo_ready[s], phase[0] + i)
                sp.dma_start(w_raw[s][:, 0:k, :],
                             src[i + off, s].rearrange("p (k m) -> p k m", k=k)).then_inc(raw_in[s], 16)

            def load_ada(b, u, first_use=False):
                if not first_use:
                    sp.wait_ge(ada_lo_ready, (b - 1) * 4 + u + 1)
                sp.dma_start(ada_raw[u][:], a["ada"][b, u].rearrange("p (k n) -> p k n", k=2)).then_inc(ada_in[u], 16)

            for u in range(ADA_UNITS):
                load_ada(0, u, first_use=True)
            sp.dma_start(x[:], a["x"].rearrange("p (t h n) -> p t h n", t=DT, h=2)).then_inc(x_in, 16)
            with sp.Fori(1, 4) as b:
                for u in range(ADA_UNITS):
                    load_ada(b, u)
            load_unit(UP[0], 0, 0, first_use=True)
            load_unit(UP[0], 0, 1, first_use=True)
            sp.dma_start(lc[:], a["s5_c"].rearrange("p (t r c) -> p t r c", t=NT, r=2)).then_inc(c_in, 16)

            def load_up(phase, block0, done=0):
                n_ada = 9 if block0 else 0
                if n_ada:
                    if done == 0:
                        load_unit(phase, 0, 0)
                    for u in range(ADA_UNITS):
                        load_ada(block0, u)
                    if done == 0:
                        load_unit(phase, 0, 1)
                    with sp.Fori(1, n_ada) as f:
                        load_unit(phase, f, 0)
                        for u in range(ADA_UNITS):
                            load_ada(f + block0, u)
                        load_unit(phase, f, 1)
                with sp.Fori(n_ada, HT) as f:
                    load_unit(phase, f, 0)
                    load_unit(phase, f, 1)

            def load_plain(phase):
                with sp.Fori(0, phase[1]) as i:
                    load_unit(phase, i, 0)
                    load_unit(phase, i, 1)

            load_up(UP[0], 4, done=1)
            load_unit(DOWN[0], 0, 0)
            load_unit(DOWN[0], 0, 1)
            sp.wait_ge(acc_free[1], DOWN[0][0])
            for r in range(2):
                sp.dma_start(flat(tmp[r])[:, 0:NT * 32], a["s5_b"][r]).then_inc(b_in, 16)
            with sp.Fori(1, 4) as i:
                load_unit(DOWN[0], i, 0)
                load_unit(DOWN[0], i, 1)
            load_up(UP[1], 13)
            load_plain(DOWN[1])
            load_plain(PROJ_U)
            sp.wait_ge(rstd_ready, 2)
            sp.wait_ge(hs_lo_ready, 2)
            for r in range(2):
                sp.dma_start(rope[r], a["rope"][r]).then_inc(rope_in, 16)
            load_plain(PROJ_REST)
            load_unit(GLU, 0, 0)
            load_unit(GLU, 0, 1)
            sp.wait_ge(y_used, 16 + 1)
            sp.wait_ge(xi_ready, 16 + 2)
            sp.dma_start(h0[:], a["h0"].rearrange("p (r t b) -> p r t b", r=2, t=NT)).then_inc(h0_in, 16)
            sp.dma_start(hsm[:], a["head_small"].rearrange("p (h n) -> p h n", h=HEADS)).then_inc(hsm_in, 16)
            sp.wait_ge(x_last_ready, 2 * CT)
            sp.dma_start(a["ssm_prompt"], x_last[:].rearrange("p r t -> p (r t)")).then_inc(stored, 16)
            sp.dma_start(hc[:], a["head_consts"][0]).then_inc(hc_in, 16)
            sp.dma_start(s0[:], a["s0"][0].rearrange("p (b v) -> p b v", b=DEC_BATCH)).then_inc(s0_in, 16)
            sp.wait_ge(xs_last_ready, 1)
            sp.dma_start(a["ssm_sample"], xs_last[:].rearrange("p r t b -> p (r t b)")).then_inc(stored, 16)

            def load_masks(h):
                sp.wait_ge(scm_ready, h)
                sp.dma_start(hc[:], a["head_consts"][h]).then_inc(hc_in, 16)

            def store_head(h):
                sp.wait_ge(sp_ready, h + 1)
                sp.dma_start(a["ret_prompt"][h], sp_out[:]).then_inc(head_stored, 16)
                sp.dma_start(a["ret_sample"][h], sn[:].rearrange("p b v -> p (b v)")).then_inc(head_stored, 16)
            with sp.Fori(0, HEADS - 1) as h:
                load_masks(h + 1)
                sp.wait_ge(sn_ready, h + 1)
                sp.dma_start(s0[:], a["s0"][h + 1].rearrange("p (b v) -> p b v", b=DEC_BATCH)).then_inc(s0_in, 16)
                store_head(h)
            sp.wait_ge(sn_ready, HEADS)
            store_head(HEADS - 1)
            with sp.Fori(1, 4) as i:
                load_unit(GLU, i, 0)
                load_unit(GLU, i, 1)
            load_plain(OUT)
            for phase in (UP[2], UP[3]):
                load_up(phase, 0)
                load_plain(DOWN[UP.index(phase)])
            with sp.Fori(0, DT // 2) as i:
                sp.wait_ge(y_even, i + 1)
                sp.dma_start(a["y"][2 * i].rearrange("p (h n) -> p h n", h=2), x[:, 2 * i]).then_inc(stored, 16)
                sp.wait_ge(y_odd, i + 1)
                sp.dma_start(a["y"][2 * i + 1].rearrange("p (h n) -> p h n", h=2), x[:, 2 * i + 1]).then_inc(stored, 16)
            sp.wait_ge(stored, 16 * (2 + DT))
            sp.wait_ge(head_stored, 16 * 2 * HEADS + 16)

        @block.gpsimd
        def _(pool):
            st = Steps(pool, pool_step)

            def tt(out, in0, in1, op, moving=False):
                if moving:
                    pool.sem_inc(pool_settled, 1)
                return pool.tensor_tensor(out, in0, in1, op)

            def split_lo(pair, s, k):
                pool.wait_ge(hi_ready[s], pair + 1)
                tt(w_lo[s][:, 0:k], w_raw[s][:, 0:k], w_hi[s][:, 0:k].bitcast(F32), ALU.subtract).then_inc(lo_ready[s], 1)

            def split_pairs(phase, start=0):
                first, n, k = phase
                with pool.Fori(start, n) as i:
                    split_lo(i + first, 0, k)
                    split_lo(i + first, 1, k)

            def norm_lo(j):
                pool.wait_ge(hs_hi_ready, j + 1)
                tt(h_lo[:, :, :, HP:HALF], hs32, h_hi[:, :, :, HP:HALF].bitcast(F32), ALU.subtract).then_inc(hs_lo_ready, 1)
                for i in range(DT // 2):
                    pool.wait_ge(h_hi_ready[0], DT // 2 * j + i + 1)
                    tt(prompt(h_lo[:, 2 * i]), prompt(norm_out[:, 2 * i]), prompt(h_hi[:, 2 * i]).bitcast(F32), ALU.subtract)\
                        .then_inc(h_lo_ready[0], 1)

            def normed_phase(j, phase):
                split_lo(phase[0], 0, phase[2])
                split_lo(phase[0], 1, phase[2])
                norm_lo(j)
                split_pairs(phase, 1)

            pool.wait_ge(x_in, 16)
            st.step(pool.memset(sumsq[:], 0.0))
            with st.loop(0, DT, 2) as m:
                st.step(tt(root[:], x[:, m], x[:, m], ALU.mult, moving=True))
                st.step(tt(sumsq[:], sumsq[:], root[:], ALU.add))
            pool.sem_inc(sumsq_ready, 1)
            normed_phase(0, UP[0])
            split_pairs(DOWN[0])
            split_pairs(UP[1])
            split_pairs(DOWN[1])
            normed_phase(1, PROJ_U)

            pool.sem_inc(xi_ready, 2)

            def segment(ct, j):
                gi, b = 4 * ct + j, j % 2
                er, ei = et[:, 0, bass.ds(4 * ct, 4), :], et[:, 1, bass.ds(4 * ct, 4), :]
                pa_, pb_ = view4(h32[0]), view4(h32[1])
                pool.wait_ge(z_ready, gi + 1)
                pool.wait_ge(y_ready, gi + 1)
                pool.wait_ge(xi_ready, gi + 2)
                st.mark(tt(pa_, z[b][:, 0], ei, ALU.mult, moving=True))
                st.step(tt(pb_, z[b][:, 1], er, ALU.mult))
                tt(xc[b][:, 1], pa_, pb_, ALU.add).then_inc(xi_ready, 1)

            def channel_tile(ct, k_next):
                qa = 2 * ct + PROJ_REST[0]
                split_lo(qa, 1, DT)
                segment(ct, 0)
                split_lo(qa + 1, 0, DT)
                pool.wait_ge(qsw_ready, ct + 1)
                q_tile = proj[:, 4 * ct + 4]
                st.mark(tt(q_tile, q_tile, rope[0], ALU.mult, moving=True))
                st.step(tt(swap[:], swap[:], rope[1], ALU.mult))
                tt(q_tile, q_tile, swap[:], ALU.add, moving=True).then_inc(qrot_ready, 1)
                segment(ct, 1)
                split_lo(qa + 1, 1, DT)
                segment(ct, 2)
                split_lo(qa + 2, 0, k_next)
                segment(ct, 3)
                pool.wait_ge(xi_ready, 4 * ct + 4 + 2)
                pool.tensor_copy(x_last[:, 1, bass.ds(4 * ct, 4)], xc[1][:, 1, :, SEG - 1]).then_inc(x_last_ready, 1)

            split_lo(PROJ_REST[0], 0, DT)
            pool.wait_ge(rope_in, 32)
            with st.loop(0, CT - 1, 10) as ct:
                channel_tile(ct, DT)
            channel_tile(CT - 1, GLU[2])

            split_lo(GLU[0], 1, GLU[2])

            pool.sem_inc(r_lo_ready, 1)
            st.step(pool.memset(epsm[:, :, 0:1], EPS))
            st.step(pool.memset(epsm[:, :, 1:2], -0.5))
            pool.wait_ge(hsm_in, 16)

            def spread_v(h):
                pool.wait_ge(kt_ready, h + 1)
                if not (isinstance(h, int) and h == 0):
                    pool.wait_ge(snp_ready, h)
                tt(vm[0:NS], vt[0:NS, 4, :].unsqueeze(1).broadcast_to([NS, DEC_BATCH, DV]),
                   hsv(h, "bmask")[0:NS].unsqueeze(2).broadcast_to([NS, DEC_BATCH, DV]), ALU.mult, moving=True).then_inc(vm_ready, 1)

            def head(h, last=False):
                pool.wait_ge(mv_ready, h + 1)
                st.step(tt(hrstd[:], mv[:, :, 1:2], epsm[:, :, 0:1], ALU.add))
                tt(hrstd[:], hrstd[:], epsm[:, :, 1:2], ALU.pow).then_inc(hrstd_ready, 1)
                if not last:
                    spread_v(h + 1)
                pool.wait_ge(r_hi_ready, h + 1)
                tt(h_lo[:, h + 4], tmp[1][:], h_hi[:, h + 4].bitcast(F32), ALU.subtract, moving=True).then_inc(r_lo_ready, 1)
                pool.wait_ge(g_hi_ready, h + 1)
                for n, part in ((HP, prompt), (HS, sample)):
                    at = 0 if part is prompt else SEQ
                    ins = tt(part(h_lo[:, h]), proj[:, h, at:at + 2 * n].rearrange("p (h n) -> p h n", h=2),
                             part(h_hi[:, h]).bitcast(F32), ALU.subtract, moving=True)
                ins.then_inc(g_lo_ready, 1)
            spread_v(0)
            with st.loop(0, HEADS - 1, 1) as h:
                head(h)
            head(HEADS - 1, last=True)
            split_pairs(GLU, 1)
            split_pairs(OUT)
            normed_phase(2, UP[2])
            split_pairs(DOWN[2])
            split_pairs(UP[3])
            split_pairs(DOWN[3])

        @block.scalar
        def _(act):
            st = Steps(act, act_step)

            def copy(out, in_, scale=1.0):
                return nc.scalar.activation(out, in_, ACT.Copy, scale=scale)

            def split_hi(pair, s, k, first_use=False):
                act.wait_ge(raw_in[s], 16 * pair + 16)
                if not first_use:
                    act.wait_ge(acc_ready[s], pair)
                copy(w_hi[s][:, 0:k], w_raw[s][:, 0:k]).then_inc(hi_ready[s], 1)

            def ada_split(b, u):
                act.wait_ge(ada_in[u], 16 * b + 16)
                if not (isinstance(b, int) and b == 0 and u < 2):
                    act.wait_ge(ada_used, 4 * b + (u - 1))
                copy(ada_hi[u % 2][:], ada_raw[u][:]).then_inc(ada_hi_ready, 1)

            def ada_read(b):
                act.wait_ge(ada_used, 4 * b + 4)
                if not (isinstance(b, int) and b == 0):
                    act.wait_ge(ada_turned, b)
                copy(ada_row, pa[0:2 * NC_, :]).then_inc(ada_row_ready, 1)

            act.wait_ge(prm_in, 16)
            act_c = h32[0][:, 0, 0:DT * NC_]
            nc.scalar.activation(act_c, prmv("c"), ACT.Silu).then_inc(silu_c, 1)
            act.wait_ge(silu_c, 1)
            copy(c_split[:, :, 0:NC_], act_c.rearrange("p (t n) -> p t n", n=NC_)).then_inc(c_hi_ready, 1)
            for u in range(2):
                ada_split(0, u)
            lam = prmv("lam").rearrange("p (a t) -> p a t", a=3)
            nc.scalar.activation(s5t[:, 0], lam[:, 2], ACT.Exp).then_inc(s5_exp, 1)
            for u in range(2, 4):
                ada_split(0, u)
            ada_read(0)
            act.wait_ge(s5_angle, 1)
            nc.scalar.activation(s5r[:], s5t[:, 1], ACT.Exp)
            nc.scalar.activation(s5pow[:, 1, 0], s5t[:, 2], ACT.Sin)
            nc.scalar.activation(s5pow[:, 0, 0], s5t[:, 3], ACT.Sin).then_inc(s5_trig, 1)
            with act.Fori(1, 4) as b:
                for u in range(4):
                    ada_split(b, u)
                ada_read(b)
            split_hi(UP[0][0], 0, DT, first_use=True)

            def norm_root(j):
                if j == 0:
                    nc.scalar.activation(hrstd[:, 0], eps_t[:], ACT.Sqrt)
                act.wait_ge(ms_ready, j + 1)
                nc.scalar.activation(rms[:, 0:4], pn[:, 0, HALF:HALF + 4], ACT.Sqrt, bias=eps_t[:])
                nc.scalar.activation(rms[0:HS, 4:6], pn[0:HS, 0, HALF + 4:HALF + 6], ACT.Sqrt, bias=eps_t[0:HS]).then_inc(root_ready, 1)

            def odd_tile(m, out, in_):
                return nc.scalar.activation(prompt(out), prompt(in_), ACT.Identity, bias=mod[:, m[1], 0:1], scale=mod[:, m[0], 0:1])

            def norm_hi(j, sc, sh):
                for i in range(DT // 2):
                    done = DT // 2 * j + i + 1
                    even, odd = 2 * i, 2 * i + 1
                    act.wait_ge(scaled, done)
                    odd_tile((odd + sc, odd + sh), norm_out[:, odd], norm_tmp[:, odd]).then_inc(tile_ready[1], 1)
                    act.wait_ge(tile_ready[0], done)
                    copy(prompt(h_hi[:, even]), prompt(norm_out[:, even])).then_inc(h_hi_ready[0], 1)
                    if i == 0:
                        act.wait_ge(hs_ready, j + 1)
                        copy(h_hi[:, :, :, HP:HALF], hs32).then_inc(hs_hi_ready, 1)
                    act.wait_ge(tile_ready[1], done)
                    copy(prompt(h_hi[:, odd]), prompt(norm_out[:, odd])).then_inc(h_hi_ready[1], 1)

            def up(phase, block0, normed=False):
                first = phase[0]

                def hidden(f, ada, first_use=False, k_next=DT, split=False):
                    pair = f + first
                    b = f + block0
                    if not split:
                        split_hi(pair, 1, DT)
                    if ada:
                        ada_split(b, 0)
                        ada_split(b, 1)
                    act.wait_ge(acc_ready[0], pair + 1)
                    if not first_use:
                        act.wait_ge(acc_free[1], pair)
                    nc.scalar.activation(tmp[0][:], acc[0][:, :, 0:HALF], ACT.Silu).then_inc(acc_free[0], 1)
                    split_hi(pair + 1, 0, k_next)
                    if ada:
                        ada_split(b, 2)
                        ada_split(b, 3)
                    act.wait_ge(acc_free[1], pair + 1)
                    copy(hid_hi[:, f], h32[0][:]).then_inc(hid_hi_ready, 1)
                    if ada:
                        ada_read(b)

                n_ada = 9 if block0 else 1
                hidden(0, bool(block0), first_use=(first == 0), split=normed)
                if block0:
                    with act.Fori(1, n_ada) as f:
                        hidden(f, True)
                with act.Fori(n_ada, HT - 1) as f:
                    hidden(f, False)
                hidden(HT - 1, False, k_next=KMAX)

            def splits(phase, start=0):
                first, n, k = phase
                with act.Fori(start, n - 1) as i:
                    split_hi(i + first, 1, k)
                    split_hi(i + (first + 1), 0, k)
                split_hi(first + n - 1, 1, k)
                if first + n < PAIRS:
                    split_hi(first + n, 0, k_tiles(first + n))

            split_hi(UP[0][0], 1, DT, first_use=True)
            act.wait_ge(eps_ready, 1)
            norm_root(0)
            norm_hi(0, SC1, SH1)
            up(UP[0], 4, normed=True)
            act.wait_ge(c_in, 16)
            st.step(nc.scalar.activation(lc[:, :, 1, :], lc[:, :, 1, :], ACT.Copy, scale=-1.0))
            splits(DOWN[0])
            act.wait_ge(bbar_turned, 1)
            copy(lb[:], pn[:].rearrange("p r (t n) -> p t r n", t=CT)).then_inc(lb_ready, 1)
            act.wait_ge(table_done, 1)
            up(UP[1], 13)
            splits(DOWN[1])
            split_hi(PROJ_U[0], 1, DT)
            norm_root(1)
            norm_hi(1, SC2, SH2)

            def mixer_order(t):
                return (t[:, 0:SEQ].rearrange("p (h n) -> p h n", h=2), t[:, SEQ:TOK].rearrange("p (h n) -> p h n", h=2))

            def read_proj(pair, s, m, func=ACT.Copy):
                act.wait_ge(acc_ready[s], pair + 1)
                out_p, out_s = mixer_order(proj[:, m])
                nc.scalar.activation(out_p, prompt(acc[s]), func)
                return nc.scalar.activation(out_s, sample(acc[s]), func)

            def read_swapped(s):
                lower, upper = slice(0, P // 2), slice(P // 2, P)
                for to, from_ in ((lower, upper), (upper, lower)):
                    out_p, out_s = mixer_order(swap[to])
                    copy(out_p, prompt(acc[s][from_]))
                    ins = copy(out_s, sample(acc[s][from_]))
                return ins

            for i in range(PROJ_U[1]):
                pair = PROJ_U[0] + i
                if i:
                    split_hi(pair, 1, DT)
                read_proj(pair, 0, 2 * i).then_inc(acc_free[0], 1)
                split_hi(pair + 1, 0, DT)
                read_proj(pair, 1, 2 * i + 1).then_inc(acc_free[1], 1)

            act.sem_inc(bu_ready, 1)
            act.sem_inc(bus_ready, 1)
            act.wait_ge(lbs_clear, 1)
            for s in range(2):
                act.wait_ge(acc_free[s], PROJ_REST[0])
            act.wait_ge(lb_ready, 1)

            def stage(ct):
                for i in range(4):
                    r = slice(32 * i, 32 * i + 32)
                    ins = copy(lbs[r, :, i, :], lb[r, ct])
                ins.then_inc(staged, 1)

            def channel_tile(ct, k_next, first=False, last=False):
                qa = 2 * ct + PROJ_REST[0]

                def read_bu(j):
                    gi = 4 * ct + j
                    act.wait_ge(b_done, gi + 1)
                    act.wait_ge(bu_used, gi + 1)
                    copy(bu[j % 2][:], pn[:].rearrange("p r (t n) -> p r t n", t=4)).then_inc(bu_ready, 1)

                read_bu(0)
                split_hi(qa, 1, DT)
                act.wait_ge(bs_done, ct + 1)
                copy(bus[:, :, bass.ds(4 * ct, 4), :],
                     pt[:, 0:2 * 4 * NS].rearrange("p (r t n) -> p r t n", r=2, t=4)).then_inc(bus_ready, 1)
                read_proj(qa, 0, 4 * ct + 4)
                if not first:
                    act.wait_ge(krot_ready, ct)
                read_swapped(0).then_inc(qsw_ready, 1)
                act.wait_ge(qsw_ready, ct + 1)
                act.sem_inc(acc_free[0], 1)
                split_hi(qa + 1, 0, DT)
                read_bu(1)
                if not first:
                    act.wait_ge(y_ready, 4 * ct + 2)
                copy(lcs[:], lc[:, bass.ds(4 * ct, 4)]).then_inc(lcs_staged, 1)
                read_proj(qa, 1, 4 * ct + 5)
                act.wait_ge(qrot_ready, ct + 1)
                read_swapped(1).then_inc(ksw_ready, 1)
                act.wait_ge(ksw_ready, ct + 1)
                act.sem_inc(acc_free[1], 1)
                split_hi(qa + 1, 1, DT)
                read_bu(2)
                read_proj(qa + 1, 0, 4 * ct + 6).then_inc(acc_free[0], 1)
                split_hi(qa + 2, 0, k_next)
                read_bu(3)
                if not last:
                    stage(ct + 1)
                read_proj(qa + 1, 1, 4 * ct + 7, ACT.Silu).then_inc(acc_free[1], 1)

            stage(0)
            channel_tile(0, DT, first=True)
            with act.Fori(1, CT - 1) as ct:
                channel_tile(ct, DT)
            channel_tile(CT - 1, GLU[2], last=True)
            split_hi(GLU[0], 1, GLU[2])

            act.wait_ge(krot_ready, CT)
            act.wait_ge(qrot_ready, CT)
            for s in range(2):
                act.wait_ge(acc_free[s], GLU[0])

            def copy_vk(h):
                if not (isinstance(h, int) and h == 0):
                    act.wait_ge(scores_ready, h)
                copy(vs, proj[:, 4 * h + 6]).then_inc(vs_ready, 1)
                copy(ks[:], proj[:, 4 * h + 5]).then_inc(ks_ready, 1)

            def read_vt(h):
                act.wait_ge(tv_ready, h + 1)
                copy(vt[:, 0:4], acc[1][:, 1].rearrange("p (t n) -> p t n", t=4)).then_inc(vt_ready, 1)

            def head(h, vt_next=True, vk_next=True):
                if vt_next:
                    read_vt(h + 1)
                if vk_next:
                    copy_vk(h + 2)
                act.wait_ge(m32_ready, h + 2)
                copy(h_hi[:, h + 4], tmp[1][:]).then_inc(r_hi_ready, 1)
                act.wait_ge(y_all, 1)
                nc.scalar.activation(proj[:, h], proj[:, h], ACT.Gelu_apprx_tanh).then_inc(gelu_ready, 1)
                act.wait_ge(gelu_ready, h + 1)
                in_p, in_s = mixer_order(proj[:, h])
                copy(prompt(h_hi[:, h]), in_p)
                copy(sample(h_hi[:, h]), in_s).then_inc(g_hi_ready, 1)

            copy_vk(0)
            read_vt(0)
            copy_vk(1)
            with act.Fori(0, HEADS - 2) as h:
                head(h)
            head(HEADS - 2, vk_next=False)
            head(HEADS - 1, vt_next=False, vk_next=False)

            def glu_tile(i, k_next):
                pair = i + GLU[0]
                if not (isinstance(i, int) and i == 0):
                    split_hi(pair, 1, GLU[2])
                act.wait_ge(acc_ready[1], pair + 1)
                act.wait_ge(acc_free[0], pair)
                nc.scalar.activation(tmp[0][:], acc[1][:, :, 0:HALF], ACT.Sigmoid).then_inc(acc_free[1], 1)
                split_hi(pair + 1, 0, k_next)
                act.wait_ge(acc_free[0], pair + 1)
                copy(glu_hi[:, i], h32[0][:]).then_inc(m_hi_ready, 1)

            glu_tile(0, GLU[2])
            with act.Fori(1, GLU[1] - 1) as i:
                glu_tile(i, GLU[2])
            glu_tile(GLU[1] - 1, OUT[2])
            split_hi(OUT[0], 1, OUT[2])
            with act.Fori(1, OUT[1]) as i:
                split_hi(i + OUT[0], 0, DT)
                split_hi(i + OUT[0], 1, DT)
            split_hi(UP[2][0], 0, DT)
            split_hi(UP[2][0], 1, DT)
            norm_root(2)
            norm_hi(2, SC3, SH3)
            up(UP[2], 0, normed=True)
            splits(DOWN[2])
            up(UP[3], 0)
            splits(DOWN[3])
            norm_root(3)
            for i in range(DT // 2):
                odd = 2 * i + 1
                act.wait_ge(scaled, DT // 2 * 3 + i + 1)
                odd_tile((odd + SCF, odd + SHF), x[:, odd], norm_tmp[:, odd]).then_inc(y_odd, 1)

        @block.vector
        def _(dve):
            st = Steps(dve, dve_step)
            v = nc.vector
            tt = v.tensor_tensor

            def ada_lo_split(b, u):
                dve.wait_ge(ada_hi_ready, 4 * b + (u + 1))
                tt(ada_lo[u % 2][:], ada_raw[u][:], ada_hi[u % 2][:].bitcast(F32), ALU.subtract).then_inc(ada_lo_ready, 1)

            def read_mod(b):
                dve.wait_ge(ada_turned, b + 1)
                tt(mod[:, bass.ds(4 * b, 4), :], pt[:, 0:4 * NC_].rearrange("p (t n) -> p t n", n=NC_),
                   prmv("bias")[:, bass.ds(4 * b, 4)].unsqueeze(2).broadcast_to([P, 4, NC_]), ALU.add).then_inc(mod_ready, 1)

            def scale_mod(j, sc, blocks):
                dve.wait_ge(mod_ready, blocks)
                gain = prmv("gain")[:, DT * j:DT * j + DT].unsqueeze(2).broadcast_to([P, DT, NC_])
                st.step(v.scalar_tensor_tensor(out=mod[:, sc:sc + DT, :], in0=mod[:, sc:sc + DT, :], scalar=1.0, in1=gain,
                                               op0=ALU.add, op1=ALU.mult))

            def halve_gate(g_, blocks):
                dve.wait_ge(mod_ready, blocks)
                st.step(v.tensor_scalar(mod[:, g_:g_ + DT, :], mod[:, g_:g_ + DT, :], 0.5, None, ALU.mult))

            def norm_rstd(j):
                dve.wait_ge(root_ready, j + 1)
                st.mark(v.reciprocal(rms[:, 0:4], rms[:, 0:4]))
                st.step(v.reciprocal(rms[0:HS, 4:6], rms[0:HS, 4:6]))
                ident = prmv("ident")
                v.scalar_tensor_tensor(out=view4(tmp[0]), in0=rms[:, 0:4].unsqueeze(2).broadcast_to([P, 4, P]), scalar=float(D_MODEL),
                                       in1=ident.unsqueeze(1).broadcast_to([P, 4, P]), op0=ALU.mult, op1=ALU.mult)
                v.scalar_tensor_tensor(out=tmp[1][0:HS, :, 0:HS], in0=rms[0:HS, 4:6].unsqueeze(2).broadcast_to([HS, 2, HS]),
                                       scalar=float(D_MODEL), in1=ident[0:HS, 0:HS].unsqueeze(1).broadcast_to([HS, 2, HS]),
                                       op0=ALU.mult, op1=ALU.mult).then_inc(diag_ready, 1)
                dve.wait_ge(rstd_ready, j + 1)

            def norm_samples(out, sc, sh):
                rs = pn[:, :, HP:HALF].unsqueeze(1).broadcast_to([P, DT, HALVES, HS])
                st.step(tt(out, x[:, :, :, HP:HALF], rs, ALU.mult))
                for n, op in ((sc, ALU.mult), (sh, ALU.add)):
                    for h in range(HALVES):
                        o = out[:, :, h].rearrange("p t (b s) -> p t b s", s=DEC_SEQ)
                        by_seq = mod[:, n:n + DT, 1 + 4 * h:5 + 4 * h].unsqueeze(3).broadcast_to([P, DT, 4, DEC_SEQ])
                        ins = tt(o, o, by_seq, op)
                        if n == sc:
                            st.mark(ins)
                    if n == sc:
                        st.wait()
                return ins

            def scaled_tiles(i):
                tt(norm_tmp[:, 2 * i:2 * i + 2, :, 0:HP], x[:, 2 * i:2 * i + 2, :, 0:HP],
                   pn[:, :, 0:HP].unsqueeze(1).broadcast_to([P, 2, HALVES, HP]), ALU.mult).then_inc(scaled, 1)

            def even_tile(j, i, out, sc, sh):
                dve.wait_ge(scaled, DT // 2 * j + i + 1)
                m = 2 * i
                return v.tensor_scalar(prompt(out), prompt(norm_tmp[:, m]), mod[:, m + sc, 0:1], mod[:, m + sh, 0:1], ALU.mult, ALU.add)

            def norm(j, sc, sh):
                norm_rstd(j)

                def odd_lo(i):
                    m = 2 * i + 1
                    dve.wait_ge(h_hi_ready[1], DT // 2 * j + i + 1)
                    tt(prompt(h_lo[:, m]), prompt(norm_out[:, m]), prompt(h_hi[:, m]).bitcast(F32), ALU.subtract)\
                        .then_inc(h_lo_ready[1], 1)

                for i in range(DT // 2):
                    scaled_tiles(i)
                    even_tile(j, i, norm_out[:, 2 * i], sc, sh).then_inc(tile_ready[0], 1)
                    if i == 0:
                        if j:
                            dve.wait_ge(hs_lo_ready, j)
                        norm_samples(hs32, sc, sh).then_inc(hs_ready, 1)
                    else:
                        odd_lo(i - 1)
                odd_lo(DT // 2 - 1)

            def up(phase, block0, before_last=None):
                first = phase[0]

                def hidden(f, ada, turned=None):
                    pair = f + first
                    b = f + block0
                    if ada:
                        ada_lo_split(b, 0)
                        ada_lo_split(b, 1)
                        if not (isinstance(f, int) and f == 0):
                            read_mod(b - 1)
                        ada_lo_split(b, 2)
                        ada_lo_split(b, 3)
                    if turned is not None:
                        read_mod(turned)
                    dve.wait_ge(acc_free[0], pair + 1)
                    dve.wait_ge(acc_ready[1], pair + 1)
                    if not (isinstance(f, int) and f == 0):
                        dve.wait_ge(hid_lo_ready, f + HT * UP.index(phase))
                    tt(h32[0][:], tmp[0][:], acc[1][:, :, 0:HALF], ALU.mult).then_inc(acc_free[1], 1)
                    dve.wait_ge(acc_free[1], pair + 1)
                    dve.wait_ge(hid_hi_ready, f + (HT * UP.index(phase) + 1))
                    tt(hid_lo[:, f], h32[0][:], hid_hi[:, f].bitcast(F32), ALU.subtract).then_inc(hid_lo_ready, 1)

                if block0:
                    hidden(0, True)
                    with dve.Fori(1, 9) as f:
                        hidden(f, True)
                    hidden(9, False, turned=block0 + 8)
                    if before_last:
                        before_last()
                    hidden(10, False)
                else:
                    with dve.Fori(0, HT) as f:
                        hidden(f, False)

            def residual(pair, s, m, gate_, square):
                dve.wait_ge(acc_ready[s], pair + 1)
                st.mark(v.scalar_tensor_tensor(out=prompt(x[:, m]), in0=prompt(acc[s]), scalar=mod[:, m + gate_, 0:1],
                                               in1=prompt(x[:, m]), op0=ALU.mult, op1=ALU.add))
                tt(gs[s][:].rearrange("p h (b s) -> p h b s", s=DEC_SEQ), sample4(acc[s]),
                   per_seq(mod[:, m + gate_, 1:NC_]), ALU.mult).then_inc(acc_free[s], 1)
                dve.wait_ge(acc_free[s], pair + 1)
                st.step(tt(sample(x[:, m]), sample(x[:, m]), gs[s][:], ALU.add))
                if square:
                    st.step(tt(tmp[s][:], x[:, m], x[:, m], ALU.mult))
                    st.step(tt(sumsq[:], sumsq[:], tmp[s][:], ALU.add))

            def residuals(phase, gate_, square, extra=None, extra_steps=0):
                if square:
                    st.step(v.memset(sumsq[:], 0.0))
                with st.loop(0, 4, (8 if square else 4) + extra_steps) as i:
                    if extra:
                        extra(i)
                    for s in range(2):
                        residual(i + phase[0], s, 2 * i + s, gate_, square)
                if square:
                    dve.sem_inc(sumsq_ready, 1)

            v.memset(eps_t[:], EPS).then_inc(eps_ready, 1)
            dve.wait_ge(c_hi_ready, 1)
            tt(c_split[:, :, NC_:2 * NC_], h32[0][:, 0, 0:DT * NC_].rearrange("p (t n) -> p t n", n=NC_),
               c_split[:, :, 0:NC_].bitcast(F32), ALU.subtract).then_inc(c_ready, 1)
            ada_lo_split(0, 0)
            ada_lo_split(0, 1)
            lam = prmv("lam").rearrange("p (a t) -> p a t", a=3)
            dve.wait_ge(s5_exp, 1)
            st.mark(tt(s5t[:, 1], lam[:, 0], s5t[:, 0], ALU.mult))
            st.step(tt(s5t[:, 2], lam[:, 1], s5t[:, 0], ALU.mult))
            magic = 1.5 * 2.0 ** 23
            st.step(v.tensor_scalar(s5t[:, 4], s5t[:, 2], float(1 / (2 * np.pi)), magic, ALU.mult, ALU.add))
            st.step(v.tensor_scalar(s5t[:, 4], s5t[:, 4], magic, None, ALU.subtract))
            for part in TWO_PI:
                st.step(v.scalar_tensor_tensor(out=s5t[:, 2], in0=s5t[:, 4], scalar=-part, in1=s5t[:, 2],
                                               op0=ALU.mult, op1=ALU.add))
            st.step(v.tensor_scalar(s5t[:, 2], s5t[:, 2], PI_LOW, -PI_LOW, ALU.min, ALU.max))
            st.step(v.tensor_scalar(s5t[:, 5], s5t[:, 2], -1.0, None, ALU.mult))
            st.step(tt(s5t[:, 3], s5t[:, 2], s5t[:, 5], ALU.max))
            v.tensor_scalar(s5t[:, 3], s5t[:, 3], -1.0, float(np.pi / 2), ALU.mult, ALU.add).then_inc(s5_angle, 1)
            ada_lo_split(0, 2)
            ada_lo_split(0, 3)
            with dve.Fori(1, 4) as b:
                ada_lo_split(b, 0)
                ada_lo_split(b, 1)
                read_mod(b - 1)
                ada_lo_split(b, 2)
                ada_lo_split(b, 3)
            read_mod(3)
            scale_mod(0, SC1, 4)

            pr, pi = s5pow[:, 0], s5pow[:, 1]
            t0, t1, t2, t3 = (s5t[:, n] for n in (4, 5, 6, 7))

            def unit_length(k):
                st.mark(tt(t0, pr[:, k], pr[:, k], ALU.mult))
                st.step(tt(t1, pi[:, k], pi[:, k], ALU.mult))
                st.step(tt(t0, t0, t1, ALU.add))
                st.step(v.tensor_scalar(t0, t0, -0.5, 1.5, ALU.mult, ALU.add))
                st.mark(tt(pr[:, k], pr[:, k], t0, ALU.mult))
                st.step(tt(pi[:, k], pi[:, k], t0, ALU.mult))

            def s5_constants():
                dve.wait_ge(s5_trig, 1)
                for k in range(8):
                    if k:
                        st.mark(tt(t0, pr[:, k - 1], pr[:, k - 1], ALU.mult))
                        st.mark(tt(t1, pi[:, k - 1], pi[:, k - 1], ALU.mult))
                        st.step(tt(t2, pr[:, k - 1], pi[:, k - 1], ALU.mult))
                        st.mark(tt(pr[:, k], t0, t1, ALU.subtract))
                        st.step(v.tensor_scalar(pi[:, k], t2, 2.0, None, ALU.mult))
                    unit_length(k)
                st.mark(tt(s5lam[:, 0], s5r[:], pr[:, 0], ALU.mult))
                st.step(tt(s5lam[:, 1], s5r[:], pi[:, 0], ALU.mult))
                st.mark(tt(t0, lam[:, 0], lam[:, 0], ALU.mult))
                st.mark(tt(t1, lam[:, 1], lam[:, 1], ALU.mult))
                st.step(v.tensor_scalar(t2, s5lam[:, 0], 1.0, None, ALU.subtract))
                st.step(tt(t0, t0, t1, ALU.add))
                st.step(v.reciprocal(t3, t0))
                st.mark(tt(t0, t2, lam[:, 0], ALU.mult))
                st.step(tt(t1, s5lam[:, 1], lam[:, 1], ALU.mult))
                st.step(tt(t0, t0, t1, ALU.add))
                st.step(tt(s5beta[:, 0], t0, t3, ALU.mult))
                st.mark(tt(t0, s5lam[:, 1], lam[:, 0], ALU.mult))
                st.step(tt(t1, t2, lam[:, 1], ALU.mult))
                st.step(tt(t0, t0, t1, ALU.subtract))
                st.step(tt(s5beta[:, 1], t0, t3, ALU.mult))

            norm(0, SC1, SH1)
            up(UP[0], 4, before_last=s5_constants)
            halve_gate(G1, 13)

            dve.wait_ge(b_in, 32)

            def by_tile(t):
                return flat(t)[:, 0:NT * 32].rearrange("p (t c) -> p t c", t=NT)
            br, bi = by_tile(tmp[0]), by_tile(tmp[1])
            beta_r, beta_i = (s5beta[:, n].unsqueeze(2).broadcast_to([P, NT, 32]) for n in range(2))
            st.mark(tt(by_tile(h32[0]), br, beta_r, ALU.mult))
            st.step(tt(by_tile(root), bi, beta_i, ALU.mult))
            st.mark(tt(by_tile(h32[0]), by_tile(h32[0]), by_tile(root), ALU.subtract))
            st.mark(tt(by_tile(h32[1]), br, beta_i, ALU.mult))
            st.step(tt(by_tile(sumsq), bi, beta_r, ALU.mult))
            tt(by_tile(h32[1]), by_tile(h32[1]), by_tile(sumsq), ALU.add).then_inc(bbar_ready, 1)
            st.mark(v.memset(et[:, 0, :, 0:1], 1.0))
            st.step(v.memset(et[:, 1, :, 0:1], 0.0))

            def table(i):
                for k in range(7):
                    n = 2 ** k
                    er, ei = (et[:, r, bass.ds(4 * i, 4), 0:n] for r in range(2))
                    o_r, o_i = (et[:, r, bass.ds(4 * i, 4), n:2 * n] for r in range(2))
                    qr, qi = (s5pow[:, r, k, bass.ds(4 * i, 4)].unsqueeze(2).broadcast_to([P, 4, n]) for r in range(2))
                    u0, u1, u2, u3 = (view4(t)[:, :, 0:n] for t in (tmp[0], tmp[1], root, sumsq))
                    st.mark(tt(u0, er, qr, ALU.mult))
                    st.mark(tt(u1, ei, qi, ALU.mult))
                    st.mark(tt(u2, er, qi, ALU.mult))
                    st.step(tt(u3, ei, qr, ALU.mult))
                    st.mark(tt(o_r, u0, u1, ALU.subtract))
                    st.step(tt(o_i, u2, u3, ALU.add))

            residuals(DOWN[0], G1, False, extra=table, extra_steps=42)
            dve.sem_inc(table_done, 1)
            dve.wait_ge(bbar_turned, 1)
            up(UP[1], 13)
            halve_gate(G3, 22)
            scale_mod(1, SC2, 22)
            scale_mod(2, SC3, 22)
            scale_mod(3, SCF, 22)
            residuals(DOWN[1], G1, True)
            norm(1, SC2, SH2)

            v.memset(lbs[:], 0.0).then_inc(lbs_clear, 1)
            dve.sem_inc(bu_used, 2)
            dve.sem_inc(y_used, 1)

            def read_y(ct, j):
                gi = 4 * ct + j
                dve.wait_ge(y_ready, gi + 3)
                v.scalar_tensor_tensor(out=proj[:, ct, SEG * j:SEG * (j + 1)], in0=proj[:, ct, SEG * j:SEG * (j + 1)],
                                       scalar=prm[:, bass.ds(ct + PRM["skip"][0], 1)], in1=pa[:, 0:SEG],
                                       op0=ALU.mult, op1=ALU.add).then_inc(y_used, 1)

            def segment(ct, j):
                gi, b = 4 * ct + j, j % 2
                er, ei = et[:, 0, bass.ds(4 * ct, 4), :], et[:, 1, bass.ds(4 * ct, 4), :]
                u0, u1 = view4(tmp[0]), view4(tmp[1])
                dve.wait_ge(bu_ready, gi + 2)
                dve.wait_ge(xi_ready, gi + 1)
                bur, bui = bu[b][:, 0], bu[b][:, 1]
                st.mark(tt(u0, bur, er, ALU.mult))
                st.step(tt(u1, bui, ei, ALU.mult))
                st.step(tt(z[b][:, 0], u0, u1, ALU.add))
                st.mark(tt(u0, bui, er, ALU.mult))
                tt(u1, bur, ei, ALU.mult).then_inc(bu_used, 1)
                dve.wait_ge(bu_used, gi + 3)
                st.step(tt(z[b][:, 1], u0, u1, ALU.subtract))
                for r in range(2):
                    for t in range(4):
                        first = 0.0 if j == 0 else carry[:, r, t:t + 1]
                        ins = v.tensor_tensor_scan(z[b][:, r, t], s5r[:, bass.ds(4 * ct + t, 1)].broadcast_to([P, SEG]),
                                                   z[b][:, r, t], first, ALU.mult, ALU.add)
                ins.then_inc(z_ready, 1)
                dve.wait_ge(z_ready, gi + 1)
                st.mark(tt(u0, z[b][:, 0], er, ALU.mult))
                st.step(tt(u1, z[b][:, 1], ei, ALU.mult))
                dve.wait_ge(y_ready, gi + 1)
                tt(xc[b][:, 0], u0, u1, ALU.subtract).then_inc(xr_ready, 1)
                if j < 3:
                    qr, qi = (s5pow[:, r, 7, bass.ds(4 * ct, 4)] for r in range(2))
                    zr, zi = z[b][:, 0, :, SEG - 1], z[b][:, 1, :, SEG - 1]
                    st.mark(tt(ct4[:, 0], zr, qr, ALU.mult))
                    st.mark(tt(ct4[:, 1], zi, qi, ALU.mult))
                    st.mark(tt(ct4[:, 2], zr, qi, ALU.mult))
                    st.step(tt(ct4[:, 3], zi, qr, ALU.mult))
                    st.mark(tt(carry[:, 0], ct4[:, 0], ct4[:, 1], ALU.subtract))
                    st.step(tt(carry[:, 1], ct4[:, 2], ct4[:, 3], ALU.add))
                else:
                    dve.wait_ge(xr_ready, gi + 1)
                    v.tensor_copy(x_last[:, 0, bass.ds(4 * ct, 4)], xc[1][:, 0, :, SEG - 1]).then_inc(x_last_ready, 1)
                if j >= 2:
                    read_y(ct, j - 2)
                elif not (isinstance(ct, int) and ct == 0):
                    read_y(ct - 1, j + 2)

            def rotate_k(ct):
                dve.wait_ge(ksw_ready, ct + 1)
                k_tile = proj[:, 4 * ct + 5]
                st.mark(tt(k_tile, k_tile, rope[0], ALU.mult))
                st.step(tt(swap[:], swap[:], rope[1], ALU.mult))
                tt(k_tile, k_tile, swap[:], ALU.add).then_inc(krot_ready, 1)

            def channel_tile(ct):
                for j in range(4):
                    segment(ct, j)
                    if j == 2:
                        rotate_k(ct)

            dve.wait_ge(rope_in, 32)
            channel_tile(0)
            with st.loop(1, CT, 4 * 7 + 3 * 6 + 2) as ct:
                channel_tile(ct)
            read_y(CT - 1, 2)
            read_y(CT - 1, 3)

            st.step(v.memset(mv[:], 1.0))
            dve.sem_inc(m32_ready, 1)
            dve.sem_inc(head_stored, 16)
            dve.wait_ge(hsm_in, 16)
            dve.wait_ge(qrot_ready, CT)

            def operands(h):
                dve.wait_ge(hc_in, 16 * h + 16)
                if not (isinstance(h, int) and h == 0):
                    dve.wait_ge(o_ready, h)
                tt(qm[:], proj[:, 4 * h + 4, SEQ:TOK].unsqueeze(1).broadcast_to([P, DEC_BATCH, NS]),
                   hcv("qmask").rearrange("p (b n) -> p b n", b=DEC_BATCH), ALU.mult).then_inc(qm_ready, 1)
                dve.wait_ge(tk_ready, h + 1)
                tt(kt[:, 0:4], pn[:, 0].rearrange("p (t n) -> p t n", t=4),
                   hsv(h, "kdec")[:, 0:4].unsqueeze(2).broadcast_to([P, 4, DK]), ALU.mult)
                v.tensor_scalar(kt[0:NS, 4], pn[0:NS, 1, 0:DK], hsv(h, "kdec")[0:NS, 4:5], None, ALU.mult)
                v.tensor_copy(vt[0:NS, 4], pn[0:NS, 1, DK:DK + DV]).then_inc(kt_ready, 1)
                dve.wait_ge(scores_ready, h + 1)
                at = 0
                for t in range(4):
                    n = SEQ - P * t
                    tt(sc[:, at:at + n], scores_at(t), hcv("mask")[:, 0:n], ALU.mult)
                    at += n
                tt(scs[:], acc[1][0:NS, 0, 2 * P:2 * P + NS], hsv(h, "smask")[0:NS], ALU.mult).then_inc(scm_ready, 1)

            def head_normed(h):
                dve.wait_ge(spp_ready, h + 1)
                dve.wait_ge(head_stored, 32 * h + 16)
                v.tensor_copy(sp_out[:], pn[:, 0, 0:DV]).then_inc(sp_ready, 1)
                dve.wait_ge(o_ready, h + 1)
                for t in range(5):
                    rows = P if t < 4 else NS
                    src = pt[:, DV * t:DV * t + DV] if t < 4 else pa[0:NS, 0:DV]
                    ins = v.bn_stats(stat[0:rows, t], src)
                st.step(ins)
                dve.sem_inc(dve_settled, 1)
                for t in range(4):
                    v.bn_aggr(mv[:, t], stat[:, t])
                v.bn_aggr(mv[0:NS, 4], stat[0:NS, 4]).then_inc(mv_ready, 1)
                dve.wait_ge(snp_ready, h + 1)
                v.scalar_tensor_tensor(out=sn[:].rearrange("p (c b) v -> p c (b v)", c=2),
                                       in0=s0[:].rearrange("p (c b) v -> p c (b v)", c=2), scalar=hsv(h, "g4"), in1=acc[0][:],
                                       op0=ALU.mult, op1=ALU.add).then_inc(sn_ready, 1)
                dve.wait_ge(hrstd_ready, h + 1)
                for t in range(5):
                    rows = P if t < 4 else NS
                    src = pt[:, DV * t:DV * t + DV] if t < 4 else pa[0:NS, 0:DV]
                    ins = v.tensor_scalar(on[0:rows, t], src, mv[0:rows, t, 0:1], hrstd[0:rows, t], ALU.subtract, ALU.mult)
                ins.then_inc(on_ready, 1)

            def gated(h):
                dve.wait_ge(ot_ready, h + 1)
                dve.wait_ge(r_lo_ready, h + 1)
                tt(prompt(tmp[1]), pt[:].rearrange("p (h n) -> p h n", h=2),
                   proj[:, 4 * h + 7, 0:SEQ].rearrange("p (h n) -> p h n", h=2), ALU.mult)
                tt(sample(tmp[1]), pn[:, 1, 2 * P:2 * P + NS].rearrange("p (h n) -> p h n", h=2),
                   proj[:, 4 * h + 7, SEQ:TOK].rearrange("p (h n) -> p h n", h=2), ALU.mult).then_inc(m32_ready, 1)

            operands(0)
            dve.wait_ge(h0_in, 16)
            dve.wait_ge(bus_ready, CT + 1)
            bus5 = bus[:].rearrange("p r t (b s) -> p r t b s", s=DEC_SEQ)
            w = [view(t, NT * DEC_BATCH).rearrange("p (t b) -> p t b", t=NT) for t in (tmp[0], tmp[1], h32[0], h32[1])]
            lr, li = (s5lam[:, r].unsqueeze(2).broadcast_to([P, NT, DEC_BATCH]) for r in range(2))
            for s in range(DEC_SEQ):
                qr, qi = (h0[:, r] if s == 0 else xs[:, r, :, :, s - 1] for r in range(2))
                st.mark(tt(w[0], qr, lr, ALU.mult))
                st.mark(tt(w[1], qi, li, ALU.mult))
                st.mark(tt(w[2], qr, li, ALU.mult))
                st.step(tt(w[3], qi, lr, ALU.mult))
                st.mark(tt(w[0], w[0], w[1], ALU.subtract))
                st.step(tt(w[2], w[2], w[3], ALU.add))
                st.mark(tt(xs[:, 0, :, :, s], w[0], bus5[:, 0, :, :, s], ALU.add))
                st.step(tt(xs[:, 1, :, :, s], w[2], bus5[:, 1, :, :, s], ALU.add))
            dve.sem_inc(xs_ready, 1)
            v.tensor_copy(xs_last[:], xs[:, :, :, :, DEC_SEQ - 1]).then_inc(xs_last_ready, 1)
            skip = prmv("skip").unsqueeze(2).broadcast_to([P, CT, NS])
            u_s = proj[:, 0:CT, SEQ:TOK]
            st.step(tt(u_s, u_s, skip, ALU.mult))
            head_normed(0)
            operands(1)
            gated(0)
            dve.wait_ge(ys_ready, 1)
            st.step(tt(u_s, u_s, pa[:, 0:CT * NS].rearrange("p (t n) -> p t n", t=CT), ALU.add))
            dve.wait_ge(y_used, 17)
            dve.sem_inc(y_all, 1)
            with st.loop(1, HEADS - 1, 1) as h:
                head_normed(h)
                operands(h + 1)
                gated(h)
            head_normed(HEADS - 1)
            gated(HEADS - 1)

            def glu_tile(i, first=False):
                pair = i + GLU[0]
                if not first:
                    dve.wait_ge(m_lo_ready, i)
                dve.wait_ge(acc_free[1], pair + 1)
                dve.wait_ge(acc_ready[0], pair + 1)
                tt(h32[0][:], tmp[0][:], acc[0][:, :, 0:HALF], ALU.mult).then_inc(acc_free[0], 1)
                dve.wait_ge(acc_free[0], pair + 1)
                dve.wait_ge(m_hi_ready, i + 1)
                tt(glu_lo[:, i], h32[0][:], glu_hi[:, i].bitcast(F32), ALU.subtract).then_inc(m_lo_ready, 1)

            glu_tile(0, first=True)
            with dve.Fori(1, GLU[1]) as i:
                glu_tile(i)
            residuals(OUT, G2, True)
            norm(2, SC3, SH3)
            up(UP[2], 0)
            residuals(DOWN[2], G3, False)
            up(UP[3], 0)
            residuals(DOWN[3], G3, True)
            norm_rstd(3)
            st.step(norm_samples(x[:, :, :, HP:HALF], SCF, SHF))

            for i in range(DT // 2):
                scaled_tiles(i)
                even_tile(3, i, x[:, 2 * i], SCF, SHF).then_inc(y_even, 1)

        @block.tensor
        def _(pe):
            mm = nc.tensor.matmul

            def unit_of(pair, s, tiles, rhs, first_use=False, ready=None):
                pe.wait_ge(hi_ready[s], pair + 1)
                if not first_use:
                    pe.wait_ge(acc_free[s], pair)
                for n, t in enumerate(tiles):
                    if ready:
                        ready(t)
                    for part in range(2):
                        for c in range(2):
                            mm(acc[s][:, c, 0:HALF], w_hi[s][:, t], rhs(t)[part][:, c], start=(n == 0 and part == 0), stop=False)
                pe.wait_ge(lo_ready[s], pair + 1)
                for n, t in enumerate(tiles):
                    for c in range(2):
                        ins = mm(acc[s][:, c, 0:HALF], w_lo[s][:, t], rhs(t)[0][:, c], start=False, stop=(n == len(tiles) - 1))
                ins.then_inc(acc_ready[s], 1)

            def both_units(pair, k, ready, first_use=False):
                for s in range(2):
                    pe.wait_ge(hi_ready[s], pair + 1)
                    pe.wait_ge(lo_ready[s], pair + 1)
                    if not first_use:
                        pe.wait_ge(acc_free[s], pair)
                for t in range(k):
                    ready(t)
                    for s in range(2):
                        for n, (w, r) in enumerate(((w_hi[s], h_hi), (w_hi[s], h_lo), (w_lo[s], h_hi))):
                            for c in range(2):
                                ins = mm(acc[s][:, c, 0:HALF], w[:, t], r[:, t, c], start=(t == 0 and n == 0),
                                         stop=(t == k - 1 and n == 2))
                        if t == k - 1:
                            ins.then_inc(acc_ready[s], 1)

            def unit(pair, s, k, r_hi, r_lo, first_use=False, ready=None):
                unit_of(pair, s, range(k), lambda t: (r_hi[:, t], r_lo[:, t]), first_use, ready)

            def ada_unit(b, u):
                pe.wait_ge(ada_lo_ready, 4 * b + (u + 1))
                if u == 0 and not (isinstance(b, int) and b == 0):
                    pe.wait_ge(ada_row_ready, b)
                for w, part in ((ada_hi[u % 2], 0), (ada_lo[u % 2], 1)):
                    for k in range(2):
                        ins = mm(pa[0:2 * NC_, :], c_split[:, 2 * u + k], w[:, k],
                                 start=(u == 0 and part == 0 and k == 0), stop=(u == 3 and part == 1 and k == 1))
                ins.then_inc(ada_used, 1)

            def ada_turn(b):
                pe.wait_ge(ada_row_ready, b + 1)
                if not (isinstance(b, int) and b == 0):
                    pe.wait_ge(mod_ready, b)
                for t in range(4):
                    ins = mm(pt[:, NC_ * t:NC_ * (t + 1)], ada_row[:, P * t:P * (t + 1)], prmv("sel")[0:2 * NC_],
                             start=True, stop=True)
                ins.then_inc(ada_turned, 1)

            def normed(j):
                def ready(t):
                    if t == 0:
                        pe.wait_ge(hs_lo_ready, j + 1)
                    pe.wait_ge(h_lo_ready[t % 2], 4 * j + t // 2 + 1)
                return ready

            def counted(sem_, base):
                return lambda t: pe.wait_ge(sem_, base + t + 1)

            def mean_square(j):
                pe.wait_ge(sumsq_ready, j + 1)
                for h in range(HALVES):
                    for c in range(3):
                        cols = slice(P * c, min(P * (c + 1), HALF))
                        rows, at = (P, 2 * h + c) if c < 2 else (HS, 4 + h)
                        ins = mm(pn[0:rows, 0, HALF + at:HALF + at + 1], sumsq[:, h, cols], prmv("mean")[:, 0:1],
                                 start=True, stop=True)
                ins.then_inc(ms_ready, 1)
                pe.wait_ge(diag_ready, j + 1)
                for h in range(HALVES):
                    mm(pn[:, h, 0:HP], prmv("mean"), view4(tmp[0])[:, 2 * h:2 * h + 2], start=True, stop=True)
                    ins = mm(pn[:, h, HP:HALF], prmv("mean")[0:HS], tmp[1][0:HS, h, 0:HS], start=True, stop=True)
                ins.then_inc(rstd_ready, 1)

            def up(phase, block0, j=None):
                first, n, k = phase

                def hidden(f, ada, first_use=False, ready=None, turned=None):
                    if ready:
                        both_units(f + first, k, ready, first_use)
                    else:
                        unit(f + first, 0, k, h_hi, h_lo)
                    if ada:
                        if not (isinstance(f, int) and f == 0):
                            ada_turn(f + (block0 - 1))
                        ada_unit(f + block0, 0)
                        ada_unit(f + block0, 1)
                    if turned is not None:
                        ada_turn(turned)
                    if not ready:
                        unit(f + first, 1, k, h_hi, h_lo)
                    if ada:
                        ada_unit(f + block0, 2)
                        ada_unit(f + block0, 3)

                ready = None if j is None else normed(j)
                if block0:
                    hidden(0, True, first_use=(first == 0), ready=ready)
                    with pe.Fori(1, 9) as f:
                        hidden(f, True)
                    hidden(9, False, turned=block0 + 8)
                    hidden(10, False)
                else:
                    hidden(0, False, ready=ready)
                    with pe.Fori(1, n) as f:
                        hidden(f, False)

            def down(phase):
                first, n, k = phase
                unit(first, 0, k, hid_hi, hid_lo, ready=counted(hid_lo_ready, HT * DOWN.index(phase)))
                unit(first, 1, k, hid_hi, hid_lo)
                with pe.Fori(1, n) as i:
                    unit(i + first, 0, k, hid_hi, hid_lo)
                    unit(i + first, 1, k, hid_hi, hid_lo)

            pe.wait_ge(prm_in, 16)
            pe.wait_ge(c_ready, 1)
            pe.wait_ge(c_hi_ready, 1)
            for u in range(4):
                ada_unit(0, u)
            with pe.Fori(1, 4) as b:
                ada_unit(b, 0)
                ada_unit(b, 1)
                ada_turn(b - 1)
                ada_unit(b, 2)
                ada_unit(b, 3)
            ada_turn(3)
            mean_square(0)
            up(UP[0], 4, j=0)
            down(DOWN[0])
            pe.wait_ge(bbar_ready, 1)
            for r in range(2):
                for t in range(CT):
                    ins = nc.tensor.transpose(pn[:, r, P * t:P * (t + 1)], flat(h32[r])[:, P * t:P * (t + 1)], prmv("ident"))
            ins.then_inc(bbar_turned, 1)
            up(UP[1], 13)
            down(DOWN[1])
            mean_square(1)

            both_units(PROJ_U[0], DT, normed(1))
            unit(PROJ_U[0] + 1, 0, DT, h_hi, h_lo)
            unit(PROJ_U[0] + 1, 1, DT, h_hi, h_lo)
            pe.sem_inc(y_ready, 2)
            def b_u(ct, j):
                pe.wait_ge(bu_ready, 4 * ct + (j + 1))
                for r in range(2):
                    for t in range(4):
                        ins = mm(pn[:, r, SEG * t:SEG * (t + 1)], lbs[:, r, t], proj[:, ct, SEG * j:SEG * (j + 1)],
                                 start=True, stop=True)
                ins.then_inc(b_done, 1)

            def c_x(ct, j):
                b = j % 2
                pe.wait_ge(xr_ready, 4 * ct + (j + 1))
                pe.wait_ge(xi_ready, 4 * ct + (j + 3))
                pe.wait_ge(y_used, 4 * ct + (j + 1))
                for t in range(4):
                    for r in range(2):
                        ins = mm(pa[32 * t:32 * t + 32, 0:SEG], lcs[:, t, r], xc[b][:, r, t], start=(r == 0), stop=(r == 1))
                ins.then_inc(y_ready, 1)

            def channel_tile(ct, first=False, last=False):
                qa = 2 * ct + PROJ_REST[0]
                pe.wait_ge(bus_ready, ct + 1)
                for r in range(2):
                    for t in range(4):
                        ins = mm(pt[:, (4 * r + t) * NS:(4 * r + t + 1) * NS], lbs[:, r, t], proj[:, ct, SEQ:TOK], start=True, stop=True)
                ins.then_inc(bs_done, 1)
                unit(qa, 0, DT, h_hi, h_lo)
                b_u(ct, 1)
                if not first:
                    c_x(ct - 1, 3)
                unit(qa, 1, DT, h_hi, h_lo)
                b_u(ct, 2)
                pe.wait_ge(lcs_staged, ct + 1)
                c_x(ct, 0)
                unit(qa + 1, 0, DT, h_hi, h_lo)
                b_u(ct, 3)
                c_x(ct, 1)
                unit(qa + 1, 1, DT, h_hi, h_lo)
                if not last:
                    pe.wait_ge(staged, ct + 2)
                    b_u(ct + 1, 0)
                c_x(ct, 2)
                if last:
                    c_x(ct, 3)

            pe.wait_ge(staged, 1)
            b_u(0, 0)
            channel_tile(0, first=True)
            with pe.Fori(1, CT - 1) as ct:
                channel_tile(ct)
            channel_tile(CT - 1, last=True)

            def samples_y():
                pe.wait_ge(xs_ready, 1)
                for ct in range(CT):
                    for t in range(4):
                        for r in range(2):
                            ins = mm(pa[32 * t:32 * t + 32, NS * ct:NS * (ct + 1)], lc[:, 4 * ct + t, r],
                                     xs[:, r, 4 * ct + t].rearrange("p b s -> p (b s)"), start=(r == 0), stop=(r == 1))
                ins.then_inc(ys_ready, 1)

            ident = prmv("ident")
            for s in range(2):
                pe.wait_ge(acc_free[s], GLU[0])
            pe.wait_ge(bu_ready, 4 * CT + 1)
            pe.wait_ge(bus_ready, CT + 1)
            pe.wait_ge(y_used, 4 * CT + 1)

            def front(h):
                pe.wait_ge(vs_ready, h + 1)
                for t in range(4):
                    nc.tensor.transpose(acc[1][:, 1, DV * t:DV * (t + 1)], vs[:, P * t:P * (t + 1)], ident)
                nc.tensor.transpose(pn[0:NS, 1, DK:DK + DV], vs[:, SEQ:TOK], ident).then_inc(tv_ready, 1)
                pe.wait_ge(ks_ready, h + 1)
                if not (isinstance(h, int) and h == 0):
                    pe.wait_ge(sp_ready, h)
                for t in range(4):
                    nc.tensor.transpose(pn[:, 0, DK * t:DK * (t + 1)], ks[:, P * t:P * (t + 1)], ident)
                nc.tensor.transpose(pn[0:NS, 1, 0:DK], ks[:, SEQ:TOK], ident).then_inc(tk_ready, 1)
                if not (isinstance(h, int) and h == 0):
                    pe.wait_ge(sn_ready, h)
                for t in range(4):
                    mm(scores_at(t), ks[:, P * t:P * (t + 1)], proj[:, 4 * h + 4, P * t:SEQ], start=True, stop=True)
                mm(acc[1][0:NS, 0, 2 * P:2 * P + NS], ks[:, SEQ:TOK], proj[:, 4 * h + 4, SEQ:TOK],
                   start=True, stop=True).then_inc(scores_ready, 1)

            def middle(h):
                pe.wait_ge(kt_ready, h + 1)
                pe.wait_ge(vt_ready, h + 1)
                for t in range(4):
                    ins = mm(pn[:, 0, 0:DV], kt[:, t], vt[:, t], start=(t == 0), stop=(t == 3))
                ins.then_inc(spp_ready, 1)
                pe.wait_ge(qm_ready, h + 1)
                pe.wait_ge(s0_in, 16 * h + 16)
                for b in range(DEC_BATCH):
                    mm(pa[0:NS, 0:DV], qm[:, b], s0[:, b], start=(b == 0), stop=False)
                pe.wait_ge(scm_ready, h + 1)
                pe.wait_ge(m32_ready, h + 1)
                for qt in range(4):
                    for t in range(qt + 1):
                        at = sum(SEQ - P * n for n in range(t)) + P * (qt - t)
                        mm(pt[:, DV * qt:DV * (qt + 1)], sc[:, at:at + P], vt[:, t], start=(t == 0), stop=(t == qt))
                mm(pa[0:NS, 0:DV], scs[:], vt[0:NS, 4], start=False, stop=True).then_inc(o_ready, 1)
                pe.wait_ge(vm_ready, h + 1)
                for c in range(2):
                    ins = mm(acc[0][:, c], kt[0:NS, 4], vm[0:NS, 4 * c:4 * c + 4].rearrange("p b v -> p (b v)"),
                             start=True, stop=True)
                ins.then_inc(snp_ready, 1)

            def back(h, last=False):
                pe.wait_ge(on_ready, h + 1)
                if not last:
                    pe.wait_ge(kt_ready, h + 2)
                for t in range(4):
                    nc.tensor.transpose(pt[:, P * t:P * (t + 1)], on[:, t], ident)
                nc.tensor.transpose(pn[:, 1, 2 * P:2 * P + NS], on[0:NS, 4], ident[0:NS, 0:NS]).then_inc(ot_ready, 1)

            front(0)
            middle(0)
            front(1)
            back(0)
            samples_y()
            pe.wait_ge(y_all, 1)
            with pe.Fori(1, HEADS - 1) as h:
                middle(h)
                front(h + 1)
                back(h)
            middle(HEADS - 1)
            back(HEADS - 1, last=True)

            unit(GLU[0], 0, GLU[2], h_hi, h_lo, ready=counted(g_lo_ready, 0))
            unit(GLU[0], 1, GLU[2], h_hi, h_lo)
            with pe.Fori(1, GLU[1]) as i:
                unit(i + GLU[0], 0, GLU[2], h_hi, h_lo)
                unit(i + GLU[0], 1, GLU[2], h_hi, h_lo)

            def mixed(t):
                return (h_hi[:, t], h_lo[:, t]) if t >= CT else (glu_hi[:, t], glu_lo[:, t])

            def mixed_ready(t):
                if t >= CT:
                    pe.wait_ge(r_lo_ready, t - CT + 2)
                else:
                    pe.wait_ge(m_lo_ready, t + 1)
            order = list(range(CT, DT)) + list(range(CT))
            unit_of(OUT[0], 0, order, mixed, ready=mixed_ready)
            unit_of(OUT[0], 1, order, mixed)
            with pe.Fori(1, OUT[1]) as i:
                unit_of(i + OUT[0], 0, order, mixed)
                unit_of(i + OUT[0], 1, order, mixed)
            mean_square(2)
            up(UP[2], 0, j=2)
            down(DOWN[2])
            up(UP[3], 0)
            down(DOWN[3])
            mean_square(3)


def head_constants():
    out = np.zeros((HEADS, P, HC_N), np.float32)
    small = np.zeros((P, HEADS, HS_N), np.float32)
    scale = np.float32(DK) ** np.float32(-0.5)
    i = np.arange(P)
    for h in range(HEADS):
        lg = np.log1p(-np.exp2(-5.0 - h))
        d = np.arange(SEQ)[None, :] - i[:, None]
        out[h, :, slice(*HC["mask"])] = np.where(d >= 0, np.exp(lg * np.maximum(d, 0)), 0.0) * scale
        n = np.arange(NS)
        seq, s = n // DEC_SEQ, n % DEC_SEQ
        qmask = (seq[None, :] == np.arange(DEC_BATCH)[:, None]) * np.exp(lg * (s + 1.0))[None, :]
        out[h, :, slice(*HC["qmask"])] = qmask.reshape(1, -1)
        kdec = np.zeros((P, 5))
        for t in range(4):
            kdec[:, t] = np.exp(lg * (SEQ - 1.0 - (P * t + i))) * scale
        kdec[:NS, 4] = np.exp(lg * (DEC_SEQ - 1.0 - s)) * scale
        small[:, h, slice(*HS_C["kdec"])] = kdec
        small[:, h, slice(*HS_C["g4"])] = np.exp(lg * DEC_SEQ)
        same = (seq[:, None] == seq[None, :]) & (s[None, :] >= s[:, None])
        small[:NS, h, slice(*HS_C["smask"])] = np.where(same, np.exp(lg * np.maximum(s[None, :] - s[:, None], 0)), 0.0) * scale
        small[:NS, h, slice(*HS_C["bmask"])] = seq[:, None] == np.arange(DEC_BATCH)[None, :]
    return out, small.reshape(P, -1)


def rope_table():
    half = DK // 2
    inv = (np.float32(10000.0) ** (-np.arange(half, dtype=np.float32) / np.float32(half))).astype(np.float32)
    pos = np.concatenate([np.arange(SEQ), PAST_LEN + np.tile(np.arange(DEC_SEQ), DEC_BATCH)]).astype(np.float32)
    ang = (pos[None, :] * inv[:, None]).astype(np.float32).astype(np.float64)
    cos, sin = np.cos(ang), np.sin(ang)
    return np.stack([np.concatenate([cos, cos]), np.concatenate([-sin, sin])]).astype(np.float32)


_OUTS = {"y": (DT, P, TOK), "ssm_prompt": (P, 2 * NT), "ssm_sample": (P, 2 * NT * DEC_BATCH),
         "ret_prompt": (HEADS, DK, DV), "ret_sample": (HEADS, DK, DEC_BATCH * DV)}


def kernel(**inputs):
    import concourse.bacc as bacc
    from concourse.bass_utils import run_bass_kernel_spmd

    v = {n: np.asarray(t) for n, t in inputs.items()}
    one = {n: t[0] if t.shape[0] == 1 and n not in ("x_prompt", "c_prompt") else t for n, t in v.items()}

    def tiled(w, k, m, order):
        return np.ascontiguousarray(w.reshape(k + m).transpose(order))

    feeds = {}
    xp = v["x_prompt"].reshape(HALVES, HP, D_MODEL)
    xs_ = v["x_sample"].reshape(HALVES, HS, D_MODEL)
    xt = np.concatenate([xp, xs_], 1)
    feeds["x"] = np.ascontiguousarray(xt.reshape(HALVES, HALF, DT, P).transpose(3, 2, 0, 1)).reshape(P, -1)
    for n in (1, 2):
        w = one[f"ffn{n}_w_in"]
        feeds[f"ffn{n}_up"] = tiled(w, (DT, P), (2, FT, P), (3, 2, 1, 0, 4)).reshape(FT, 2, P, DT * P)
        w = one[f"ffn{n}_w_out"]
        feeds[f"ffn{n}_down"] = np.ascontiguousarray(
            w.reshape(2, HT, P, DT, P).transpose(0, 3, 2, 1, 4)).reshape(2 * 4, 2, P, HT * P)
    order = list(range(CT)) + [CT + HEADS * part + h for h in range(HEADS) for part in range(4)]
    feeds["w_in"] = tiled(one["w_in_mix"], (DT, P), (20, P), (2, 1, 0, 3))[order].reshape(10, 2, P, DT * P)
    feeds["w_glu"] = tiled(one["s5_w_glu"], (4, P), (2, 4, P), (3, 2, 1, 0, 4)).reshape(4, 2, P, 4 * P)
    feeds["w_out"] = tiled(one["w_out_mix"], (DT, P), (DT, P), (2, 1, 0, 3)).reshape(4, 2, P, DT * P)
    wa = np.concatenate([one["w_ada"], v["w_ada_final"]], 1)
    feeds["ada"] = tiled(wa, (4, 2, P), (ADA_BLOCKS, ADA_N), (3, 0, 2, 1, 4)).reshape(ADA_BLOCKS, 4, P, 2 * ADA_N)

    prm = np.zeros((P, PRM_N), np.float32)

    def put(name, t):
        prm[:, slice(*PRM[name])] = t.reshape(P, -1)

    put("ident", np.eye(P, dtype=np.float32))
    put("mean", np.full((P, P), 1.0 / D_MODEL, np.float32))
    sel = np.zeros((P, NC_), np.float32)
    sel[np.arange(2 * NC_), np.arange(2 * NC_) % NC_] = 1.0
    put("sel", sel)
    put("bias", np.concatenate([one["b_ada"], v["b_ada_final"]]).reshape(MOD_TILES, P).T)
    put("gain", np.concatenate([one[n] for n in ("norm_ffn1", "norm_mix", "norm_ffn2")] + [v["norm_final"]]).reshape(4 * DT, P).T)
    put("skip", one["s5_d"].reshape(CT, P).T)

    def states(t):
        return np.moveaxis(t.reshape((NT, P) + t.shape[2:]), 0, 1)

    log_dt = np.repeat(one["s5_log_dt"][:, None], 64, 1)
    put("lam", np.stack([states(one["s5_lambda_re"]), states(one["s5_lambda_im"]), states(log_dt)], 1))
    c_all = np.concatenate([v["c_prompt"], v["c_sample"]], 0)
    put("c", c_all.reshape(NC_, DT, P).transpose(2, 1, 0))
    feeds["prm"] = prm

    def block_diagonal(t):
        out = np.zeros((P, NT, 32), np.float32)
        out[:64, :, :16] = t[:64]
        out[64:, :, 16:] = t[64:]
        return out

    feeds["s5_b"] = np.stack([block_diagonal(states(one[n])).reshape(P, -1) for n in ("s5_b_re", "s5_b_im")])
    feeds["s5_c"] = np.ascontiguousarray(np.stack(
        [block_diagonal(states(one[n].transpose(0, 2, 1))) for n in ("s5_c_re", "s5_c_im")], 2)).reshape(P, -1)
    h0 = [np.moveaxis(one[n].reshape(DEC_BATCH, NT, P), (0, 1, 2), (2, 1, 0)) for n in ("state_ssm_re", "state_ssm_im")]
    feeds["h0"] = np.ascontiguousarray(np.stack(h0, 1)).reshape(P, -1)
    feeds["s0"] = np.ascontiguousarray(one["state_ret"].transpose(1, 2, 0, 3)).reshape(HEADS, DK, -1)
    feeds["rope"] = rope_table()
    feeds["head_consts"], feeds["head_small"] = head_constants()

    nc = bacc.Bacc("TRN2", target_bir_lowering=False, num_devices=1)
    aps = {n: nc.dram_tensor(f"in_{n}", t.shape, F32, kind="ExternalInput").ap() for n, t in feeds.items()}
    aps |= {n: nc.dram_tensor(f"out_{n}", s, F32, kind="ExternalOutput").ap() for n, s in _OUTS.items()}
    build(nc, aps)
    r = run_bass_kernel_spmd(nc, [{f"in_{n}": t for n, t in feeds.items()}], core_ids=[0]).results[0]
    out = {n: np.asarray(r[f"out_{n}"]) for n in _OUTS}

    y = out["y"].reshape(DT, P, HALVES, HALF).transpose(2, 3, 0, 1).reshape(HALVES, HALF, D_MODEL)
    y_prompt = np.ascontiguousarray(y[:, :HP]).reshape(1, SEQ, D_MODEL)
    y_sample = np.ascontiguousarray(y[:, HP:]).reshape(DEC_BATCH, DEC_SEQ, D_MODEL)
    sp = out["ssm_prompt"].reshape(P, 2, NT).transpose(1, 2, 0).reshape(2, 1, 1, 32, 64)
    ss = out["ssm_sample"].reshape(P, 2, NT, DEC_BATCH).transpose(1, 3, 2, 0).reshape(2, 1, DEC_BATCH, 32, 64)
    ret_p = out["ret_prompt"].reshape(1, 1, HEADS, DK, DV)
    ret_s = np.ascontiguousarray(out["ret_sample"].reshape(HEADS, DK, DEC_BATCH, DV).transpose(2, 0, 1, 3))[None]
    return (y_prompt, y_sample, np.ascontiguousarray(sp[0]), np.ascontiguousarray(sp[1]), ret_p,
            np.ascontiguousarray(ss[0]), np.ascontiguousarray(ss[1]), ret_s)
```

```python
from contextlib import ExitStack, contextmanager

import numpy as np
import concourse.bass as bass
from concourse import mybir

F32, F32R = mybir.dt.float32, mybir.dt.float32r
ALU, ACT = mybir.AluOpType, mybir.ActivationFunctionType

P = 128
D_MODEL, SEQ, DEC_BATCH, DEC_SEQ, PAST_LEN = 1024, 512, 8, 4, 4096
D_FF = ((8 * D_MODEL // 3 + 255) // 256) * 256
EPS = 1e-6
DT = D_MODEL // P
HALVES = 2
HP, HS = SEQ // 2, DEC_BATCH * DEC_SEQ // 2
HALF = HP + HS
NS = DEC_BATCH * DEC_SEQ
TOK = SEQ + NS
NC_ = 1 + DEC_BATCH
FT = D_FF // P
HT = FT // 2
KMAX = HT
HEADS, DK, DV = 4, P, P
CT, NT, SEG = 4, 16, 128
ADA_BLOCKS, ADA_UNITS, ADA_N = 22, 4, 512
MOD_TILES = ADA_BLOCKS * 4
SH1, SC1, G1, SH2, SC2, G2, SH3, SC3, G3, SHF, SCF = range(0, MOD_TILES, DT)

UP = [(0, HT, DT), (15, HT, DT), (48, HT, DT), (63, HT, DT)]
DOWN = [(11, 4, HT), (26, 4, HT), (59, 4, HT), (74, 4, HT)]
PROJ_U, PROJ_REST, GLU, OUT = (30, 2, DT), (32, 8, DT), (40, 4, 4), (44, 4, DT)
PHASES = [UP[0], DOWN[0], UP[1], DOWN[1], PROJ_U, PROJ_REST, GLU, OUT, UP[2], DOWN[2], UP[3], DOWN[3]]
PAIRS = 78


def k_tiles(pair):
    return next(k for first, n, k in PHASES if first <= pair < first + n)


_two = np.float64(2 * np.pi)
_p0 = 6.28125
_p1 = float(np.float32(np.round((_two - _p0) * 2.0 ** 21) / 2.0 ** 21))
TWO_PI = (_p0, _p1, float(np.float32(_two - _p0 - _p1)))
PI_LOW = 3.1415925

SEL_N = NC_ + NC_ % 2
PRM = {}
_at = 0
for _name, _n in (("ident", P), ("mean", P), ("sel", SEL_N), ("bias", MOD_TILES), ("gain", 4 * DT), ("skip", CT),
                  ("lam", 3 * NT), ("c", DT * NC_)):
    PRM[_name] = (_at, _at + _n)
    _at += _n
PRM_N = _at
HC = {"mask": (0, SEQ), "qmask": (SEQ, SEQ + DEC_BATCH * NS)}
HC_N = SEQ + DEC_BATCH * NS
HS_C = {}
_at = 0
for _name, _n in (("kdec", 5), ("g4", 1), ("smask", NS), ("bmask", DEC_BATCH)):
    HS_C[_name] = (_at, _at + _n)
    _at += _n
HS_N = _at


class Steps:

    def __init__(self, eng, sem):
        self.eng, self.sem, self.base, self.k = eng, sem, 0, 0

    def mark(self, ins):
        ins.then_inc(self.sem, 1)
        self.k += 1

    def wait(self):
        self.eng.wait_ge(self.sem, self.base + self.k)

    def step(self, ins):
        self.mark(ins)
        self.wait()

    @contextmanager
    def loop(self, start, end, per):
        before = self.base + self.k
        with self.eng.Fori(start, end) as i:
            self.base, self.k = (i - start) * per + before, 0
            yield i
            assert self.k == per, (self.k, per)
        self.base, self.k = before + (end - start) * per, 0


def build(nc, a):
    with ExitStack() as ctx:
        def sb(name, shape, dt=F32):
            return ctx.enter_context(nc.sbuf_tensor(name, shape, dt))

        sems = {}

        def sem(name):
            if name not in sems:
                sems[name] = ctx.enter_context(nc.semaphore(name))
            return sems[name]

        x = sb("x", [P, DT, HALVES, HALF])
        h_hi = sb("h_hi", [P, DT, HALVES, HALF], F32R)
        h_lo = sb("h_lo", [P, DT, HALVES, HALF], F32R)
        w_raw = [sb(f"w_raw{s}", [P, KMAX, P]) for s in range(2)]
        w_hi = [sb(f"w_hi{s}", [P, KMAX, P], F32R) for s in range(2)]
        w_lo = [sb(f"w_lo{s}", [P, KMAX, P], F32R) for s in range(2)]
        mod = sb("mod", [P, MOD_TILES, NC_])
        prm = sb("prm", [P, PRM_N])
        c_split = sb("c_split", [P, DT, 2 * NC_], F32R)
        lb = sb("lb", [P, CT, 2, P])
        lc = sb("lc", [P, NT, 2, 32])
        sumsq, root = (sb(n, [P, HALVES, HALF]) for n in ("sumsq", "root"))
        rms = sb("rms", [P, 6])
        hs32 = root[:].rearrange("p h n -> p (h n)")[:, 0:DT * NS].rearrange("p (t h n) -> p t h n", t=DT, h=HALVES)
        gs = [sb(f"gs{s}", [P, HALVES, HS]) for s in range(2)]
        tmp = [sb(f"tmp{s}", [P, HALVES, HALF]) for s in range(2)]
        row = nc.sbuf_tensor("ada_row", [P, ADA_N], F32R)
        ada_row = row.__enter__()
        row.__exit__(None, None, None)
        h32 = [sb(f"h32_{s}", [P, HALVES, HALF]) for s in (1, 0)][::-1]
        sel = sb("sel", [64, SEL_N], F32R)
        s5r, s5lam, s5beta, s5pow = sb("s5r", [P, NT]), sb("s5lam", [P, 2, NT]), sb("s5beta", [P, 2, NT]), sb("s5pow", [P, 2, 8, NT])
        s5t = sb("s5t", [P, 8, NT])
        stat = sb("stat", [P, 5, 6])
        mv = sb("mv", [P, 5, 2])
        hrstd = sb("hrstd", [P, 5, 1])
        eps_t = sb("eps_t", [P, 1])
        epsm = sb("epsm", [P, 5, 2])
        x_last = sb("x_last", [P, 2, NT])
        carry = sb("carry", [P, 2, 4])
        ct4 = sb("ct4", [P, 4, 4])

        g = nc.sbuf_tensor("hid_hi", [P, HT, HALVES, HALF], F32R)
        hid_hi = g.__enter__()
        g2 = nc.sbuf_tensor("hid_lo", [P, HT, HALVES, HALF], F32R)
        hid_lo = g2.__enter__()
        glu_hi, glu_lo = hid_hi[:, 4:4 + CT], hid_lo[:, 0:CT]
        g2.__exit__(None, None, None)
        g.__exit__(None, None, None)
        proj = sb("proj", [P, 20, TOK])
        bus = sb("bus", [P, 2, NT, NS])

        norm_tmp, norm_out = (proj[:, n:n + DT].rearrange("p t (h c) -> p t h c", h=HALVES) for n in (DT, 0))

        sb("hid_rest", [P, 2 * HT * TOK - 20 * TOK - 2 * NT * NS])

        with ExitStack() as e_life:
            et = e_life.enter_context(nc.sbuf_tensor("et", [P, 2, NT, SEG], F32))
        with ExitStack() as late:
            def lsb(name, shape):
                return late.enter_context(nc.sbuf_tensor(name, shape, F32))
            xs = lsb("xs", [P, 2, NT, DEC_BATCH, DEC_SEQ])
            vm = lsb("vm", [P, DEC_BATCH, DV])
            hsm = lsb("hsm", [P, HEADS, HS_N])
            h0 = lsb("h0", [P, 2, NT, DEC_BATCH])
        sb("et_region", [P, 2 * NT * SEG])

        with ExitStack() as life:
            ada_raw = [life.enter_context(nc.sbuf_tensor(f"ada_raw{u}", [P, 2, ADA_N], F32)) for u in range(ADA_UNITS)]
            ada_hi = [life.enter_context(nc.sbuf_tensor(f"ada_hi{u}", [P, 2, ADA_N], F32R)) for u in range(2)]
            ada_lo = [life.enter_context(nc.sbuf_tensor(f"ada_lo{u}", [P, 2, ADA_N], F32R)) for u in range(2)]
        with ExitStack() as life:
            def rsb(name, shape):
                return life.enter_context(nc.sbuf_tensor(name, shape, F32))
            bu = [rsb(f"bu{s}", [P, 2, 4, SEG]) for s in range(2)]
            z = [rsb(f"z{s}", [P, 2, 4, SEG]) for s in range(2)]
            xc = [rsb(f"xc{s}", [P, 2, 4, SEG]) for s in range(2)]
            lbs = rsb("lbs", [P, 2, 4, P])
            lcs = rsb("lcs", [P, 4, 2, 32])
            swap = rsb("swap", [P, TOK])
        with ExitStack() as life:
            def rsb(name, shape):
                return life.enter_context(nc.sbuf_tensor(name, shape, F32))
            ks = rsb("ks", [P, TOK])
            vt, kt = rsb("vt", [P, 5, DV]), rsb("kt", [P, 5, DK])
            sc = rsb("sc", [P, 10 * P])
            scs = rsb("scs", [NS, NS])
            hc = rsb("hc", [P, HC_N])
            s0, sn = rsb("s0", [P, DEC_BATCH, DV]), rsb("sn", [P, DEC_BATCH, DV])
            qm = rsb("qm", [P, DEC_BATCH, NS])
            on = rsb("on", [P, 5, DV])
            sp_out = rsb("sp_out", [P, DV])
            xs_last = rsb("xs_last", [P, 2, NT, DEC_BATCH])
        sb("ada_region", [P, 2 * ADA_UNITS * 2 * ADA_N])

        def split_of(b, u):
            if isinstance(b, int) and b < 4:
                return tuple(t[:].rearrange("p t h n -> p (t h n)")[:, 2 * ADA_N * u:2 * ADA_N * (u + 1)]
                             .rearrange("p (k n) -> p k n", k=2) for t in (h_hi, h_lo))
            return ada_hi[u % 2][:], ada_lo[u % 2][:]

        def raw_of(b, u):
            if isinstance(b, int) and b in (1, 2):
                region = (et[:].rearrange("p r t n -> p (r t n)"), proj[:].rearrange("p t n -> p (t n)"))[b - 1]
                return region[:, 2 * ADA_N * u:2 * ADA_N * (u + 1)].rearrange("p (k n) -> p k n", k=2)
            return ada_raw[u][:]

        rope = [t[:].rearrange("p h n -> p (h n)") for t in (sumsq, root)]
        vs = rope[0]

        acc = [ctx.enter_context(nc.psum_tensor(f"acc{s}", [P, 2, 512], F32)) for s in range(2)]
        pn = ctx.enter_context(nc.psum_tensor("pn", [P, 2, 512], F32))
        pa = ctx.enter_context(nc.psum_tensor("pa", [P, 512], F32))
        pt = ctx.enter_context(nc.psum_tensor("pt", [P, 512], F32))

        def prmv(name):
            return prm[:, PRM[name][0]:PRM[name][1]]

        def hcv(name):
            return hc[:, HC[name][0]:HC[name][1]]

        def hsv(h, name):
            return hsm[:, h, HS_C[name][0]:HS_C[name][1]]

        def prompt(t):
            return t[:, :, 0:HP]

        def sample(t):
            return t[:, :, HP:HALF]

        def sample4(t):
            return sample(t).rearrange("p h (b s) -> p h b s", s=DEC_SEQ)

        def per_seq(t):
            return t.rearrange("p (h b) -> p h b", h=2).unsqueeze(3).broadcast_to([P, 2, 4, DEC_SEQ])

        def flat(t):
            return t[:].rearrange("p h n -> p (h n)")

        def view4(t):
            return flat(t)[:, 0:4 * SEG].rearrange("p (t n) -> p t n", t=4)

        def view(t, n):
            return flat(t)[:, 0:n]

        def scores_at(t):
            return (acc[0][:, 0, 0:SEQ], acc[0][:, 1, 0:3 * P], acc[1][:, 0, 0:2 * P], acc[0][:, 1, 3 * P:4 * P])[t]

        raw_in = [sem(f"raw_in{s}") for s in range(2)]
        hi_ready = [sem(f"hi_ready{s}") for s in range(2)]
        lo_ready = [sem(f"lo_ready{s}") for s in range(2)]
        acc_ready = [sem(f"acc_ready{s}") for s in range(2)]
        acc_free = [sem(f"acc_free{s}") for s in range(2)]
        ada_in = [sem(f"ada_in{u}") for u in range(ADA_UNITS)]
        ada_early = [[sem(f"ada_early{b}_{u}") for u in range(ADA_UNITS)] for b in (1, 2)]

        def ada_arrival(b, u):
            if isinstance(b, int) and b in (1, 2):
                return ada_early[b - 1][u], 16
            return ada_in[u], 16 if isinstance(b, int) and b == 0 else 16 * b - 16

        ada_hi_ready, ada_lo_ready, ada_used = sem("ada_hi_ready"), sem("ada_lo_ready"), sem("ada_used")
        ada_row_ready, ada_turned, mod_ready = sem("ada_row_ready"), sem("ada_turned"), sem("mod_ready")
        ada_row_hi, row_clear, sel_ready, zeros_ready = sem("ada_row_hi"), sem("row_clear"), sem("sel_ready"), sem("zeros_ready")
        prm_in, x_in, b_in, c_in = sem("prm_in"), sem("x_in"), sem("b_in"), sem("c_in")
        rope_in, h0_in, hc_in, s0_in, hsm_in = sem("rope_in"), sem("h0_in"), sem("hc_in"), sem("s0_in"), sem("hsm_in")
        silu_c, c_hi_ready, c_ready = sem("silu_c"), sem("c_hi_ready"), sem("c_ready")
        sumsq_ready, ms_ready, root_ready = sem("sumsq_ready"), sem("ms_ready"), sem("root_ready")
        squares = sem("squares")
        scale1_ready = sem("scale1_ready")
        diag_ready, rstd_ready = sem("diag_ready"), sem("rstd_ready")
        tile_ready = [sem("tile_even"), sem("tile_odd")]
        h_hi_ready = [sem("h_hi_even"), sem("h_hi_odd")]
        h_lo_ready = [sem("h_lo_even"), sem("h_lo_odd")]
        hs_ready, hs_hi_ready, hs_lo_ready, scaled = sem("hs_ready"), sem("hs_hi_ready"), sem("hs_lo_ready"), sem("scaled")
        hid_hi_ready, hid_lo_ready = sem("hid_hi_ready"), sem("hid_lo_ready")
        y_even, y_odd = sem("y_even"), sem("y_odd")
        stored = sem("stored")
        act_step, dve_step, pool_step = sem("act_step"), sem("dve_step"), sem("pool_step")
        s5_angle, s5_exp, s5_trig, bbar_ready, bbar_turned, lb_ready = (sem(n) for n in (
            "s5_angle", "s5_exp", "s5_trig", "bbar_ready", "bbar_turned", "lb_ready"))

        staged, b_done, bs_done = sem("staged"), sem("b_done"), sem("bs_done")
        bu_ready, bus_ready, y_used = sem("bu_ready"), sem("bus_ready"), sem("y_used")
        bu_used, xi_ready, y_ready = sem("bu_used"), sem("xi_ready"), sem("y_ready")
        z_ready, xr_ready, x_last_ready, lbs_clear = (sem(n) for n in ("z_ready", "xr_ready", "x_last_ready", "lbs_clear"))
        xs_ready, xs_last_ready, ys_ready, y_all = (sem(n) for n in ("xs_ready", "xs_last_ready", "ys_ready", "y_all"))
        gelu_ready, g_hi_ready, g_lo_ready, m_hi_ready, m_lo_ready = (sem(n) for n in (
            "gelu_ready", "g_hi_ready", "g_lo_ready", "m_hi_ready", "m_lo_ready"))
        lcs_staged, krot_ready, qrot_ready, qsw_ready, ksw_ready = (sem(n) for n in (
            "lcs_staged", "krot_ready", "qrot_ready", "qsw_ready", "ksw_ready"))
        m32_ready, r_lo_ready = sem("m32_ready"), sem("r_lo_ready")
        tv_ready, snp_ready, o_ready, ks_ready, r_hi_ready = (sem(n) for n in (
            "tv_ready", "snp_ready", "o_ready", "ks_ready", "r_hi_ready"))
        vs_ready, vt_ready, vm_ready = (sem(n) for n in ("vs_ready", "vt_ready", "vm_ready"))
        mv_ready, hrstd_ready, on_ready, kt_ready, qm_ready, scm_ready = (sem(n) for n in (
            "mv_ready", "hrstd_ready", "on_ready", "kt_ready", "qm_ready", "scm_ready"))
        tk_ready, scores_ready, spp_ready, sp_ready, sn_ready, ot_ready, head_stored = (sem(n) for n in (
            "tk_ready", "scores_ready", "spp_ready", "sp_ready", "sn_ready", "ot_ready", "head_stored"))
        eps_ready, table_done, pool_settled, dve_settled = (sem(n) for n in (
            "eps_ready", "table_done", "pool_settled", "dve_settled"))

        block = ctx.enter_context(nc.Block())

        @block.sync
        def _(sp):
            sp.dma_start(prm[:], a["prm"]).then_inc(prm_in, 16)

            def source(phase):
                first, n, k = phase
                name = ("up" if phase in UP else "down" if phase in DOWN else
                        {PROJ_U: "w_in", PROJ_REST: "w_in", GLU: "w_glu", OUT: "w_out"}[phase])
                if name in ("up", "down"):
                    j = (UP if name == "up" else DOWN).index(phase)
                    return a[f"ffn{1 + j // 2}_{name}"], (j % 2) * n
                return a[name], 2 if phase == PROJ_REST else 0

            def load_unit(phase, i, s, first_use=False):
                src, off = source(phase)
                k = phase[2]
                if not first_use:
                    sp.wait_ge(lo_ready[s], phase[0] + i)
                sp.dma_start(w_raw[s][:, 0:k, :],
                             src[i + off, s].rearrange("p (k m) -> p k m", k=k)).then_inc(raw_in[s], 16)

            def load_ada(b, u):
                if not isinstance(b, int) or b > 3:
                    sp.wait_ge(ada_lo_ready, (b - 1) * 4 + u + 1)
                elif b == 3:
                    sp.wait_ge(ada_lo_ready, u + 1)
                sp.dma_start(raw_of(b, u), a["ada"][b, u].rearrange("p (k n) -> p k n", k=2)).then_inc(ada_arrival(b, u)[0], 16)

            for u in range(ADA_UNITS):
                load_ada(0, u)
            sp.dma_start(x[:], a["x"].rearrange("p (t h n) -> p t h n", t=DT, h=2)).then_inc(x_in, 16)
            for b in range(1, 4):
                for u in range(ADA_UNITS):
                    load_ada(b, u)
            load_unit(UP[0], 0, 0, first_use=True)
            load_unit(UP[0], 0, 1, first_use=True)
            sp.dma_start(lc[:], a["s5_c"].rearrange("p (t r c) -> p t r c", t=NT, r=2)).then_inc(c_in, 16)

            def load_up(phase, block0, done=0):
                n_ada = 9 if block0 else 0
                if n_ada:
                    if done == 0:
                        load_unit(phase, 0, 0)
                    for u in range(ADA_UNITS):
                        load_ada(block0, u)
                    if done == 0:
                        load_unit(phase, 0, 1)
                    with sp.Fori(1, n_ada) as f:
                        load_unit(phase, f, 0)
                        for u in range(ADA_UNITS):
                            load_ada(f + block0, u)
                        load_unit(phase, f, 1)
                with sp.Fori(n_ada, HT) as f:
                    load_unit(phase, f, 0)
                    load_unit(phase, f, 1)

            def load_plain(phase):
                with sp.Fori(0, phase[1]) as i:
                    load_unit(phase, i, 0)
                    load_unit(phase, i, 1)

            load_up(UP[0], 4, done=1)
            load_unit(DOWN[0], 0, 0)
            load_unit(DOWN[0], 0, 1)
            sp.wait_ge(acc_free[1], DOWN[0][0])
            for r in range(2):
                sp.dma_start(flat(tmp[r])[:, 0:NT * 32], a["s5_b"][r]).then_inc(b_in, 16)
            with sp.Fori(1, 4) as i:
                load_unit(DOWN[0], i, 0)
                load_unit(DOWN[0], i, 1)
            load_up(UP[1], 13)
            load_plain(DOWN[1])
            load_plain(PROJ_U)
            sp.wait_ge(rstd_ready, 2)
            sp.wait_ge(hs_lo_ready, 2)
            for r in range(2):
                sp.dma_start(rope[r], a["rope"][r]).then_inc(rope_in, 16)
            load_plain(PROJ_REST)
            load_unit(GLU, 0, 0)
            load_unit(GLU, 0, 1)
            sp.wait_ge(y_used, 16 + 1)
            sp.wait_ge(xi_ready, 16 + 2)
            sp.dma_start(h0[:], a["h0"].rearrange("p (r t b) -> p r t b", r=2, t=NT)).then_inc(h0_in, 16)
            sp.dma_start(hsm[:], a["head_small"].rearrange("p (h n) -> p h n", h=HEADS)).then_inc(hsm_in, 16)
            sp.wait_ge(x_last_ready, 2 * CT)
            sp.dma_start(a["ssm_prompt"], x_last[:].rearrange("p r t -> p (r t)")).then_inc(stored, 16)
            sp.dma_start(hc[:], a["head_consts"][0]).then_inc(hc_in, 16)
            sp.dma_start(s0[:], a["s0"][0].rearrange("p (b v) -> p b v", b=DEC_BATCH)).then_inc(s0_in, 16)
            sp.wait_ge(xs_last_ready, 1)
            sp.dma_start(a["ssm_sample"], xs_last[:].rearrange("p r t b -> p (r t b)")).then_inc(stored, 16)

            def load_masks(h):
                sp.wait_ge(scm_ready, h)
                sp.dma_start(hc[:], a["head_consts"][h]).then_inc(hc_in, 16)

            def store_head(h):
                sp.wait_ge(sp_ready, h + 1)
                sp.dma_start(a["ret_prompt"][h], sp_out[:]).then_inc(head_stored, 16)
                sp.dma_start(a["ret_sample"][h], sn[:].rearrange("p b v -> p (b v)")).then_inc(head_stored, 16)
            with sp.Fori(0, HEADS - 1) as h:
                load_masks(h + 1)
                sp.wait_ge(sn_ready, h + 1)
                sp.dma_start(s0[:], a["s0"][h + 1].rearrange("p (b v) -> p b v", b=DEC_BATCH)).then_inc(s0_in, 16)
                store_head(h)
            sp.wait_ge(sn_ready, HEADS)
            store_head(HEADS - 1)
            with sp.Fori(1, 4) as i:
                load_unit(GLU, i, 0)
                load_unit(GLU, i, 1)
            load_plain(OUT)
            for phase in (UP[2], UP[3]):
                load_up(phase, 0)
                load_plain(DOWN[UP.index(phase)])
            with sp.Fori(0, DT // 2) as i:
                sp.wait_ge(y_even, i + 1)
                sp.dma_start(a["y"][2 * i].rearrange("p (h n) -> p h n", h=2), x[:, 2 * i]).then_inc(stored, 16)
                sp.wait_ge(y_odd, i + 1)
                sp.dma_start(a["y"][2 * i + 1].rearrange("p (h n) -> p h n", h=2), x[:, 2 * i + 1]).then_inc(stored, 16)
            sp.wait_ge(stored, 16 * (2 + DT))
            sp.wait_ge(head_stored, 16 * 2 * HEADS + 16)

        @block.gpsimd
        def _(pool):
            st = Steps(pool, pool_step)

            def tt(out, in0, in1, op, moving=False):
                if moving:
                    pool.sem_inc(pool_settled, 1)
                return pool.tensor_tensor(out, in0, in1, op)

            def split_lo(pair, s, k):
                pool.wait_ge(hi_ready[s], pair + 1)
                tt(w_lo[s][:, 0:k], w_raw[s][:, 0:k], w_hi[s][:, 0:k].bitcast(F32), ALU.subtract).then_inc(lo_ready[s], 1)

            def split_pairs(phase, start=0):
                first, n, k = phase
                with pool.Fori(start, n) as i:
                    split_lo(i + first, 0, k)
                    split_lo(i + first, 1, k)

            def norm_lo(j):
                for i in range(DT // 2):
                    pool.wait_ge(h_hi_ready[0], DT // 2 * j + i + 1)
                    tt(prompt(h_lo[:, 2 * i]), prompt(norm_out[:, 2 * i]), prompt(h_hi[:, 2 * i]).bitcast(F32), ALU.subtract)\
                        .then_inc(h_lo_ready[0], 1)

            def normed_phase(j, phase):
                split_lo(phase[0], 0, phase[2])
                split_lo(phase[0], 1, phase[2])
                norm_lo(j)
                split_pairs(phase, 1)

            pool.wait_ge(x_in, 16)
            for m in range(DT // 2, DT):
                ins = tt(norm_tmp[:, m], x[:, m], x[:, m], ALU.mult)
            st.step(ins)
            st.step(tt(sumsq[:], norm_tmp[:, DT - 1], norm_tmp[:, DT - 2], ALU.add))
            for m in range(DT - 3, -1, -1):
                if m < DT // 2:
                    pool.wait_ge(squares, DT // 2)
                st.step(tt(sumsq[:], sumsq[:], norm_tmp[:, m], ALU.add))
            pool.sem_inc(sumsq_ready, 1)
            normed_phase(0, UP[0])
            split_pairs(DOWN[0])
            split_pairs(UP[1])
            split_pairs(DOWN[1])
            normed_phase(1, PROJ_U)

            pool.sem_inc(xi_ready, 2)

            def segment(ct, j):
                gi, b = 4 * ct + j, j % 2
                er, ei = et[:, 0, bass.ds(4 * ct, 4), :], et[:, 1, bass.ds(4 * ct, 4), :]
                pa_, pb_ = view4(h32[0]), view4(h32[1])
                pool.wait_ge(z_ready, gi + 1)
                pool.wait_ge(y_ready, gi + 1)
                pool.wait_ge(xi_ready, gi + 2)
                st.mark(tt(pa_, z[b][:, 0], ei, ALU.mult, moving=True))
                st.step(tt(pb_, z[b][:, 1], er, ALU.mult))
                tt(xc[b][:, 1], pa_, pb_, ALU.add).then_inc(xi_ready, 1)

            def rotate(m, swapped, ct, rotated):
                pool.wait_ge(swapped, ct + 1)
                tile = proj[:, m]
                st.mark(tt(tile, tile, rope[0], ALU.mult, moving=True))
                st.step(tt(swap[:], swap[:], rope[1], ALU.mult))
                tt(tile, tile, swap[:], ALU.add, moving=True).then_inc(rotated, 1)

            def channel_tile(ct, k_next):
                qa = 2 * ct + PROJ_REST[0]
                split_lo(qa, 1, DT)
                segment(ct, 0)
                split_lo(qa + 1, 0, DT)
                rotate(4 * ct + 4, qsw_ready, ct, qrot_ready)
                segment(ct, 1)
                split_lo(qa + 1, 1, DT)
                rotate(4 * ct + 5, ksw_ready, ct, krot_ready)
                segment(ct, 2)
                split_lo(qa + 2, 0, k_next)
                segment(ct, 3)
                pool.wait_ge(xi_ready, 4 * ct + 4 + 2)
                pool.tensor_copy(x_last[:, 1, bass.ds(4 * ct, 4)], xc[1][:, 1, :, SEG - 1]).then_inc(x_last_ready, 1)

            split_lo(PROJ_REST[0], 0, DT)
            pool.wait_ge(rope_in, 32)
            with st.loop(0, CT - 1, 12) as ct:
                channel_tile(ct, DT)
            channel_tile(CT - 1, GLU[2])

            split_lo(GLU[0], 1, GLU[2])

            pool.sem_inc(r_lo_ready, 1)
            st.step(pool.memset(epsm[:, :, 0:1], EPS))
            st.step(pool.memset(epsm[:, :, 1:2], -0.5))
            pool.wait_ge(hsm_in, 16)

            def spread_v(h):
                pool.wait_ge(kt_ready, h + 1)
                if not (isinstance(h, int) and h == 0):
                    pool.wait_ge(snp_ready, h)
                tt(vm[0:NS], vt[0:NS, 4, :].unsqueeze(1).broadcast_to([NS, DEC_BATCH, DV]),
                   hsv(h, "bmask")[0:NS].unsqueeze(2).broadcast_to([NS, DEC_BATCH, DV]), ALU.mult, moving=True).then_inc(vm_ready, 1)

            def head(h, split_g=False, last=False):
                pool.wait_ge(mv_ready, h + 1)
                st.step(tt(hrstd[:], mv[:, :, 1:2], epsm[:, :, 0:1], ALU.add))
                tt(hrstd[:], hrstd[:], epsm[:, :, 1:2], ALU.pow).then_inc(hrstd_ready, 1)
                if not last:
                    spread_v(h + 1)
                pool.wait_ge(r_hi_ready, h + 1)
                tt(h_lo[:, h + 4], tmp[1][:], h_hi[:, h + 4].bitcast(F32), ALU.subtract, moving=True).then_inc(r_lo_ready, 1)
                if split_g:
                    for m in (2 * h, 2 * h + 1):
                        pool.wait_ge(g_hi_ready, m + 1)
                        for n, part in ((HP, prompt), (HS, sample)):
                            at = 0 if part is prompt else SEQ
                            ins = tt(part(h_lo[:, m]), proj[:, m, at:at + 2 * n].rearrange("p (h n) -> p h n", h=2),
                                     part(h_hi[:, m]).bitcast(F32), ALU.subtract, moving=True)
                        ins.then_inc(g_lo_ready, 1)
            spread_v(0)
            with st.loop(0, HEADS // 2, 1) as h:
                head(h, split_g=True)
            for h in range(HEADS // 2, HEADS):
                head(h, last=(h == HEADS - 1))
            split_pairs(GLU, 1)
            split_pairs(OUT)
            normed_phase(2, UP[2])
            split_pairs(DOWN[2])
            split_pairs(UP[3])
            split_pairs(DOWN[3])

        @block.scalar
        def _(act):
            st = Steps(act, act_step)

            def copy(out, in_, scale=1.0):
                return nc.scalar.activation(out, in_, ACT.Copy, scale=scale)

            def split_hi(pair, s, k, first_use=False):
                act.wait_ge(raw_in[s], 16 * pair + 16)
                if not first_use:
                    act.wait_ge(acc_ready[s], pair)
                copy(w_hi[s][:, 0:k], w_raw[s][:, 0:k]).then_inc(hi_ready[s], 1)

            def ada_split(b, u):
                act.wait_ge(*ada_arrival(b, u))
                if not (isinstance(b, int) and b < 4):
                    act.wait_ge(ada_used, 4 * b + (u - 1))
                elif b:
                    act.wait_ge(ada_used, 4 * b + (u - 3))
                copy(split_of(b, u)[0], raw_of(b, u)).then_inc(ada_hi_ready, 1)

            def ada_read(b):
                act.wait_ge(ada_used, 4 * b + 4)
                if not (isinstance(b, int) and b == 0):
                    act.wait_ge(ada_turned, b)
                copy(ada_row[0:2 * NC_], pa[0:2 * NC_, :]).then_inc(ada_row_hi, 1)

            act.wait_ge(prm_in, 16)
            copy(sel[:], prmv("sel")[0:64]).then_inc(sel_ready, 1)

            def clear_row(n):
                act.wait_ge(zeros_ready, n)
                copy(ada_row[0:64], view(tmp[1], ADA_N)[0:64]).then_inc(row_clear, 1)
                act.wait_ge(row_clear, n)
            clear_row(1)
            act_c = h32[0][:, 0, 0:DT * NC_]
            nc.scalar.activation(act_c, prmv("c"), ACT.Silu).then_inc(silu_c, 1)
            act.wait_ge(silu_c, 1)
            copy(c_split[:, :, 0:NC_], act_c.rearrange("p (t n) -> p t n", n=NC_)).then_inc(c_hi_ready, 1)
            lam = prmv("lam").rearrange("p (a t) -> p a t", a=3)

            def s5_step_sizes():
                nc.scalar.activation(s5t[:, 0], lam[:, 2], ACT.Exp).then_inc(s5_exp, 1)

            def s5_trig_values():
                act.wait_ge(s5_angle, 1)
                nc.scalar.activation(s5r[:], s5t[:, 1], ACT.Exp)
                nc.scalar.activation(s5pow[:, 1, 0], s5t[:, 2], ACT.Sin)
                nc.scalar.activation(s5pow[:, 0, 0], s5t[:, 3], ACT.Sin).then_inc(s5_trig, 1)

            def norm_root(j):
                if j == 0:
                    nc.scalar.activation(hrstd[:, 0], eps_t[:], ACT.Sqrt)
                act.wait_ge(ms_ready, j + 1)
                nc.scalar.activation(rms[:, 0:4], pn[:, 0, HALF:HALF + 4], ACT.Sqrt, bias=eps_t[:])
                nc.scalar.activation(rms[0:HS, 4:6], pn[0:HS, 0, HALF + 4:HALF + 6], ACT.Sqrt, bias=eps_t[0:HS]).then_inc(root_ready, 1)

            for b in range(4):
                if b == 3:
                    act.wait_ge(eps_ready, 1)
                    norm_root(0)
                for u in range(ADA_UNITS):
                    ada_split(b, u)
                    if u == 0 and b:
                        ada_read(b - 1)
                    if (b, u) == (0, 1):
                        s5_step_sizes()
                if b == 0:
                    s5_trig_values()
                if b == 1:
                    act.wait_ge(x_in, 16)
                    for m in range(DT // 2):
                        nc.scalar.activation(norm_tmp[:, m], x[:, m], ACT.Square).then_inc(squares, 1)
            split_hi(UP[0][0], 0, DT, first_use=True)
            split_hi(UP[0][0], 1, DT, first_use=True)
            ada_read(3)

            def odd_tile(m, out, in_):
                return nc.scalar.activation(prompt(out), prompt(in_), ACT.Identity, bias=mod[:, m[1], 0:1], scale=mod[:, m[0], 0:1])

            def norm_hi(j, sc, sh):
                for i in range(DT // 2):
                    done = DT // 2 * j + i + 1
                    even, odd = 2 * i, 2 * i + 1

                    def even_hi():
                        act.wait_ge(tile_ready[0], done)
                        copy(prompt(h_hi[:, even]), prompt(norm_out[:, even])).then_inc(h_hi_ready[0], 1)
                    if i == 0:
                        even_hi()
                        act.wait_ge(hs_ready, j + 1)
                        copy(h_hi[:, :, :, HP:HALF], hs32).then_inc(hs_hi_ready, 1)
                    act.wait_ge(scaled, 5 * j + i + 2)
                    odd_tile((odd + sc, odd + sh), norm_out[:, odd], norm_tmp[:, odd]).then_inc(tile_ready[1], 1)
                    if i:
                        even_hi()
                    act.wait_ge(tile_ready[1], done)
                    copy(prompt(h_hi[:, odd]), prompt(norm_out[:, odd])).then_inc(h_hi_ready[1], 1)

            def up(phase, block0, split=False, tmp_free=None, before_row=None):
                first = phase[0]

                def hidden(f, ada, first_use=False, k_next=DT, split=False):
                    pair = f + first
                    b = f + block0
                    if not split:
                        split_hi(pair, 1, DT)
                    if ada:
                        ada_split(b, 0)
                        ada_split(b, 1)
                    act.wait_ge(acc_ready[0], pair + 1)
                    if not first_use:
                        act.wait_ge(acc_free[1], pair)
                    if tmp_free and isinstance(f, int) and f == 0:
                        tmp_free()
                    nc.scalar.activation(tmp[0][:], acc[0][:, :, 0:HALF], ACT.Silu).then_inc(acc_free[0], 1)
                    split_hi(pair + 1, 0, k_next)
                    if ada:
                        ada_split(b, 2)
                        ada_split(b, 3)
                    act.wait_ge(acc_free[1], pair + 1)
                    copy(hid_hi[:, f], h32[0][:]).then_inc(hid_hi_ready, 1)
                    if ada:
                        if before_row and isinstance(f, int) and f == 0:
                            before_row()
                        ada_read(b)

                n_ada = 9 if block0 else 1
                hidden(0, bool(block0), first_use=(first == 0), split=split)
                if block0:
                    with act.Fori(1, n_ada) as f:
                        hidden(f, True)
                with act.Fori(n_ada, HT - 1) as f:
                    hidden(f, False)
                hidden(HT - 1, False, k_next=KMAX)

            def splits(phase, start=0):
                first, n, k = phase
                with act.Fori(start, n - 1) as i:
                    split_hi(i + first, 1, k)
                    split_hi(i + (first + 1), 0, k)
                split_hi(first + n - 1, 1, k)
                if first + n < PAIRS:
                    split_hi(first + n, 0, k_tiles(first + n))

            act.wait_ge(scale1_ready, 1)
            norm_hi(0, SC1, SH1)
            up(UP[0], 4, split=True)
            act.wait_ge(c_in, 16)
            st.step(nc.scalar.activation(lc[:, :, 1, :], lc[:, :, 1, :], ACT.Copy, scale=-1.0))
            splits(DOWN[0])
            act.wait_ge(bbar_turned, 1)
            copy(lb[:], pn[:].rearrange("p r (t n) -> p t r n", t=CT)).then_inc(lb_ready, 1)
            split_hi(UP[1][0], 1, DT)
            up(UP[1], 13, split=True, tmp_free=lambda: act.wait_ge(table_done, 1), before_row=lambda: clear_row(2))
            splits(DOWN[1])
            split_hi(PROJ_U[0], 1, DT)
            norm_root(1)
            norm_hi(1, SC2, SH2)

            def mixer_order(t):
                return (t[:, 0:SEQ].rearrange("p (h n) -> p h n", h=2), t[:, SEQ:TOK].rearrange("p (h n) -> p h n", h=2))

            def read_proj(pair, s, m, func=ACT.Copy):
                act.wait_ge(acc_ready[s], pair + 1)
                out_p, out_s = mixer_order(proj[:, m])
                nc.scalar.activation(out_p, prompt(acc[s]), func)
                return nc.scalar.activation(out_s, sample(acc[s]), func)

            def read_swapped(s):
                lower, upper = slice(0, P // 2), slice(P // 2, P)
                for to, from_ in ((lower, upper), (upper, lower)):
                    out_p, out_s = mixer_order(swap[to])
                    copy(out_p, prompt(acc[s][from_]))
                    ins = copy(out_s, sample(acc[s][from_]))
                return ins

            for i in range(PROJ_U[1]):
                pair = PROJ_U[0] + i
                if i:
                    split_hi(pair, 1, DT)
                read_proj(pair, 0, 2 * i).then_inc(acc_free[0], 1)
                split_hi(pair + 1, 0, DT)
                read_proj(pair, 1, 2 * i + 1).then_inc(acc_free[1], 1)

            act.sem_inc(bu_ready, 1)
            act.sem_inc(bus_ready, 1)
            act.wait_ge(lbs_clear, 1)
            for s in range(2):
                act.wait_ge(acc_free[s], PROJ_REST[0])
            act.wait_ge(lb_ready, 1)

            def stage(ct):
                for i in range(4):
                    r = slice(32 * i, 32 * i + 32)
                    ins = copy(lbs[r, :, i, :], lb[r, ct])
                ins.then_inc(staged, 1)

            def read_bu(ct, j):
                gi = 4 * ct + j
                act.wait_ge(b_done, gi + 1)
                act.wait_ge(bu_used, gi + 1)
                copy(bu[j % 2][:], pn[:].rearrange("p r (t n) -> p r t n", t=4)).then_inc(bu_ready, 1)

            def channel_tile(ct, k_next, first=False, last=False):
                qa = 2 * ct + PROJ_REST[0]
                read_bu(ct, 1)
                split_hi(qa, 1, DT)
                act.wait_ge(bs_done, ct + 1)
                copy(bus[:, :, bass.ds(4 * ct, 4), :],
                     pt[:, 0:2 * 4 * NS].rearrange("p (r t n) -> p r t n", r=2, t=4)).then_inc(bus_ready, 1)
                read_proj(qa, 0, 4 * ct + 4)
                if not first:
                    act.wait_ge(krot_ready, ct)
                read_swapped(0).then_inc(qsw_ready, 1)
                act.wait_ge(qsw_ready, ct + 1)
                act.sem_inc(acc_free[0], 1)
                read_bu(ct, 2)
                split_hi(qa + 1, 0, DT)
                if not first:
                    act.wait_ge(y_ready, 4 * ct + 2)
                copy(lcs[:], lc[:, bass.ds(4 * ct, 4)]).then_inc(lcs_staged, 1)
                read_proj(qa, 1, 4 * ct + 5)
                act.wait_ge(qrot_ready, ct + 1)
                read_swapped(1).then_inc(ksw_ready, 1)
                act.wait_ge(ksw_ready, ct + 1)
                act.sem_inc(acc_free[1], 1)
                read_bu(ct, 3)
                if not last:
                    stage(ct + 1)
                split_hi(qa + 1, 1, DT)
                read_proj(qa + 1, 0, 4 * ct + 6).then_inc(acc_free[0], 1)
                if not last:
                    read_bu(ct + 1, 0)
                split_hi(qa + 2, 0, k_next)
                read_proj(qa + 1, 1, 4 * ct + 7, ACT.Silu).then_inc(acc_free[1], 1)

            stage(0)
            read_bu(0, 0)
            channel_tile(0, DT, first=True)
            with act.Fori(1, CT - 1) as ct:
                channel_tile(ct, DT)
            channel_tile(CT - 1, GLU[2], last=True)
            split_hi(GLU[0], 1, GLU[2])

            act.wait_ge(krot_ready, CT)
            act.wait_ge(qrot_ready, CT)
            for s in range(2):
                act.wait_ge(acc_free[s], GLU[0])

            def copy_vk(h):
                if not (isinstance(h, int) and h == 0):
                    act.wait_ge(scores_ready, h)
                copy(vs, proj[:, 4 * h + 6]).then_inc(vs_ready, 1)
                copy(ks[:], proj[:, 4 * h + 5]).then_inc(ks_ready, 1)

            def read_vt(h):
                act.wait_ge(tv_ready, h + 1)
                copy(vt[:, 0:4], acc[1][:, 1].rearrange("p (t n) -> p t n", t=4)).then_inc(vt_ready, 1)

            def gelu(m):
                nc.scalar.activation(proj[:, m], proj[:, m], ACT.Gelu_apprx_tanh).then_inc(gelu_ready, 1)
                act.wait_ge(gelu_ready, m + 1)
                in_p, in_s = mixer_order(proj[:, m])
                copy(prompt(h_hi[:, m]), in_p)
                copy(sample(h_hi[:, m]), in_s).then_inc(g_hi_ready, 1)

            def head(h, vt_next=True, vk_next=True):
                if vt_next:
                    read_vt(h + 1)
                if vk_next:
                    copy_vk(h + 2)
                act.wait_ge(m32_ready, h + 2)
                copy(h_hi[:, h + 4], tmp[1][:]).then_inc(r_hi_ready, 1)
                if vk_next:
                    act.wait_ge(y_all, 1)
                    gelu(2 * h)
                    gelu(2 * h + 1)

            copy_vk(0)
            read_vt(0)
            copy_vk(1)
            with act.Fori(0, HEADS - 2) as h:
                head(h)
            head(HEADS - 2, vk_next=False)
            head(HEADS - 1, vt_next=False, vk_next=False)

            def glu_tile(i, k_next):
                pair = i + GLU[0]
                if not (isinstance(i, int) and i == 0):
                    split_hi(pair, 1, GLU[2])
                act.wait_ge(acc_ready[0], pair + 1)
                act.wait_ge(acc_free[1], pair)
                nc.scalar.activation(tmp[0][:], acc[0][:, :, 0:HALF], ACT.Sigmoid).then_inc(acc_free[0], 1)
                split_hi(pair + 1, 0, k_next)
                act.wait_ge(acc_free[1], pair + 1)
                copy(glu_hi[:, i], h32[0][:]).then_inc(m_hi_ready, 1)

            glu_tile(0, GLU[2])
            with act.Fori(1, GLU[1] - 1) as i:
                glu_tile(i, GLU[2])
            glu_tile(GLU[1] - 1, OUT[2])
            split_hi(OUT[0], 1, OUT[2])
            with act.Fori(1, OUT[1]) as i:
                split_hi(i + OUT[0], 0, DT)
                split_hi(i + OUT[0], 1, DT)
            split_hi(UP[2][0], 0, DT)
            split_hi(UP[2][0], 1, DT)
            norm_root(2)
            norm_hi(2, SC3, SH3)
            up(UP[2], 0, split=True)
            splits(DOWN[2])
            up(UP[3], 0)
            splits(DOWN[3])
            norm_root(3)
            for i in range(DT // 2):
                odd = 2 * i + 1
                act.wait_ge(scaled, 5 * 3 + i + 2)
                odd_tile((odd + SCF, odd + SHF), x[:, odd], norm_tmp[:, odd]).then_inc(y_odd, 1)

        @block.vector
        def _(dve):
            st = Steps(dve, dve_step)
            v = nc.vector
            tt = v.tensor_tensor

            def ada_lo_split(b, u):
                dve.wait_ge(ada_hi_ready, 4 * b + (u + 1))
                hi, lo = split_of(b, u)
                tt(lo, raw_of(b, u), hi.bitcast(F32), ALU.subtract).then_inc(ada_lo_ready, 1)

            def row_lo(b):
                dve.wait_ge(ada_row_hi, b + 1)
                tt(ada_row[32:32 + 2 * NC_], pa[0:2 * NC_, :], ada_row[0:2 * NC_].bitcast(F32), ALU.subtract).then_inc(ada_row_ready, 1)

            def read_mod(b):
                dve.wait_ge(ada_turned, b + 1)
                tt(mod[:, bass.ds(4 * b, 4), :], pt[:, 0:4 * SEL_N].rearrange("p (t n) -> p t n", n=SEL_N)[:, :, 0:NC_],
                   prmv("bias")[:, bass.ds(4 * b, 4)].unsqueeze(2).broadcast_to([P, 4, NC_]), ALU.add).then_inc(mod_ready, 1)

            def scale_mod(j, sc, blocks):
                dve.wait_ge(mod_ready, blocks)
                gain = prmv("gain")[:, DT * j:DT * j + DT].unsqueeze(2).broadcast_to([P, DT, NC_])
                st.step(v.scalar_tensor_tensor(out=mod[:, sc:sc + DT, :], in0=mod[:, sc:sc + DT, :], scalar=1.0, in1=gain,
                                               op0=ALU.add, op1=ALU.mult))

            def halve_gate(g_, blocks):
                dve.wait_ge(mod_ready, blocks)
                st.step(v.tensor_scalar(mod[:, g_:g_ + DT, :], mod[:, g_:g_ + DT, :], 0.5, None, ALU.mult))

            def norm_rstd(j):
                dve.wait_ge(root_ready, j + 1)
                st.mark(v.reciprocal(rms[:, 0:4], rms[:, 0:4]))
                st.step(v.reciprocal(rms[0:HS, 4:6], rms[0:HS, 4:6]))
                ident = prmv("ident")
                v.scalar_tensor_tensor(out=view4(tmp[0]), in0=rms[:, 0:4].unsqueeze(2).broadcast_to([P, 4, P]), scalar=float(D_MODEL),
                                       in1=ident.unsqueeze(1).broadcast_to([P, 4, P]), op0=ALU.mult, op1=ALU.mult)
                v.scalar_tensor_tensor(out=tmp[1][0:HS, :, 0:HS], in0=rms[0:HS, 4:6].unsqueeze(2).broadcast_to([HS, 2, HS]),
                                       scalar=float(D_MODEL), in1=ident[0:HS, 0:HS].unsqueeze(1).broadcast_to([HS, 2, HS]),
                                       op0=ALU.mult, op1=ALU.mult).then_inc(diag_ready, 1)
                dve.wait_ge(rstd_ready, j + 1)

            def norm_samples(sc, sh):
                rs = pn[:, :, HP:HALF].unsqueeze(1).broadcast_to([P, DT, HALVES, HS])
                st.step(tt(hs32, x[:, :, :, HP:HALF], rs, ALU.mult))
                by_seq = hs32.rearrange("p t h (b s) -> p t (h b) s", s=DEC_SEQ)
                scale, shift = (mod[:, n:n + DT, 1:NC_].unsqueeze(3).broadcast_to([P, DT, DEC_BATCH, DEC_SEQ]) for n in (sc, sh))
                st.step(tt(by_seq, by_seq, scale, ALU.mult))
                return tt(by_seq, by_seq, shift, ALU.add)

            steps = ((0,), (1,), (2, 3), (4, 5), (6, 7))

            def scaled_tiles(tiles):
                lo, n = tiles[0], len(tiles)
                tt(norm_tmp[:, lo:lo + n, :, 0:HP], x[:, lo:lo + n, :, 0:HP],
                   pn[:, :, 0:HP].unsqueeze(1).broadcast_to([P, n, HALVES, HP]), ALU.mult).then_inc(scaled, 1)

            def even_tile(j, m, out, sc, sh):
                dve.wait_ge(scaled, 5 * j + (1, 3, 4, 5)[m // 2])
                return v.tensor_scalar(prompt(out), prompt(norm_tmp[:, m]), mod[:, m + sc, 0:1], mod[:, m + sh, 0:1], ALU.mult, ALU.add)

            def norm(j, sc, sh, scaled_before=0):
                if not scaled_before:
                    norm_rstd(j)

                def odd_lo(m):
                    dve.wait_ge(h_hi_ready[1], DT // 2 * j + m // 2 + 1)
                    tt(prompt(h_lo[:, m]), prompt(norm_out[:, m]), prompt(h_hi[:, m]).bitcast(F32), ALU.subtract)\
                        .then_inc(h_lo_ready[1], 1)

                for n, tiles in enumerate(steps):
                    if n >= scaled_before:
                        scaled_tiles(tiles)
                    m = tiles[0]
                    if m % 2 == 0:
                        even_tile(j, m, norm_out[:, m], sc, sh).then_inc(tile_ready[0], 1)
                        if m:
                            odd_lo(m - 1)
                        else:
                            norm_samples(sc, sh).then_inc(hs_ready, 1)
                    else:
                        dve.wait_ge(hs_hi_ready, j + 1)
                        tt(h_lo[:, :, :, HP:HALF], hs32, h_hi[:, :, :, HP:HALF].bitcast(F32), ALU.subtract).then_inc(hs_lo_ready, 1)
                odd_lo(DT - 1)

            def up(phase, block0, between=None):
                first = phase[0]

                def hidden(f, ada, turned=None):
                    pair = f + first
                    b = f + block0
                    if ada:
                        if not (isinstance(f, int) and f == 0):
                            row_lo(b - 1)
                        ada_lo_split(b, 0)
                        ada_lo_split(b, 1)
                        if not (isinstance(f, int) and f == 0):
                            read_mod(b - 1)
                        ada_lo_split(b, 2)
                        ada_lo_split(b, 3)
                    if turned is not None:
                        row_lo(turned)
                        read_mod(turned)
                    dve.wait_ge(acc_free[0], pair + 1)
                    dve.wait_ge(acc_ready[1], pair + 1)
                    if not (isinstance(f, int) and f == 0):
                        dve.wait_ge(hid_lo_ready, f + HT * UP.index(phase))
                    tt(h32[0][:], tmp[0][:], acc[1][:, :, 0:HALF], ALU.mult).then_inc(acc_free[1], 1)
                    dve.wait_ge(acc_free[1], pair + 1)
                    dve.wait_ge(hid_hi_ready, f + (HT * UP.index(phase) + 1))
                    tt(hid_lo[:, f], h32[0][:], hid_hi[:, f].bitcast(F32), ALU.subtract).then_inc(hid_lo_ready, 1)

                if block0:
                    hidden(0, True)
                    with dve.Fori(1, 9) as f:
                        hidden(f, True)
                    if between:
                        between[0]()
                    hidden(9, False, turned=block0 + 8)
                    if between:
                        between[1]()
                    hidden(10, False)
                else:
                    with dve.Fori(0, HT) as f:
                        hidden(f, False)

            def residual(pair, s, m, gate_, square):
                dve.wait_ge(acc_ready[s], pair + 1)
                st.mark(v.scalar_tensor_tensor(out=prompt(x[:, m]), in0=prompt(acc[s]), scalar=mod[:, m + gate_, 0:1],
                                               in1=prompt(x[:, m]), op0=ALU.mult, op1=ALU.add))
                tt(gs[s][:].rearrange("p h (b s) -> p h b s", s=DEC_SEQ), sample4(acc[s]),
                   per_seq(mod[:, m + gate_, 1:NC_]), ALU.mult).then_inc(acc_free[s], 1)
                dve.wait_ge(acc_free[s], pair + 1)
                st.step(tt(sample(x[:, m]), sample(x[:, m]), gs[s][:], ALU.add))
                if square:
                    st.step(tt(tmp[s][:], x[:, m], x[:, m], ALU.mult))
                    st.step(tt(sumsq[:], sumsq[:], tmp[s][:], ALU.add))

            def residuals(phase, gate_, square, extra=None, extra_steps=0):
                if square:
                    st.step(v.memset(sumsq[:], 0.0))
                with st.loop(0, phase[1], (8 if square else 4) + extra_steps) as i:
                    for s in range(2):
                        residual(i + phase[0], s, 2 * i + s, gate_, square)
                        if extra and s == 0:
                            extra(i)
                if square:
                    dve.sem_inc(sumsq_ready, 1)

            v.memset(eps_t[:], EPS).then_inc(eps_ready, 1)
            v.memset(view(tmp[1], ADA_N), 0.0).then_inc(zeros_ready, 1)
            dve.wait_ge(c_hi_ready, 1)
            tt(c_split[:, :, NC_:2 * NC_], h32[0][:, 0, 0:DT * NC_].rearrange("p (t n) -> p t n", n=NC_),
               c_split[:, :, 0:NC_].bitcast(F32), ALU.subtract).then_inc(c_ready, 1)
            ada_lo_split(0, 0)
            ada_lo_split(0, 1)
            lam = prmv("lam").rearrange("p (a t) -> p a t", a=3)
            dve.wait_ge(s5_exp, 1)
            st.mark(tt(s5t[:, 1], lam[:, 0], s5t[:, 0], ALU.mult))
            st.step(tt(s5t[:, 2], lam[:, 1], s5t[:, 0], ALU.mult))
            magic = 1.5 * 2.0 ** 23
            st.step(v.tensor_scalar(s5t[:, 4], s5t[:, 2], float(1 / (2 * np.pi)), magic, ALU.mult, ALU.add))
            st.step(v.tensor_scalar(s5t[:, 4], s5t[:, 4], magic, None, ALU.subtract))
            for part in TWO_PI:
                st.step(v.scalar_tensor_tensor(out=s5t[:, 2], in0=s5t[:, 4], scalar=-part, in1=s5t[:, 2],
                                               op0=ALU.mult, op1=ALU.add))
            st.step(v.tensor_scalar(s5t[:, 2], s5t[:, 2], PI_LOW, -PI_LOW, ALU.min, ALU.max))
            st.step(v.tensor_scalar(s5t[:, 5], s5t[:, 2], -1.0, None, ALU.mult))
            st.step(tt(s5t[:, 3], s5t[:, 2], s5t[:, 5], ALU.max))
            v.tensor_scalar(s5t[:, 3], s5t[:, 3], -1.0, float(np.pi / 2), ALU.mult, ALU.add).then_inc(s5_angle, 1)
            ada_lo_split(0, 2)
            ada_lo_split(0, 3)
            for b in range(1, 4):
                if b == 3:
                    norm_rstd(0)
                for u in range(ADA_UNITS):
                    ada_lo_split(b, u)
                    if u == 0:
                        row_lo(b - 1)
                read_mod(b - 1)
            for tiles in steps[:2]:
                scaled_tiles(tiles)
            row_lo(3)
            read_mod(3)
            scale_mod(0, SC1, 4)
            dve.sem_inc(scale1_ready, 1)

            pr, pi = s5pow[:, 0], s5pow[:, 1]
            t0, t1, t2, t3 = (s5t[:, n] for n in (4, 5, 6, 7))

            def unit_length(k):
                st.mark(tt(t0, pr[:, k], pr[:, k], ALU.mult))
                st.step(tt(t1, pi[:, k], pi[:, k], ALU.mult))
                st.step(tt(t0, t0, t1, ALU.add))
                st.step(v.tensor_scalar(t0, t0, -0.5, 1.5, ALU.mult, ALU.add))
                st.mark(tt(pr[:, k], pr[:, k], t0, ALU.mult))
                st.step(tt(pi[:, k], pi[:, k], t0, ALU.mult))

            def powers(ks_):
                dve.wait_ge(s5_trig, 1)
                for k in ks_:
                    if k:
                        st.mark(tt(t0, pr[:, k - 1], pr[:, k - 1], ALU.mult))
                        st.mark(tt(t1, pi[:, k - 1], pi[:, k - 1], ALU.mult))
                        st.step(tt(t2, pr[:, k - 1], pi[:, k - 1], ALU.mult))
                        st.mark(tt(pr[:, k], t0, t1, ALU.subtract))
                        st.step(v.tensor_scalar(pi[:, k], t2, 2.0, None, ALU.mult))
                    unit_length(k)

            norm(0, SC1, SH1, scaled_before=2)
            up(UP[0], 4, between=(lambda: powers(range(3)), lambda: powers(range(3, 8))))
            halve_gate(G1, 13)

            st.mark(tt(s5lam[:, 0], s5r[:], pr[:, 0], ALU.mult))
            st.step(tt(s5lam[:, 1], s5r[:], pi[:, 0], ALU.mult))
            st.mark(tt(t0, lam[:, 0], lam[:, 0], ALU.mult))
            st.mark(tt(t1, lam[:, 1], lam[:, 1], ALU.mult))
            st.step(v.tensor_scalar(t2, s5lam[:, 0], 1.0, None, ALU.subtract))
            st.step(tt(t0, t0, t1, ALU.add))
            st.step(v.reciprocal(t3, t0))
            st.mark(tt(t0, t2, lam[:, 0], ALU.mult))
            st.step(tt(t1, s5lam[:, 1], lam[:, 1], ALU.mult))
            st.step(tt(t0, t0, t1, ALU.add))
            st.step(tt(s5beta[:, 0], t0, t3, ALU.mult))
            st.mark(tt(t0, s5lam[:, 1], lam[:, 0], ALU.mult))
            st.step(tt(t1, t2, lam[:, 1], ALU.mult))
            st.step(tt(t0, t0, t1, ALU.subtract))
            st.step(tt(s5beta[:, 1], t0, t3, ALU.mult))
            dve.wait_ge(b_in, 32)

            def by_tile(t):
                return flat(t)[:, 0:NT * 32].rearrange("p (t c) -> p t c", t=NT)
            br, bi = by_tile(tmp[0]), by_tile(tmp[1])
            beta_r, beta_i = (s5beta[:, n].unsqueeze(2).broadcast_to([P, NT, 32]) for n in range(2))
            st.mark(tt(by_tile(h32[0]), br, beta_r, ALU.mult))
            st.step(tt(by_tile(root), bi, beta_i, ALU.mult))
            st.mark(tt(by_tile(h32[0]), by_tile(h32[0]), by_tile(root), ALU.subtract))
            st.mark(tt(by_tile(h32[1]), br, beta_i, ALU.mult))
            st.step(tt(by_tile(sumsq), bi, beta_r, ALU.mult))
            tt(by_tile(h32[1]), by_tile(h32[1]), by_tile(sumsq), ALU.add).then_inc(bbar_ready, 1)
            st.mark(v.memset(et[:, 0, :, 0:1], 1.0))
            st.step(v.memset(et[:, 1, :, 0:1], 0.0))

            def table(i):
                for k in range(7):
                    n = 2 ** k
                    er, ei = (et[:, r, bass.ds(4 * i, 4), 0:n] for r in range(2))
                    o_r, o_i = (et[:, r, bass.ds(4 * i, 4), n:2 * n] for r in range(2))
                    qr, qi = (s5pow[:, r, k, bass.ds(4 * i, 4)].unsqueeze(2).broadcast_to([P, 4, n]) for r in range(2))
                    u0, u1, u2, u3 = (view4(t)[:, :, 0:n] for t in (tmp[0], tmp[1], root, sumsq))
                    st.mark(tt(u0, er, qr, ALU.mult))
                    st.mark(tt(u1, ei, qi, ALU.mult))
                    st.mark(tt(u2, er, qi, ALU.mult))
                    st.step(tt(u3, ei, qr, ALU.mult))
                    st.mark(tt(o_r, u0, u1, ALU.subtract))
                    st.step(tt(o_i, u2, u3, ALU.add))

            residuals(DOWN[0], G1, False, extra=table, extra_steps=42)
            dve.sem_inc(table_done, 1)
            dve.wait_ge(bbar_turned, 1)
            v.memset(view(tmp[1], ADA_N), 0.0).then_inc(zeros_ready, 1)
            up(UP[1], 13)
            halve_gate(G3, 22)
            scale_mod(1, SC2, 22)
            scale_mod(2, SC3, 22)
            scale_mod(3, SCF, 22)
            residuals(DOWN[1], G1, True)
            norm(1, SC2, SH2)

            v.memset(lbs[:], 0.0).then_inc(lbs_clear, 1)
            dve.sem_inc(bu_used, 2)
            dve.sem_inc(y_used, 1)

            def read_y(ct, j):
                gi = 4 * ct + j
                dve.wait_ge(y_ready, gi + 3)
                v.scalar_tensor_tensor(out=proj[:, ct, SEG * j:SEG * (j + 1)], in0=proj[:, ct, SEG * j:SEG * (j + 1)],
                                       scalar=prm[:, bass.ds(ct + PRM["skip"][0], 1)], in1=pa[:, 0:SEG],
                                       op0=ALU.mult, op1=ALU.add).then_inc(y_used, 1)

            def segment(ct, j):
                gi, b = 4 * ct + j, j % 2
                er, ei = et[:, 0, bass.ds(4 * ct, 4), :], et[:, 1, bass.ds(4 * ct, 4), :]
                u0, u1 = view4(tmp[0]), view4(tmp[1])
                dve.wait_ge(bu_ready, gi + 2)
                dve.wait_ge(xi_ready, gi + 1)
                bur, bui = bu[b][:, 0], bu[b][:, 1]
                st.mark(tt(u0, bur, er, ALU.mult))
                st.step(tt(u1, bui, ei, ALU.mult))
                st.step(tt(z[b][:, 0], u0, u1, ALU.add))
                st.mark(tt(u0, bui, er, ALU.mult))
                tt(u1, bur, ei, ALU.mult).then_inc(bu_used, 1)
                dve.wait_ge(bu_used, gi + 3)
                st.step(tt(z[b][:, 1], u0, u1, ALU.subtract))
                for r in range(2):
                    for t in range(4):
                        first = 0.0 if j == 0 else carry[:, r, t:t + 1]
                        ins = v.tensor_tensor_scan(z[b][:, r, t], s5r[:, bass.ds(4 * ct + t, 1)].broadcast_to([P, SEG]),
                                                   z[b][:, r, t], first, ALU.mult, ALU.add)
                ins.then_inc(z_ready, 1)
                dve.wait_ge(z_ready, gi + 1)
                st.mark(tt(u0, z[b][:, 0], er, ALU.mult))
                st.step(tt(u1, z[b][:, 1], ei, ALU.mult))
                dve.wait_ge(y_ready, gi + 1)
                tt(xc[b][:, 0], u0, u1, ALU.subtract).then_inc(xr_ready, 1)
                if j < 3:
                    qr, qi = (s5pow[:, r, 7, bass.ds(4 * ct, 4)] for r in range(2))
                    zr, zi = z[b][:, 0, :, SEG - 1], z[b][:, 1, :, SEG - 1]
                    st.mark(tt(ct4[:, 0], zr, qr, ALU.mult))
                    st.mark(tt(ct4[:, 1], zi, qi, ALU.mult))
                    st.mark(tt(ct4[:, 2], zr, qi, ALU.mult))
                    st.step(tt(ct4[:, 3], zi, qr, ALU.mult))
                    st.mark(tt(carry[:, 0], ct4[:, 0], ct4[:, 1], ALU.subtract))
                    st.step(tt(carry[:, 1], ct4[:, 2], ct4[:, 3], ALU.add))
                else:
                    dve.wait_ge(xr_ready, gi + 1)
                    v.tensor_copy(x_last[:, 0, bass.ds(4 * ct, 4)], xc[1][:, 0, :, SEG - 1]).then_inc(x_last_ready, 1)
                if j >= 2:
                    read_y(ct, j - 2)
                elif not (isinstance(ct, int) and ct == 0):
                    read_y(ct - 1, j + 2)

            def channel_tile(ct):
                for j in range(4):
                    segment(ct, j)

            channel_tile(0)
            with st.loop(1, CT, 4 * 7 + 3 * 6) as ct:
                channel_tile(ct)
            read_y(CT - 1, 2)
            read_y(CT - 1, 3)

            st.step(v.memset(mv[:], 1.0))
            dve.sem_inc(m32_ready, 1)
            dve.sem_inc(head_stored, 16)
            dve.wait_ge(hsm_in, 16)
            dve.wait_ge(qrot_ready, CT)
            dve.wait_ge(krot_ready, CT)

            def operands(h):
                dve.wait_ge(hc_in, 16 * h + 16)
                if not (isinstance(h, int) and h == 0):
                    dve.wait_ge(o_ready, h)
                tt(qm[:], proj[:, 4 * h + 4, SEQ:TOK].unsqueeze(1).broadcast_to([P, DEC_BATCH, NS]),
                   hcv("qmask").rearrange("p (b n) -> p b n", b=DEC_BATCH), ALU.mult).then_inc(qm_ready, 1)
                dve.wait_ge(tk_ready, h + 1)
                tt(kt[:, 0:4], pn[:, 0].rearrange("p (t n) -> p t n", t=4),
                   hsv(h, "kdec")[:, 0:4].unsqueeze(2).broadcast_to([P, 4, DK]), ALU.mult)
                v.tensor_scalar(kt[0:NS, 4], pn[0:NS, 1, 0:DK], hsv(h, "kdec")[0:NS, 4:5], None, ALU.mult)
                v.tensor_copy(vt[0:NS, 4], pn[0:NS, 1, DK:DK + DV]).then_inc(kt_ready, 1)
                dve.wait_ge(scores_ready, h + 1)
                at = 0
                for t in range(4):
                    n = SEQ - P * t
                    tt(sc[:, at:at + n], scores_at(t), hcv("mask")[:, 0:n], ALU.mult)
                    at += n
                tt(scs[:], acc[1][0:NS, 0, 2 * P:2 * P + NS], hsv(h, "smask")[0:NS], ALU.mult).then_inc(scm_ready, 1)

            def head_normed(h):
                dve.wait_ge(spp_ready, h + 1)
                dve.wait_ge(head_stored, 32 * h + 16)
                v.tensor_copy(sp_out[:], pn[:, 0, 0:DV]).then_inc(sp_ready, 1)
                dve.wait_ge(o_ready, h + 1)
                for t in range(5):
                    rows = P if t < 4 else NS
                    src = pt[:, DV * t:DV * t + DV] if t < 4 else pa[0:NS, 0:DV]
                    ins = v.bn_stats(stat[0:rows, t], src)
                st.step(ins)
                dve.sem_inc(dve_settled, 1)
                for t in range(4):
                    v.bn_aggr(mv[:, t], stat[:, t])
                v.bn_aggr(mv[0:NS, 4], stat[0:NS, 4]).then_inc(mv_ready, 1)
                dve.wait_ge(snp_ready, h + 1)
                v.scalar_tensor_tensor(out=sn[:].rearrange("p (c b) v -> p c (b v)", c=2),
                                       in0=s0[:].rearrange("p (c b) v -> p c (b v)", c=2), scalar=hsv(h, "g4"), in1=acc[0][:],
                                       op0=ALU.mult, op1=ALU.add).then_inc(sn_ready, 1)
                dve.wait_ge(hrstd_ready, h + 1)
                for t in range(5):
                    rows = P if t < 4 else NS
                    src = pt[:, DV * t:DV * t + DV] if t < 4 else pa[0:NS, 0:DV]
                    ins = v.tensor_scalar(on[0:rows, t], src, mv[0:rows, t, 0:1], hrstd[0:rows, t], ALU.subtract, ALU.mult)
                ins.then_inc(on_ready, 1)

            def gated(h):
                dve.wait_ge(ot_ready, h + 1)
                dve.wait_ge(r_lo_ready, h + 1)
                tt(prompt(tmp[1]), pt[:].rearrange("p (h n) -> p h n", h=2),
                   proj[:, 4 * h + 7, 0:SEQ].rearrange("p (h n) -> p h n", h=2), ALU.mult)
                tt(sample(tmp[1]), pn[:, 1, 2 * P:2 * P + NS].rearrange("p (h n) -> p h n", h=2),
                   proj[:, 4 * h + 7, SEQ:TOK].rearrange("p (h n) -> p h n", h=2), ALU.mult).then_inc(m32_ready, 1)

            operands(0)
            dve.wait_ge(h0_in, 16)
            dve.wait_ge(bus_ready, CT + 1)
            bus5 = bus[:].rearrange("p r t (b s) -> p r t b s", s=DEC_SEQ)
            w = [view(t, NT * DEC_BATCH).rearrange("p (t b) -> p t b", t=NT) for t in (tmp[0], tmp[1], h32[0], h32[1])]
            lr, li = (s5lam[:, r].unsqueeze(2).broadcast_to([P, NT, DEC_BATCH]) for r in range(2))
            for s in range(DEC_SEQ):
                qr, qi = (h0[:, r] if s == 0 else xs[:, r, :, :, s - 1] for r in range(2))
                st.mark(tt(w[0], qr, lr, ALU.mult))
                st.mark(tt(w[1], qi, li, ALU.mult))
                st.mark(tt(w[2], qr, li, ALU.mult))
                st.step(tt(w[3], qi, lr, ALU.mult))
                st.mark(tt(w[0], w[0], w[1], ALU.subtract))
                st.step(tt(w[2], w[2], w[3], ALU.add))
                st.mark(tt(xs[:, 0, :, :, s], w[0], bus5[:, 0, :, :, s], ALU.add))
                st.step(tt(xs[:, 1, :, :, s], w[2], bus5[:, 1, :, :, s], ALU.add))
            dve.sem_inc(xs_ready, 1)
            v.tensor_copy(xs_last[:], xs[:, :, :, :, DEC_SEQ - 1]).then_inc(xs_last_ready, 1)
            skip = prmv("skip").unsqueeze(2).broadcast_to([P, CT, NS])
            u_s = proj[:, 0:CT, SEQ:TOK]
            st.step(tt(u_s, u_s, skip, ALU.mult))
            head_normed(0)
            operands(1)
            gated(0)
            dve.wait_ge(ys_ready, 1)
            st.step(tt(u_s, u_s, pa[:, 0:CT * NS].rearrange("p (t n) -> p t n", t=CT), ALU.add))
            dve.wait_ge(y_used, 17)
            dve.sem_inc(y_all, 1)
            with st.loop(1, HEADS - 1, 1) as h:
                head_normed(h)
                operands(h + 1)
                gated(h)
            head_normed(HEADS - 1)
            gated(HEADS - 1)

            def glu_tile(i, first=False):
                pair = i + GLU[0]
                if not first:
                    dve.wait_ge(m_lo_ready, i)
                dve.wait_ge(acc_free[0], pair + 1)
                dve.wait_ge(acc_ready[1], pair + 1)
                tt(h32[0][:], tmp[0][:], acc[1][:, :, 0:HALF], ALU.mult).then_inc(acc_free[1], 1)
                dve.wait_ge(acc_free[1], pair + 1)
                dve.wait_ge(m_hi_ready, i + 1)
                tt(glu_lo[:, i], h32[0][:], glu_hi[:, i].bitcast(F32), ALU.subtract).then_inc(m_lo_ready, 1)

            glu_tile(0, first=True)
            with dve.Fori(1, GLU[1]) as i:
                glu_tile(i)
            residuals(OUT, G2, True)
            norm(2, SC3, SH3)
            up(UP[2], 0)
            residuals(DOWN[2], G3, False)
            up(UP[3], 0)
            residuals(DOWN[3], G3, True)
            norm_rstd(3)
            st.step(norm_samples(SCF, SHF))
            st.step(v.tensor_copy(x[:, :, :, HP:HALF], hs32))

            for tiles in steps:
                scaled_tiles(tiles)
                m = tiles[0]
                if m % 2 == 0:
                    even_tile(3, m, x[:, m], SCF, SHF).then_inc(y_even, 1)

        @block.tensor
        def _(pe):
            mm = nc.tensor.matmul

            def unit_of(pair, s, tiles, rhs, first_use=False, ready=None):
                pe.wait_ge(hi_ready[s], pair + 1)
                if not first_use:
                    pe.wait_ge(acc_free[s], pair)
                for n, t in enumerate(tiles):
                    if ready:
                        ready(t)
                    for part in range(2):
                        for c in range(2):
                            mm(acc[s][:, c, 0:HALF], w_hi[s][:, t], rhs(t)[part][:, c], start=(n == 0 and part == 0), stop=False)
                pe.wait_ge(lo_ready[s], pair + 1)
                for n, t in enumerate(tiles):
                    for c in range(2):
                        ins = mm(acc[s][:, c, 0:HALF], w_lo[s][:, t], rhs(t)[0][:, c], start=False, stop=(n == len(tiles) - 1))
                ins.then_inc(acc_ready[s], 1)

            def both_units(pair, k, ready, first_use=False):
                for s in range(2):
                    pe.wait_ge(hi_ready[s], pair + 1)
                    pe.wait_ge(lo_ready[s], pair + 1)
                    if not first_use:
                        pe.wait_ge(acc_free[s], pair)
                for t in range(k):
                    ready(t)
                    for s in range(2):
                        for n, (w, r) in enumerate(((w_hi[s], h_hi), (w_hi[s], h_lo), (w_lo[s], h_hi))):
                            for c in range(2):
                                ins = mm(acc[s][:, c, 0:HALF], w[:, t], r[:, t, c], start=(t == 0 and n == 0),
                                         stop=(t == k - 1 and n == 2))
                        if t == k - 1:
                            ins.then_inc(acc_ready[s], 1)

            def unit(pair, s, k, r_hi, r_lo, first_use=False, ready=None):
                unit_of(pair, s, range(k), lambda t: (r_hi[:, t], r_lo[:, t]), first_use, ready)

            def ada_unit(b, u):
                pe.wait_ge(ada_lo_ready, 4 * b + (u + 1))
                if u == 0 and not (isinstance(b, int) and b == 0):
                    pe.wait_ge(ada_row_ready, b)
                for part, w in enumerate(split_of(b, u)):
                    for k in range(2):
                        ins = mm(pa[0:2 * NC_, :], c_split[:, 2 * u + k], w[:, k],
                                 start=(u == 0 and part == 0 and k == 0), stop=(u == 3 and part == 1 and k == 1))
                ins.then_inc(ada_used, 1)

            def ada_turn(b):
                pe.wait_ge(ada_row_ready, b + 1)
                if not (isinstance(b, int) and b == 0):
                    pe.wait_ge(mod_ready, b)
                for t in range(4):
                    ins = mm(pt[:, SEL_N * t:SEL_N * (t + 1)], ada_row[0:64, P * t:P * (t + 1)], sel[:],
                             start=True, stop=True)
                ins.then_inc(ada_turned, 1)

            def normed(j):
                def ready(t):
                    if t == 0:
                        pe.wait_ge(hs_lo_ready, j + 1)
                    pe.wait_ge(h_lo_ready[t % 2], 4 * j + t // 2 + 1)
                return ready

            def counted(sem_, base):
                return lambda t: pe.wait_ge(sem_, base + t + 1)

            def keep_warm(n):
                c = c_split[:].rearrange("p t n -> p (t n)")
                for _ in range(n):
                    mm(pt[:, 0:DT * 2 * NC_], c[:, 0:P], c, start=True, stop=True)

            def mean_square(j):
                if j:
                    keep_warm(40)
                pe.wait_ge(sumsq_ready, j + 1)
                for h in range(HALVES):
                    for c in range(3):
                        cols = slice(P * c, min(P * (c + 1), HALF))
                        rows, at = (P, 2 * h + c) if c < 2 else (HS, 4 + h)
                        ins = mm(pn[0:rows, 0, HALF + at:HALF + at + 1], sumsq[:, h, cols], prmv("mean")[:, 0:1],
                                 start=True, stop=True)
                ins.then_inc(ms_ready, 1)
                if j:
                    keep_warm(20)
                pe.wait_ge(diag_ready, j + 1)
                for h in range(HALVES):
                    mm(pn[:, h, 0:HP], prmv("mean"), view4(tmp[0])[:, 2 * h:2 * h + 2], start=True, stop=True)
                    ins = mm(pn[:, h, HP:HALF], prmv("mean")[0:HS], tmp[1][0:HS, h, 0:HS], start=True, stop=True)
                ins.then_inc(rstd_ready, 1)
                if j in (1, 2):
                    keep_warm(45)

            def up(phase, block0, j=None):
                first, n, k = phase

                def hidden(f, ada, first_use=False, ready=None, turned=None):
                    if ready:
                        both_units(f + first, k, ready, first_use)
                    else:
                        unit(f + first, 0, k, h_hi, h_lo)
                    if ada:
                        if not (isinstance(f, int) and f == 0):
                            ada_turn(f + (block0 - 1))
                        ada_unit(f + block0, 0)
                        ada_unit(f + block0, 1)
                    if turned is not None:
                        ada_turn(turned)
                    if not ready:
                        unit(f + first, 1, k, h_hi, h_lo)
                    if ada:
                        ada_unit(f + block0, 2)
                        ada_unit(f + block0, 3)

                ready = None if j is None else normed(j)
                if block0:
                    hidden(0, True, first_use=(first == 0), ready=ready)
                    with pe.Fori(1, 9) as f:
                        hidden(f, True)
                    hidden(9, False, turned=block0 + 8)
                    hidden(10, False)
                else:
                    hidden(0, False, ready=ready)
                    with pe.Fori(1, n) as f:
                        hidden(f, False)

            def down(phase):
                first, n, k = phase
                unit(first, 0, k, hid_hi, hid_lo, ready=counted(hid_lo_ready, HT * DOWN.index(phase)))
                unit(first, 1, k, hid_hi, hid_lo)
                with pe.Fori(1, n) as i:
                    unit(i + first, 0, k, hid_hi, hid_lo)
                    unit(i + first, 1, k, hid_hi, hid_lo)

            pe.wait_ge(prm_in, 16)
            pe.wait_ge(c_ready, 1)
            pe.wait_ge(c_hi_ready, 1)
            pe.wait_ge(sel_ready, 1)
            for u in range(4):
                ada_unit(0, u)
            def ada_block(b):
                ada_unit(b, 0)
                ada_unit(b, 1)
                ada_turn(b - 1)
                ada_unit(b, 2)
                ada_unit(b, 3)

            ada_block(1)
            ada_block(2)
            mean_square(0)
            ada_block(3)
            ada_turn(3)
            pe.wait_ge(mod_ready, 4)
            keep_warm(22)
            up(UP[0], 4, j=0)
            down(DOWN[0])
            pe.wait_ge(bbar_ready, 1)
            for r in range(2):
                for t in range(CT):
                    ins = nc.tensor.transpose(pn[:, r, P * t:P * (t + 1)], flat(h32[r])[:, P * t:P * (t + 1)], prmv("ident"))
            ins.then_inc(bbar_turned, 1)
            up(UP[1], 13)
            down(DOWN[1])
            mean_square(1)

            both_units(PROJ_U[0], DT, normed(1))
            unit(PROJ_U[0] + 1, 0, DT, h_hi, h_lo)
            unit(PROJ_U[0] + 1, 1, DT, h_hi, h_lo)
            pe.sem_inc(y_ready, 2)
            def b_u(ct, j):
                pe.wait_ge(bu_ready, 4 * ct + (j + 1))
                for r in range(2):
                    for t in range(4):
                        ins = mm(pn[:, r, SEG * t:SEG * (t + 1)], lbs[:, r, t], proj[:, ct, SEG * j:SEG * (j + 1)],
                                 start=True, stop=True)
                ins.then_inc(b_done, 1)

            def c_x(ct, j):
                b = j % 2
                pe.wait_ge(xr_ready, 4 * ct + (j + 1))
                pe.wait_ge(xi_ready, 4 * ct + (j + 3))
                pe.wait_ge(y_used, 4 * ct + (j + 1))
                for t in range(4):
                    for r in range(2):
                        ins = mm(pa[32 * t:32 * t + 32, 0:SEG], lcs[:, t, r], xc[b][:, r, t], start=(r == 0), stop=(r == 1))
                ins.then_inc(y_ready, 1)

            def channel_tile(ct, first=False, last=False):
                qa = 2 * ct + PROJ_REST[0]
                pe.wait_ge(bus_ready, ct + 1)
                for r in range(2):
                    for t in range(4):
                        ins = mm(pt[:, (4 * r + t) * NS:(4 * r + t + 1) * NS], lbs[:, r, t], proj[:, ct, SEQ:TOK], start=True, stop=True)
                ins.then_inc(bs_done, 1)
                b_u(ct, 1)
                unit(qa, 0, DT, h_hi, h_lo)
                if not first:
                    c_x(ct - 1, 3)
                b_u(ct, 2)
                unit(qa, 1, DT, h_hi, h_lo)
                pe.wait_ge(lcs_staged, ct + 1)
                c_x(ct, 0)
                b_u(ct, 3)
                unit(qa + 1, 0, DT, h_hi, h_lo)
                c_x(ct, 1)
                if not last:
                    pe.wait_ge(staged, ct + 2)
                    b_u(ct + 1, 0)
                unit(qa + 1, 1, DT, h_hi, h_lo)
                c_x(ct, 2)
                if last:
                    c_x(ct, 3)

            pe.wait_ge(staged, 1)
            b_u(0, 0)
            channel_tile(0, first=True)
            with pe.Fori(1, CT - 1) as ct:
                channel_tile(ct)
            channel_tile(CT - 1, last=True)

            def samples_y():
                pe.wait_ge(xs_ready, 1)
                for ct in range(CT):
                    for t in range(4):
                        for r in range(2):
                            ins = mm(pa[32 * t:32 * t + 32, NS * ct:NS * (ct + 1)], lc[:, 4 * ct + t, r],
                                     xs[:, r, 4 * ct + t].rearrange("p b s -> p (b s)"), start=(r == 0), stop=(r == 1))
                ins.then_inc(ys_ready, 1)

            ident = prmv("ident")
            for s in range(2):
                pe.wait_ge(acc_free[s], GLU[0])
            pe.wait_ge(bu_ready, 4 * CT + 1)
            pe.wait_ge(bus_ready, CT + 1)
            pe.wait_ge(y_used, 4 * CT + 1)

            def front(h):
                pe.wait_ge(vs_ready, h + 1)
                for t in range(4):
                    nc.tensor.transpose(acc[1][:, 1, DV * t:DV * (t + 1)], vs[:, P * t:P * (t + 1)], ident)
                nc.tensor.transpose(pn[0:NS, 1, DK:DK + DV], vs[:, SEQ:TOK], ident).then_inc(tv_ready, 1)
                pe.wait_ge(ks_ready, h + 1)
                if not (isinstance(h, int) and h == 0):
                    pe.wait_ge(sp_ready, h)
                for t in range(4):
                    nc.tensor.transpose(pn[:, 0, DK * t:DK * (t + 1)], ks[:, P * t:P * (t + 1)], ident)
                nc.tensor.transpose(pn[0:NS, 1, 0:DK], ks[:, SEQ:TOK], ident).then_inc(tk_ready, 1)
                if not (isinstance(h, int) and h == 0):
                    pe.wait_ge(sn_ready, h)
                for t in range(4):
                    mm(scores_at(t), ks[:, P * t:P * (t + 1)], proj[:, 4 * h + 4, P * t:SEQ], start=True, stop=True)
                mm(acc[1][0:NS, 0, 2 * P:2 * P + NS], ks[:, SEQ:TOK], proj[:, 4 * h + 4, SEQ:TOK],
                   start=True, stop=True).then_inc(scores_ready, 1)

            def middle(h):
                pe.wait_ge(kt_ready, h + 1)
                pe.wait_ge(vt_ready, h + 1)
                for t in range(4):
                    ins = mm(pn[:, 0, 0:DV], kt[:, t], vt[:, t], start=(t == 0), stop=(t == 3))
                ins.then_inc(spp_ready, 1)
                pe.wait_ge(qm_ready, h + 1)
                pe.wait_ge(s0_in, 16 * h + 16)
                for b in range(DEC_BATCH):
                    mm(pa[0:NS, 0:DV], qm[:, b], s0[:, b], start=(b == 0), stop=False)
                pe.wait_ge(scm_ready, h + 1)
                pe.wait_ge(m32_ready, h + 1)
                for qt in range(4):
                    for t in range(qt + 1):
                        at = sum(SEQ - P * n for n in range(t)) + P * (qt - t)
                        mm(pt[:, DV * qt:DV * (qt + 1)], sc[:, at:at + P], vt[:, t], start=(t == 0), stop=(t == qt))
                mm(pa[0:NS, 0:DV], scs[:], vt[0:NS, 4], start=False, stop=True).then_inc(o_ready, 1)
                pe.wait_ge(vm_ready, h + 1)
                for c in range(2):
                    ins = mm(acc[0][:, c], kt[0:NS, 4], vm[0:NS, 4 * c:4 * c + 4].rearrange("p b v -> p (b v)"),
                             start=True, stop=True)
                ins.then_inc(snp_ready, 1)

            def back(h, last=False):
                pe.wait_ge(on_ready, h + 1)
                if not last:
                    pe.wait_ge(kt_ready, h + 2)
                for t in range(4):
                    nc.tensor.transpose(pt[:, P * t:P * (t + 1)], on[:, t], ident)
                nc.tensor.transpose(pn[:, 1, 2 * P:2 * P + NS], on[0:NS, 4], ident[0:NS, 0:NS]).then_inc(ot_ready, 1)

            front(0)
            middle(0)
            front(1)
            back(0)
            samples_y()
            pe.wait_ge(y_all, 1)
            with pe.Fori(1, HEADS - 1) as h:
                middle(h)
                front(h + 1)
                back(h)
            middle(HEADS - 1)

            pe.wait_ge(sn_ready, HEADS)
            unit(GLU[0], 0, GLU[2], h_hi, h_lo, ready=counted(g_lo_ready, 0))
            back(HEADS - 1, last=True)
            unit(GLU[0], 1, GLU[2], h_hi, h_lo)
            with pe.Fori(1, GLU[1]) as i:
                unit(i + GLU[0], 0, GLU[2], h_hi, h_lo)
                unit(i + GLU[0], 1, GLU[2], h_hi, h_lo)

            def mixed(t):
                return (h_hi[:, t], h_lo[:, t]) if t >= CT else (glu_hi[:, t], glu_lo[:, t])

            def mixed_ready(t):
                if t >= CT:
                    pe.wait_ge(r_lo_ready, t - CT + 2)
                else:
                    pe.wait_ge(m_lo_ready, t + 1)
            order = list(range(CT, DT)) + list(range(CT))
            unit_of(OUT[0], 0, order, mixed, ready=mixed_ready)
            unit_of(OUT[0], 1, order, mixed)
            with pe.Fori(1, OUT[1]) as i:
                unit_of(i + OUT[0], 0, order, mixed)
                unit_of(i + OUT[0], 1, order, mixed)
            mean_square(2)
            up(UP[2], 0, j=2)
            down(DOWN[2])
            up(UP[3], 0)
            down(DOWN[3])
            mean_square(3)


def head_constants():
    out = np.zeros((HEADS, P, HC_N), np.float32)
    small = np.zeros((P, HEADS, HS_N), np.float32)
    scale = np.float32(DK) ** np.float32(-0.5)
    i = np.arange(P)
    for h in range(HEADS):
        lg = np.log1p(-np.exp2(-5.0 - h))
        d = np.arange(SEQ)[None, :] - i[:, None]
        out[h, :, slice(*HC["mask"])] = np.where(d >= 0, np.exp(lg * np.maximum(d, 0)), 0.0) * scale
        n = np.arange(NS)
        seq, s = n // DEC_SEQ, n % DEC_SEQ
        qmask = (seq[None, :] == np.arange(DEC_BATCH)[:, None]) * np.exp(lg * (s + 1.0))[None, :]
        out[h, :, slice(*HC["qmask"])] = qmask.reshape(1, -1)
        kdec = np.zeros((P, 5))
        for t in range(4):
            kdec[:, t] = np.exp(lg * (SEQ - 1.0 - (P * t + i))) * scale
        kdec[:NS, 4] = np.exp(lg * (DEC_SEQ - 1.0 - s)) * scale
        small[:, h, slice(*HS_C["kdec"])] = kdec
        small[:, h, slice(*HS_C["g4"])] = np.exp(lg * DEC_SEQ)
        same = (seq[:, None] == seq[None, :]) & (s[None, :] >= s[:, None])
        small[:NS, h, slice(*HS_C["smask"])] = np.where(same, np.exp(lg * np.maximum(s[None, :] - s[:, None], 0)), 0.0) * scale
        small[:NS, h, slice(*HS_C["bmask"])] = seq[:, None] == np.arange(DEC_BATCH)[None, :]
    return out, small.reshape(P, -1)


def rope_table():
    half = DK // 2
    inv = (np.float32(10000.0) ** (-np.arange(half, dtype=np.float32) / np.float32(half))).astype(np.float32)
    pos = np.concatenate([np.arange(SEQ), PAST_LEN + np.tile(np.arange(DEC_SEQ), DEC_BATCH)]).astype(np.float32)
    ang = (pos[None, :] * inv[:, None]).astype(np.float32).astype(np.float64)
    cos, sin = np.cos(ang), np.sin(ang)
    return np.stack([np.concatenate([cos, cos]), np.concatenate([-sin, sin])]).astype(np.float32)


_OUTS = {"y": (DT, P, TOK), "ssm_prompt": (P, 2 * NT), "ssm_sample": (P, 2 * NT * DEC_BATCH),
         "ret_prompt": (HEADS, DK, DV), "ret_sample": (HEADS, DK, DEC_BATCH * DV)}


def kernel(**inputs):
    import concourse.bacc as bacc
    from concourse.bass_utils import run_bass_kernel_spmd

    v = {n: np.asarray(t) for n, t in inputs.items()}
    one = {n: t[0] if t.shape[0] == 1 and n not in ("x_prompt", "c_prompt") else t for n, t in v.items()}

    def tiled(w, k, m, order):
        return np.ascontiguousarray(w.reshape(k + m).transpose(order))

    feeds = {}
    xp = v["x_prompt"].reshape(HALVES, HP, D_MODEL)
    xs_ = v["x_sample"].reshape(HALVES, HS, D_MODEL)
    xt = np.concatenate([xp, xs_], 1)
    feeds["x"] = np.ascontiguousarray(xt.reshape(HALVES, HALF, DT, P).transpose(3, 2, 0, 1)).reshape(P, -1)
    for n in (1, 2):
        w = one[f"ffn{n}_w_in"]
        feeds[f"ffn{n}_up"] = tiled(w, (DT, P), (2, FT, P), (3, 2, 1, 0, 4)).reshape(FT, 2, P, DT * P)
        w = one[f"ffn{n}_w_out"]
        feeds[f"ffn{n}_down"] = np.ascontiguousarray(
            w.reshape(2, HT, P, DT, P).transpose(0, 3, 2, 1, 4)).reshape(2 * 4, 2, P, HT * P)
    order = list(range(CT)) + [CT + HEADS * part + h for h in range(HEADS) for part in range(4)]
    feeds["w_in"] = tiled(one["w_in_mix"], (DT, P), (20, P), (2, 1, 0, 3))[order].reshape(10, 2, P, DT * P)
    feeds["w_glu"] = tiled(one["s5_w_glu"], (4, P), (2, 4, P), (3, 2, 1, 0, 4))[:, ::-1].reshape(4, 2, P, 4 * P)
    feeds["w_out"] = tiled(one["w_out_mix"], (DT, P), (DT, P), (2, 1, 0, 3)).reshape(4, 2, P, DT * P)
    wa = np.concatenate([one["w_ada"], v["w_ada_final"]], 1)
    feeds["ada"] = tiled(wa, (4, 2, P), (ADA_BLOCKS, ADA_N), (3, 0, 2, 1, 4)).reshape(ADA_BLOCKS, 4, P, 2 * ADA_N)

    prm = np.zeros((P, PRM_N), np.float32)

    def put(name, t):
        prm[:, slice(*PRM[name])] = t.reshape(P, -1)

    put("ident", np.eye(P, dtype=np.float32))
    put("mean", np.full((P, P), 1.0 / D_MODEL, np.float32))
    sel = np.zeros((P, SEL_N), np.float32)
    for at in (0, 32):
        sel[at + np.arange(2 * NC_), np.arange(2 * NC_) % NC_] = 1.0
    put("sel", sel)
    put("bias", np.concatenate([one["b_ada"], v["b_ada_final"]]).reshape(MOD_TILES, P).T)
    put("gain", np.concatenate([one[n] for n in ("norm_ffn1", "norm_mix", "norm_ffn2")] + [v["norm_final"]]).reshape(4 * DT, P).T)
    put("skip", one["s5_d"].reshape(CT, P).T)

    def states(t):
        return np.moveaxis(t.reshape((NT, P) + t.shape[2:]), 0, 1)

    log_dt = np.repeat(one["s5_log_dt"][:, None], 64, 1)
    put("lam", np.stack([states(one["s5_lambda_re"]), states(one["s5_lambda_im"]), states(log_dt)], 1))
    c_all = np.concatenate([v["c_prompt"], v["c_sample"]], 0)
    put("c", c_all.reshape(NC_, DT, P).transpose(2, 1, 0))
    feeds["prm"] = prm

    def block_diagonal(t):
        out = np.zeros((P, NT, 32), np.float32)
        out[:64, :, :16] = t[:64]
        out[64:, :, 16:] = t[64:]
        return out

    feeds["s5_b"] = np.stack([block_diagonal(states(one[n])).reshape(P, -1) for n in ("s5_b_re", "s5_b_im")])
    feeds["s5_c"] = np.ascontiguousarray(np.stack(
        [block_diagonal(states(one[n].transpose(0, 2, 1))) for n in ("s5_c_re", "s5_c_im")], 2)).reshape(P, -1)
    h0 = [np.moveaxis(one[n].reshape(DEC_BATCH, NT, P), (0, 1, 2), (2, 1, 0)) for n in ("state_ssm_re", "state_ssm_im")]
    feeds["h0"] = np.ascontiguousarray(np.stack(h0, 1)).reshape(P, -1)
    feeds["s0"] = np.ascontiguousarray(one["state_ret"].transpose(1, 2, 0, 3)).reshape(HEADS, DK, -1)
    feeds["rope"] = rope_table()
    feeds["head_consts"], feeds["head_small"] = head_constants()

    nc = bacc.Bacc("TRN2", target_bir_lowering=False, num_devices=1)
    aps = {n: nc.dram_tensor(f"in_{n}", t.shape, F32, kind="ExternalInput").ap() for n, t in feeds.items()}
    aps |= {n: nc.dram_tensor(f"out_{n}", s, F32, kind="ExternalOutput").ap() for n, s in _OUTS.items()}
    build(nc, aps)
    r = run_bass_kernel_spmd(nc, [{f"in_{n}": t for n, t in feeds.items()}], core_ids=[0]).results[0]
    out = {n: np.asarray(r[f"out_{n}"]) for n in _OUTS}

    y = out["y"].reshape(DT, P, HALVES, HALF).transpose(2, 3, 0, 1).reshape(HALVES, HALF, D_MODEL)
    y_prompt = np.ascontiguousarray(y[:, :HP]).reshape(1, SEQ, D_MODEL)
    y_sample = np.ascontiguousarray(y[:, HP:]).reshape(DEC_BATCH, DEC_SEQ, D_MODEL)
    sp = out["ssm_prompt"].reshape(P, 2, NT).transpose(1, 2, 0).reshape(2, 1, 1, 32, 64)
    ss = out["ssm_sample"].reshape(P, 2, NT, DEC_BATCH).transpose(1, 3, 2, 0).reshape(2, 1, DEC_BATCH, 32, 64)
    ret_p = out["ret_prompt"].reshape(1, 1, HEADS, DK, DV)
    ret_s = np.ascontiguousarray(out["ret_sample"].reshape(HEADS, DK, DEC_BATCH, DV).transpose(2, 0, 1, 3))[None]
    return (y_prompt, y_sample, np.ascontiguousarray(sp[0]), np.ascontiguousarray(sp[1]), ret_p,
            np.ascontiguousarray(ss[0]), np.ascontiguousarray(ss[1]), ret_s)
```
